# Optimizing a Trainium2 kernel written in Bass

```python
import math
import jax, jax.numpy as jnp
from jax import lax
import numpy as np
import jax
import jax.numpy as jnp

D_MODEL = 1024
BATCH = 1
SEQ = 256
DEPTH = 1

D_MIX = D_MODEL
D_MLSTM = D_MIX // 2
D_DIFF = D_MIX - D_MLSTM
ML_HEADS = 4
ML_HD = D_MLSTM // ML_HEADS
CONV_W = 4
CHUNK = 128
DA_HEADS = 4
DA_VD = D_DIFF // DA_HEADS
DA_QD = DA_VD // 2
Q_BLOCK = 128
REL_BUCKETS = 32
REL_MAX_DIST = 128
N_GROUPS = 4
EXP_PER_GROUP = 8
N_EXPERTS = N_GROUPS * EXP_PER_GROUP
TOP_K_FINE = 2
D_FF_EXP = 512
EPS = 1e-6
SUBLN_EPS = 1e-5
IN_COLS = 3 * D_MLSTM + 3 * D_DIFF


def rmsnorm(x, g, eps=EPS):
    xf = x.astype(jnp.float32)
    y = xf * lax.rsqrt(jnp.mean(xf * xf, axis=-1, keepdims=True) + eps)
    return (y * g.astype(jnp.float32)).astype(x.dtype)

def head_layernorm(h, g):
    mu = jnp.mean(h, axis=-1, keepdims=True)
    var = jnp.mean(jnp.square(h - mu), axis=-1, keepdims=True)
    return (h - mu) * lax.rsqrt(var + EPS) * g.astype(jnp.float32)

def causal_conv(x, w, b):
    c = x.shape[-1]
    y = lax.conv_general_dilated(x, w[:, None, :].astype(x.dtype), window_strides=(1,),
                                 padding=[(CONV_W - 1, 0)],
                                 dimension_numbers=('NWC', 'WIO', 'NWC'),
                                 feature_group_count=c)
    return y + b.astype(x.dtype)

def mlstm_chunkwise(q, k, v, i_pre, logf):
    bsz, s, nh, d = q.shape
    nc = s // CHUNK
    def chunks(t):
        return t.reshape(bsz, nc, CHUNK, nh, d).transpose(1, 0, 3, 2, 4)
    def gchunks(t):
        return t.reshape(bsz, nc, CHUNK, nh).transpose(1, 0, 3, 2)
    tril = jnp.tril(jnp.ones((CHUNK, CHUNK), dtype=bool))

    def step(carry, xs):
        cmat, nvec, m = carry
        qc, kc, vc, ic, fc = xs
        b = jnp.cumsum(fc, axis=-1)
        inter = b + m[..., None]
        dmat = jnp.where(tril, b[..., :, None] - b[..., None, :] + ic[..., None, :], -jnp.inf)
        m_t = jnp.maximum(inter, jnp.max(dmat, axis=-1))
        w = jnp.exp(dmat - m_t[..., None]) * jnp.einsum('bhtd,bhsd->bhts', qc, kc)
        sp = jnp.exp(inter - m_t)
        num = sp[..., None] * jnp.einsum('bhtk,bhvk->bhtv', qc, cmat) + jnp.einsum('bhts,bhsv->bhtv', w, vc)
        den = sp * jnp.einsum('bhtk,bhk->bht', qc, nvec) + jnp.sum(w, axis=-1)
        h = num / jnp.maximum(jnp.abs(den), jnp.exp(-m_t))[..., None]
        b_end = b[..., -1]
        g = b_end[..., None] - b + ic
        m_new = jnp.maximum(b_end + m, jnp.max(g, axis=-1))
        wk = jnp.exp(g - m_new[..., None])
        decay = jnp.exp(b_end + m - m_new)
        c_new = decay[..., None, None] * cmat + jnp.einsum('bhs,bhsv,bhsk->bhvk', wk, vc, kc)
        n_new = decay[..., None] * nvec + jnp.einsum('bhs,bhsk->bhk', wk, kc)
        return (c_new, n_new, m_new), h

    init = (jnp.zeros((bsz, nh, d, d), jnp.float32), jnp.zeros((bsz, nh, d), jnp.float32),
            jnp.zeros((bsz, nh), jnp.float32))
    _, hs = lax.scan(step, init, (chunks(q), chunks(k), chunks(v), gchunks(i_pre), gchunks(logf)))
    return hs.transpose(1, 0, 3, 2, 4).reshape(bsz, s, nh, d)

def mlstm_group(c, v, z, conv_w, conv_b, w_mq, w_mk, w_mgate, b_mgate, m_norm_g, m_skip):
    bsz, s, _ = c.shape
    c_act = jax.nn.silu(causal_conv(c, conv_w, conv_b))
    ch = c_act.reshape(bsz, s, ML_HEADS, ML_HD)
    q = jnp.einsum('bshd,hde->bshe', ch, w_mq)
    k = jnp.einsum('bshd,hde->bshe', ch, w_mk)
    vh = v.reshape(bsz, s, ML_HEADS, ML_HD)
    gin = jnp.concatenate([q.reshape(bsz, s, -1), k.reshape(bsz, s, -1), v], axis=-1)
    gates = (gin @ w_mgate).astype(jnp.float32) + b_mgate.astype(jnp.float32)
    i_pre = gates[..., :ML_HEADS]
    logf = jax.nn.log_sigmoid(gates[..., ML_HEADS:])
    h = mlstm_chunkwise(q.astype(jnp.float32), (k * (ML_HD ** -0.5)).astype(jnp.float32),
                        vh.astype(jnp.float32), i_pre, logf)
    h = head_layernorm(h, m_norm_g.reshape(ML_HEADS, ML_HD)).reshape(bsz, s, D_MLSTM)
    h = h + m_skip.astype(jnp.float32) * c_act.astype(jnp.float32)
    o = jax.nn.sigmoid(z.astype(jnp.float32))
    return (o * h).astype(c.dtype)

def rel_bucket(qpos, kpos):
    n = jnp.maximum(qpos[:, None] - kpos[None, :], 0)
    max_exact = REL_BUCKETS // 2
    large = max_exact + (jnp.log(jnp.maximum(n, 1).astype(jnp.float32) / max_exact)
                         / math.log(REL_MAX_DIST / max_exact) * (REL_BUCKETS - max_exact)).astype(jnp.int32)
    large = jnp.minimum(large, REL_BUCKETS - 1)
    return jnp.where(n < max_exact, n, large)

def diff_attention(q, k, v, lam, rel_bias):
    bsz, s = q.shape[0], q.shape[1]
    nb = s // Q_BLOCK
    scale = DA_QD ** -0.5
    qb = jnp.moveaxis(q.reshape(bsz, nb, Q_BLOCK, DA_HEADS, 2, DA_QD), 1, 0)
    kpos = jnp.arange(s)

    def block(args):
        q_blk, bi = args
        qpos = bi * Q_BLOCK + jnp.arange(Q_BLOCK)
        bias = rel_bias[rel_bucket(qpos, kpos)].transpose(2, 0, 1).astype(jnp.float32)
        mask = kpos[None, :] <= qpos[:, None]
        logits = jnp.einsum('bqhcd,bkhcd->bchqk', q_blk, k).astype(jnp.float32) * scale + bias[None, None]
        p = jax.nn.softmax(jnp.where(mask, logits, -jnp.inf), axis=-1)
        a = p[:, 0] - lam * p[:, 1]
        return jnp.einsum('bhqk,bkhd->bqhd', a.astype(v.dtype), v)

    out = lax.map(block, (qb, jnp.arange(nb)))
    return jnp.moveaxis(out, 0, 1).reshape(bsz, s, DA_HEADS, DA_VD)

def hier_moe(h, w_rg, b_rg, w_re, b_re, w_eg, w_eu, w_ed):
    bsz, s, d = h.shape
    t = h.reshape(-1, d)
    lg = (t @ w_rg).astype(jnp.float32) + b_rg.astype(jnp.float32)
    pg = jax.nn.softmax(lg, axis=-1)
    _, g_idx = lax.top_k(lg, 1)
    pg_sel = jnp.take_along_axis(pg, g_idx, axis=-1)
    le = jnp.einsum('nd,dge->nge', t, w_re).astype(jnp.float32) + b_re.astype(jnp.float32)
    le_sel = jnp.take_along_axis(le, g_idx[:, :, None], axis=1)[:, 0]
    top_v, top_i = lax.top_k(le_sel, TOP_K_FINE)
    pw = jax.nn.softmax(top_v, axis=-1)
    eid = g_idx * EXP_PER_GROUP + top_i
    gates = jnp.sum(jax.nn.one_hot(eid, N_EXPERTS, dtype=jnp.float32) * (pg_sel * pw)[..., None], axis=1)
    gates = gates.astype(t.dtype)
    out = jnp.zeros_like(t)
    for e in range(N_EXPERTS):
        hid = jax.nn.silu(t @ w_eg[e]) * (t @ w_eu[e])
        out = out + gates[:, e:e + 1] * (hid @ w_ed[e])
    return out.reshape(bsz, s, d)

def first_inputs(seed: int = 0) -> dict:
    key = jax.random.key(seed)
    ks = jax.random.split(key, 32)
    f32 = jnp.float32
    def nrm(k, shape, sc):
        return jax.random.normal(k, shape, f32) * sc
    L = DEPTH
    b_i = nrm(ks[7], (L, ML_HEADS), 0.1)
    b_f = jnp.linspace(3.0, 6.0, ML_HEADS, dtype=f32)[None, :] + nrm(ks[8], (L, ML_HEADS), 0.01)
    return {
        'x': nrm(ks[0], (BATCH, SEQ, D_MODEL), 1.0),
        'w_in': nrm(ks[1], (L, D_MODEL, IN_COLS), D_MODEL ** -0.5),
        'conv_w': nrm(ks[2], (L, CONV_W, D_MLSTM), CONV_W ** -0.5),
        'conv_b': nrm(ks[3], (L, D_MLSTM), 0.01),
        'w_mq': nrm(ks[4], (L, ML_HEADS, ML_HD, ML_HD), ML_HD ** -0.5),
        'w_mk': nrm(ks[5], (L, ML_HEADS, ML_HD, ML_HD), ML_HD ** -0.5),
        'w_mgate': nrm(ks[6], (L, 3 * D_MLSTM, 2 * ML_HEADS), 0.1 * (3 * D_MLSTM) ** -0.5),
        'b_mgate': jnp.concatenate([b_i, b_f], axis=-1),
        'm_norm_g': 1.0 + nrm(ks[9], (L, D_MLSTM), 0.02),
        'm_skip': 1.0 + nrm(ks[10], (L, D_MLSTM), 0.02),
        'lambda_qk': nrm(ks[11], (L, 4, DA_QD), 0.1),
        'da_norm_g': 1.0 + nrm(ks[12], (L, DA_VD), 0.02),
        'rel_bias': nrm(ks[13], (REL_BUCKETS, DA_HEADS), 0.2),
        'w_out': nrm(ks[14], (L, D_MIX, D_MODEL), D_MIX ** -0.5),
        'norm1_g': 1.0 + nrm(ks[15], (L, D_MODEL), 0.02),
        'norm2_g': 1.0 + nrm(ks[16], (L, D_MODEL), 0.02),
        'w_rg': nrm(ks[17], (L, D_MODEL, N_GROUPS), D_MODEL ** -0.5),
        'b_rg': nrm(ks[18], (L, N_GROUPS), 0.01),
        'w_re': nrm(ks[19], (L, D_MODEL, N_GROUPS, EXP_PER_GROUP), D_MODEL ** -0.5),
        'b_re': nrm(ks[20], (L, N_GROUPS, EXP_PER_GROUP), 0.01),
        'w_eg': nrm(ks[21], (L, N_EXPERTS, D_MODEL, D_FF_EXP), D_MODEL ** -0.5),
        'w_eu': nrm(ks[22], (L, N_EXPERTS, D_MODEL, D_FF_EXP), D_MODEL ** -0.5),
        'w_ed': nrm(ks[23], (L, N_EXPERTS, D_FF_EXP, D_MODEL), D_FF_EXP ** -0.5),
        'normf_g': 1.0 + nrm(ks[24], (D_MODEL,), 0.02),
    }

def first_block(x, w_in, conv_w, conv_b, w_mq, w_mk, w_mgate, b_mgate, m_norm_g, m_skip,
              lambda_qk, da_norm_g, rel_bias, w_out, norm1_g, norm2_g, w_rg, b_rg, w_re, b_re,
              w_eg, w_eu, w_ed, normf_g):
    bsz, s, _ = x.shape
    splits = [D_MLSTM, 2 * D_MLSTM, 3 * D_MLSTM, 3 * D_MLSTM + D_DIFF, 3 * D_MLSTM + 2 * D_DIFF]
    for l in range(DEPTH):
        lam_init = 0.8 - 0.6 * math.exp(-0.3 * l)
        h = rmsnorm(x, norm1_g[l])
        proj = h @ w_in[l]
        c, vm, z, qd, kd, vd = jnp.split(proj, splits, axis=-1)
        y_m = mlstm_group(c, vm, z, conv_w[l], conv_b[l], w_mq[l], w_mk[l], w_mgate[l], b_mgate[l],
                          m_norm_g[l], m_skip[l])
        lq = lambda_qk[l].astype(jnp.float32)
        lam = jnp.exp(jnp.dot(lq[0], lq[1])) - jnp.exp(jnp.dot(lq[2], lq[3])) + lam_init
        y_d = diff_attention(qd.reshape(bsz, s, DA_HEADS, 2, DA_QD), kd.reshape(bsz, s, DA_HEADS, 2, DA_QD),
                             vd.reshape(bsz, s, DA_HEADS, DA_VD), lam, rel_bias)
        y_d = (rmsnorm(y_d, da_norm_g[l], SUBLN_EPS) * (1.0 - lam_init)).reshape(bsz, s, D_DIFF)
        x = x + jnp.concatenate([y_m, y_d.astype(x.dtype)], axis=-1) @ w_out[l]
        h2 = rmsnorm(x, norm2_g[l])
        x = x + hier_moe(h2, w_rg[l], b_rg[l], w_re[l], b_re[l], w_eg[l], w_eu[l], w_ed[l])
    return rmsnorm(x, normf_g)


DEPTH_2 = 2

HEAD_DIM = 64
ROT_DIM = HEAD_DIM // 4
ROPE_THETA = 500000.0
NORM_EPS = 1e-6
NEG_INF = -1e30

NSA_HEADS = 8
NSA_GROUPS = 2
NSA_HPG = NSA_HEADS // NSA_GROUPS
CMP_LEN = 32
CMP_STRIDE = 16
CMP_HIDDEN = 256
SLC_LEN = 64
SLC_TOPN = 8
WINDOW = 256
SB_HEADS = 8
GLA_HEADS = 4
GLA_DK = 64
GLA_DV = 128
GLA_RANK = 16
GLA_TAU = 16.0
GLA_CHUNK = 64
FOX_HEADS = 8

BRANCH_WIDTH = 512
N_BRANCH = 4
D_FF = 4 * D_MODEL

NSA_QW = NSA_HEADS * HEAD_DIM
NSA_KVW = NSA_GROUPS * HEAD_DIM
SB_W = SB_HEADS * HEAD_DIM
FOX_W = FOX_HEADS * HEAD_DIM
SPLITS = (NSA_QW, NSA_KVW, NSA_KVW, NSA_KVW, NSA_KVW, NSA_KVW, NSA_KVW, NSA_HEADS * 3,
          SB_W, SB_W, SB_W,
          GLA_HEADS * GLA_DK, GLA_HEADS * GLA_DK, GLA_HEADS * GLA_DV, GLA_RANK, GLA_HEADS * GLA_DV,
          FOX_W, FOX_W, FOX_W, FOX_HEADS,
          N_BRANCH * D_MODEL)
D_IN = sum(SPLITS)


def rms_norm(x, g):
    xf = x.astype(jnp.float32)
    xf = xf * lax.rsqrt(jnp.mean(xf * xf, axis=-1, keepdims=True) + NORM_EPS)
    return (xf * g.astype(jnp.float32)).astype(x.dtype)

def masked_softmax(logits, mask):
    logits = jnp.where(mask, logits.astype(jnp.float32), NEG_INF)
    return jax.nn.softmax(logits, axis=-1) * mask

def rope_partial(x, pos):
    half = ROT_DIM // 2
    inv = ROPE_THETA ** (-jnp.arange(0, ROT_DIM, 2, dtype=jnp.float32) / ROT_DIM)
    ang = pos.astype(jnp.float32)[..., None] * inv
    ang = ang.reshape(ang.shape[:2] + (1,) * (x.ndim - 3) + (half,))
    cos = jnp.cos(ang).astype(x.dtype)
    sin = jnp.sin(ang).astype(x.dtype)
    x1, x2, xp = x[..., :half], x[..., half:ROT_DIM], x[..., ROT_DIM:]
    return jnp.concatenate([x1 * cos - x2 * sin, x2 * cos + x1 * sin, xp], axis=-1)

def nsa_mixer(q, k_cmp, v_cmp, k_slc, v_slc, k_win, v_win, gate_logits, pos,
              cmp_pos_k, cmp_pos_v, cmp_wk1, cmp_wk2, cmp_wv1, cmp_wv2):
    B, S = q.shape[:2]
    G, HPG, D = NSA_GROUPS, NSA_HPG, HEAD_DIM
    scale = D ** -0.5
    q = rope_partial(q.reshape(B, S, G, HPG, D), pos)
    k_cmp, v_cmp, k_slc, v_slc, k_win, v_win = [t.reshape(B, S, G, D) for t in (k_cmp, v_cmp, k_slc, v_slc, k_win, v_win)]
    k_slc = rope_partial(k_slc, pos)
    k_win = rope_partial(k_win, pos)
    tok = np.arange(S)

    n_cmp = (S - CMP_LEN) // CMP_STRIDE + 1
    cmp_start = np.arange(n_cmp) * CMP_STRIDE
    cmp_end = cmp_start + CMP_LEN - 1
    cmp_idx = cmp_start[:, None] + np.arange(CMP_LEN)[None, :]

    def compress(t, pe, w1, w2):
        blk = t[:, cmp_idx] + pe[:, None, :]
        blk = jnp.moveaxis(blk, 3, 2).reshape(B, n_cmp, G, CMP_LEN * D)
        return jax.nn.gelu(blk @ w1) @ w2

    kc = rope_partial(compress(k_cmp, cmp_pos_k, cmp_wk1, cmp_wk2), pos[:, cmp_end])
    vc = compress(v_cmp, cmp_pos_v, cmp_wv1, cmp_wv2)
    s_cmp = jnp.einsum('bsghd,bcgd->bghsc', q, kc) * scale
    p_cmp = masked_softmax(s_cmp, cmp_end[None, :] <= tok[:, None])
    o_cmp = jnp.einsum('bghsc,bcgd->bsghd', p_cmp.astype(vc.dtype), vc)

    n_sel = S // SLC_LEN
    top_n = min(SLC_TOPN, n_sel)
    sel_start = np.arange(n_sel) * SLC_LEN
    overlap = np.clip(np.minimum(cmp_start[:, None] + CMP_LEN, sel_start[None, :] + SLC_LEN)
                      - np.maximum(cmp_start[:, None], sel_start[None, :]), 0, None) / CMP_LEN
    imp = jnp.einsum('bghsc,cj->bgsj', p_cmp, jnp.asarray(overlap, jnp.float32))
    forced = (sel_start[None, :] == 0) | (np.arange(n_sel)[None, :] == (tok // SLC_LEN)[:, None])
    imp = jnp.where(forced, jnp.inf, jnp.where(sel_start[None, :] <= tok[:, None], imp, -jnp.inf))
    _, sel = lax.top_k(imp, top_n)
    n_qb = S // Q_BLOCK

    def to_blocks(t):
        return jnp.moveaxis(t.reshape(B, n_sel, SLC_LEN, G, D), 3, 1).reshape(B, G, n_sel, SLC_LEN * D)

    ks_blk = to_blocks(k_slc)
    vs_blk = to_blocks(v_slc)
    q_blk = jnp.moveaxis(q.reshape(B, n_qb, Q_BLOCK, G, HPG, D), 1, 0)
    sel_blk = jnp.moveaxis(sel.reshape(B, G, n_qb, Q_BLOCK, top_n), 2, 0)

    def select_block(args):
        qc, ic, t_start = args
        flat = ic.reshape(B, G, Q_BLOCK * top_n, 1)
        kg = jnp.take_along_axis(ks_blk, flat, axis=2).reshape(B, G, Q_BLOCK, top_n * SLC_LEN, D)
        vg = jnp.take_along_axis(vs_blk, flat, axis=2).reshape(B, G, Q_BLOCK, top_n * SLC_LEN, D)
        key_tok = (ic[..., None] * SLC_LEN + jnp.arange(SLC_LEN)).reshape(B, G, Q_BLOCK, top_n * SLC_LEN)
        t = t_start + jnp.arange(Q_BLOCK)
        s = jnp.einsum('bqghd,bgqkd->bghqk', qc, kg) * scale
        p = masked_softmax(s, (key_tok <= t[:, None])[:, :, None])
        return jnp.einsum('bghqk,bgqkd->bqghd', p.astype(vg.dtype), vg)

    o_slc = lax.map(select_block, (q_blk, sel_blk, jnp.arange(n_qb) * Q_BLOCK))
    o_slc = jnp.moveaxis(o_slc, 0, 1).reshape(B, S, G, HPG, D)

    n_band = Q_BLOCK + WINDOW
    band_idx = np.arange(n_qb)[:, None] * Q_BLOCK + np.arange(n_band)[None, :]
    band_tok = band_idx - WINDOW
    pad = ((0, 0), (WINDOW, 0), (0, 0), (0, 0))
    kb = jnp.pad(k_win, pad)[:, band_idx]
    vb = jnp.pad(v_win, pad)[:, band_idx]
    tq = tok.reshape(n_qb, Q_BLOCK)
    win_mask = ((band_tok[:, None, :] <= tq[:, :, None]) & (band_tok[:, None, :] > tq[:, :, None] - WINDOW)
                & (band_tok[:, None, :] >= 0))
    s_win = jnp.einsum('bnqghd,bnkgd->bnghqk', q.reshape(B, n_qb, Q_BLOCK, G, HPG, D), kb) * scale
    p_win = masked_softmax(s_win, win_mask[None, :, None, None])
    o_win = jnp.einsum('bnghqk,bnkgd->bnqghd', p_win.astype(vb.dtype), vb).reshape(B, S, G, HPG, D)

    g = jax.nn.sigmoid(gate_logits.astype(jnp.float32)).reshape(B, S, G, HPG, 3).astype(q.dtype)
    o = g[..., 0:1] * o_cmp + g[..., 1:2] * o_slc + g[..., 2:3] * o_win
    return o.reshape(B, S, NSA_HEADS * D)

def stick_breaking_mixer(q, k, v):
    B, S = q.shape[:2]
    H, D = SB_HEADS, HEAD_DIM
    scale = D ** -0.5
    n_qb = S // Q_BLOCK
    kT = jnp.moveaxis(k.reshape(B, S, H, D), 1, 2)
    vT = jnp.moveaxis(v.reshape(B, S, H, D), 1, 2)
    qb = q.reshape(B, n_qb, Q_BLOCK, H, D).transpose(1, 0, 3, 2, 4)
    key_pos = jnp.arange(S)

    def block(args):
        qc, t_start = args
        z = jnp.einsum('bhqd,bhkd->bhqk', qc, kT).astype(jnp.float32) * scale
        t = t_start + jnp.arange(Q_BLOCK)
        valid = key_pos[None, :] < t[:, None]
        sp = jnp.where(valid, jax.nn.softplus(z), 0.0)
        later = lax.cumsum(sp, axis=3, reverse=True) - sp
        a = jnp.where(valid, jnp.exp(jax.nn.log_sigmoid(z) - later), 0.0)
        return jnp.einsum('bhqk,bhkd->bhqd', a.astype(vT.dtype), vT)

    o = lax.map(block, (qb, jnp.arange(n_qb) * Q_BLOCK))
    return o.transpose(1, 0, 3, 2, 4).reshape(B, S, H * D)

def gla_mixer(q, k, v, a_lr, gate, w_alpha, b_alpha, norm_g):
    B, S = q.shape[:2]
    H, DK, DV, C = GLA_HEADS, GLA_DK, GLA_DV, GLA_CHUNK
    n_ch = S // C
    log_a = jax.nn.log_sigmoid((a_lr @ w_alpha + b_alpha).astype(jnp.float32)) / GLA_TAU

    def chunks(t, f):
        return t.reshape(B, n_ch, C, H, f).transpose(1, 0, 3, 2, 4)

    qc_all = chunks(q * DK ** -0.5, DK)
    kc_all = chunks(k, DK)
    vc_all = chunks(v, DV)
    la_all = chunks(log_a, DK)
    causal = np.tril(np.ones((C, C), dtype=bool))

    def step(state, inp):
        qc, kc, vc, lac = inp
        b = jnp.cumsum(lac, axis=2)
        o_inter = jnp.einsum('bhtk,bhkv->bhtv', qc * jnp.exp(b), state)
        diff = jnp.where(causal[:, :, None], b[:, :, :, None, :] - b[:, :, None, :, :], -jnp.inf)
        att = jnp.einsum('bhtk,bhsk,bhtsk->bhts', qc, kc, jnp.exp(diff))
        o_intra = jnp.einsum('bhts,bhsv->bhtv', att, vc)
        b_last = b[:, :, -1:, :]
        state = (jnp.exp(b_last[:, :, 0])[..., None] * state
                 + jnp.einsum('bhsk,bhsv->bhkv', kc * jnp.exp(b_last - b), vc))
        return state, o_inter + o_intra

    state0 = jnp.zeros((B, H, DK, DV), jnp.float32)
    _, o = lax.scan(step, state0, (qc_all, kc_all, vc_all, la_all))
    o = o.transpose(1, 0, 3, 2, 4).reshape(B, S, H, DV)
    o = o * lax.rsqrt(jnp.mean(o * o, axis=-1, keepdims=True) + NORM_EPS) * norm_g.astype(jnp.float32)
    y = o.astype(v.dtype) * jax.nn.silu(gate).reshape(B, S, H, DV)
    return y.reshape(B, S, H * DV)

def forgetting_mixer(q, k, v, f_logit, b_f):
    B, S = q.shape[:2]
    H, D = FOX_HEADS, HEAD_DIM
    scale = D ** -0.5
    n_qb = S // Q_BLOCK
    log_f = jax.nn.log_sigmoid(f_logit.astype(jnp.float32) + b_f.astype(jnp.float32))
    cumT = jnp.moveaxis(jnp.cumsum(log_f, axis=1), 1, 2)
    kT = jnp.moveaxis(k.reshape(B, S, H, D), 1, 2)
    vT = jnp.moveaxis(v.reshape(B, S, H, D), 1, 2)
    qb = q.reshape(B, n_qb, Q_BLOCK, H, D).transpose(1, 0, 3, 2, 4)
    cb = cumT.reshape(B, H, n_qb, Q_BLOCK).transpose(2, 0, 1, 3)
    key_pos = jnp.arange(S)

    def block(args):
        qc, ct, t_start = args
        s = jnp.einsum('bhqd,bhkd->bhqk', qc, kT).astype(jnp.float32) * scale
        s = s + ct[..., None] - cumT[:, :, None, :]
        t = t_start + jnp.arange(Q_BLOCK)
        p = masked_softmax(s, key_pos[None, :] <= t[:, None])
        return jnp.einsum('bhqk,bhkd->bhqd', p.astype(vT.dtype), vT)

    o = lax.map(block, (qb, cb, jnp.arange(n_qb) * Q_BLOCK))
    return o.transpose(1, 0, 3, 2, 4).reshape(B, S, H * D)

def hybrid_layer(x, positions, norm_mix, w_in, b_gate, cmp_pos_k, cmp_pos_v, cmp_wk1, cmp_wk2,
                 cmp_wv1, cmp_wv2, gla_w_alpha, gla_b_alpha, gla_norm, fox_b_f, w_branch, w_out,
                 norm_ff, w_ff1, w_ff2):
    B, S, _ = x.shape
    h = rms_norm(x, norm_mix)
    proj = h @ w_in
    offsets = np.cumsum(SPLITS)[:-1].tolist()
    (nsa_q, nsa_kc, nsa_vc, nsa_ks, nsa_vs, nsa_kw, nsa_vw, nsa_g,
     sb_q, sb_k, sb_v,
     gla_q, gla_k, gla_v, gla_a, gla_g,
     fox_q, fox_k, fox_v, fox_f,
     gate_logits) = jnp.split(proj, offsets, axis=-1)

    y_nsa = nsa_mixer(nsa_q, nsa_kc, nsa_vc, nsa_ks, nsa_vs, nsa_kw, nsa_vw, nsa_g, positions,
                      cmp_pos_k, cmp_pos_v, cmp_wk1, cmp_wk2, cmp_wv1, cmp_wv2)
    y_sb = stick_breaking_mixer(sb_q, sb_k, sb_v)
    y_gla = gla_mixer(gla_q.reshape(B, S, GLA_HEADS, GLA_DK), gla_k.reshape(B, S, GLA_HEADS, GLA_DK),
                      gla_v.reshape(B, S, GLA_HEADS, GLA_DV), gla_a, gla_g, gla_w_alpha, gla_b_alpha, gla_norm)
    y_fox = forgetting_mixer(fox_q, fox_k, fox_v, fox_f, fox_b_f)

    ys = jnp.stack([y_nsa, y_sb, y_gla, y_fox], axis=2)
    branch = jnp.einsum('bsnc,ncd->bsnd', ys, w_branch)
    gates = jax.nn.sigmoid((gate_logits + b_gate).astype(jnp.float32)).astype(x.dtype)
    mixed = jnp.sum(gates.reshape(B, S, N_BRANCH, D_MODEL) * branch, axis=2)
    x = x + mixed @ w_out
    h2 = rms_norm(x, norm_ff)
    return x + jnp.square(jax.nn.relu(h2 @ w_ff1)) @ w_ff2

def second_inputs(seed: int = 0) -> dict:
    key = jax.random.key(seed)
    ks = jax.random.split(key, 21)
    L = DEPTH_2

    def nrm(k, shape, scale):
        return jax.random.normal(k, shape, jnp.float32) * scale

    x = nrm(ks[0], (BATCH, SEQ, D_MODEL), 1.0)
    offset = jax.random.randint(ks[1], (BATCH, 1), 0, 4096, dtype=jnp.int32)
    positions = jnp.arange(SEQ, dtype=jnp.int32)[None, :] + offset
    return {
        'x': x,
        'positions': positions,
        'norm_mix': 1.0 + nrm(ks[2], (L, D_MODEL), 0.02),
        'w_in': nrm(ks[3], (L, D_MODEL, D_IN), D_MODEL ** -0.5),
        'b_gate': nrm(ks[4], (L, N_BRANCH * D_MODEL), 0.02),
        'nsa_cmp_pos_k': nrm(ks[5], (L, CMP_LEN, HEAD_DIM), 0.1),
        'nsa_cmp_pos_v': nrm(ks[6], (L, CMP_LEN, HEAD_DIM), 0.1),
        'nsa_cmp_wk1': nrm(ks[7], (L, CMP_LEN * HEAD_DIM, CMP_HIDDEN), (CMP_LEN * HEAD_DIM) ** -0.5),
        'nsa_cmp_wk2': nrm(ks[8], (L, CMP_HIDDEN, HEAD_DIM), CMP_HIDDEN ** -0.5),
        'nsa_cmp_wv1': nrm(ks[9], (L, CMP_LEN * HEAD_DIM, CMP_HIDDEN), (CMP_LEN * HEAD_DIM) ** -0.5),
        'nsa_cmp_wv2': nrm(ks[10], (L, CMP_HIDDEN, HEAD_DIM), CMP_HIDDEN ** -0.5),
        'gla_w_alpha': nrm(ks[11], (L, GLA_RANK, GLA_HEADS * GLA_DK), GLA_RANK ** -0.5),
        'gla_b_alpha': nrm(ks[12], (L, GLA_HEADS * GLA_DK), 0.1),
        'gla_norm': 1.0 + nrm(ks[13], (L, GLA_DV), 0.02),
        'fox_b_f': 2.0 + nrm(ks[14], (L, FOX_HEADS), 0.1),
        'w_branch': nrm(ks[15], (L, N_BRANCH, BRANCH_WIDTH, D_MODEL), BRANCH_WIDTH ** -0.5),
        'w_out': nrm(ks[16], (L, D_MODEL, D_MODEL), D_MODEL ** -0.5),
        'norm_ff': 1.0 + nrm(ks[17], (L, D_MODEL), 0.02),
        'w_ff1': nrm(ks[18], (L, D_MODEL, D_FF), D_MODEL ** -0.5),
        'w_ff2': nrm(ks[19], (L, D_FF, D_MODEL), D_FF ** -0.5),
        'norm_final': 1.0 + nrm(ks[20], (D_MODEL,), 0.02),
    }

def second_block(x, positions, norm_mix, w_in, b_gate, nsa_cmp_pos_k, nsa_cmp_pos_v, nsa_cmp_wk1,
              nsa_cmp_wk2, nsa_cmp_wv1, nsa_cmp_wv2, gla_w_alpha, gla_b_alpha, gla_norm, fox_b_f,
              w_branch, w_out, norm_ff, w_ff1, w_ff2, norm_final):
    for l in range(DEPTH_2):
        x = hybrid_layer(x, positions, norm_mix[l], w_in[l], b_gate[l], nsa_cmp_pos_k[l], nsa_cmp_pos_v[l],
                         nsa_cmp_wk1[l], nsa_cmp_wk2[l], nsa_cmp_wv1[l], nsa_cmp_wv2[l], gla_w_alpha[l],
                         gla_b_alpha[l], gla_norm[l], fox_b_f[l], w_branch[l], w_out[l], norm_ff[l],
                         w_ff1[l], w_ff2[l])
    return rms_norm(x, norm_final)


def setup_inputs(seed=0):
    out = dict(first_inputs(seed))
    for name, value in second_inputs(seed + 1).items():
        if name != "x":
            out[name + "_2"] = value
    return out


def reference(
    x, w_in, conv_w, conv_b, w_mq, w_mk, w_mgate, b_mgate, m_norm_g, m_skip, lambda_qk,
    da_norm_g, rel_bias, w_out, norm1_g, norm2_g, w_rg, b_rg, w_re, b_re, w_eg, w_eu, w_ed,
    normf_g, positions_2, norm_mix_2, w_in_2, b_gate_2, nsa_cmp_pos_k_2, nsa_cmp_pos_v_2,
    nsa_cmp_wk1_2, nsa_cmp_wk2_2, nsa_cmp_wv1_2, nsa_cmp_wv2_2, gla_w_alpha_2, gla_b_alpha_2,
    gla_norm_2, fox_b_f_2, w_branch_2, w_out_2, norm_ff_2, w_ff1_2, w_ff2_2, norm_final_2,
):
    x = first_block(
        x, w_in, conv_w, conv_b, w_mq, w_mk, w_mgate, b_mgate, m_norm_g, m_skip, lambda_qk,
        da_norm_g, rel_bias, w_out, norm1_g, norm2_g, w_rg, b_rg, w_re, b_re, w_eg, w_eu, w_ed,
        normf_g,
    )
    return second_block(
        x, positions_2, norm_mix_2, w_in_2, b_gate_2, nsa_cmp_pos_k_2, nsa_cmp_pos_v_2,
        nsa_cmp_wk1_2, nsa_cmp_wk2_2, nsa_cmp_wv1_2, nsa_cmp_wv2_2, gla_w_alpha_2,
        gla_b_alpha_2, gla_norm_2, fox_b_f_2, w_branch_2, w_out_2, norm_ff_2, w_ff1_2, w_ff2_2,
        norm_final_2,
    )


_drawn_inputs = setup_inputs


def setup_inputs(seed=0):
    import zlib

    import numpy as np

    out = dict(_drawn_inputs(seed))
    spreads = {}
    factors = {'m_skip': 3.014,
     'b_rg': 3.817,
     'b_re': 3.769,
     'b_gate_2': 8.0,
     'nsa_cmp_pos_k_2': 34.935,
     'nsa_cmp_pos_v_2': 2.958,
     'gla_b_alpha_2': 2.882,
     'gla_norm_2': 6.712,
     'fox_b_f_2': 28.344,
     'norm_final_2': 8.044,
     'norm_ff_2': 3.283}
    for name, (base, spread) in spreads.items():
        noise = np.random.default_rng([zlib.crc32(name.encode()), seed]).standard_normal(out[name].shape)
        drawn = base * np.exp(spread * noise) if base else spread * noise
        out[name] = jnp.asarray(drawn.astype(out[name].dtype))
    for name, factor in factors.items():
        out[name] = (out[name] * factor).astype(out[name].dtype)
    return out
```

```python
import numpy as np
import concourse.bass as bass
from concourse import mybir

F32 = mybir.dt.float32
I32 = mybir.dt.int32
U32 = mybir.dt.uint32
ALU = mybir.AluOpType
ACT = mybir.ActivationFunctionType
AX = mybir.AxisListType

P = 128
S = 256
TT = S // P
D = 1024
KT = D // P
CHUNK_COLS = 4096
BANKS = 8
SLOTS = 4
BIG = 1.0e30

ML_HEADS, ML_HD = 4, 128
DA_HEADS, DA_QD, DA_VD = 4, 64, 128
CONV_W = 4
N_GROUPS, EXP_PER_GROUP = 4, 8
N_EXPERTS = N_GROUPS * EXP_PER_GROUP
D_FF_EXP = 512
REL_BUCKETS, REL_MAX_DIST = 32, 128
LAM_INIT = 0.8 - 0.6 * float(np.exp(-0.3 * 0))
EPS, SUBLN_EPS = 1e-6, 1e-5
LAYERS = 2
HEADS, HD = 8, 64
NSA_GROUPS, NSA_HPG = 2, 4
CMP_LEN, CMP_STRIDE, CMP_HIDDEN = 32, 16, 256
N_CMP = (S - CMP_LEN) // CMP_STRIDE + 1
ROT_HALF = HD // 8
ROPE_THETA = 500000.0
GLA_HEADS, GLA_DK, GLA_DV, GLA_RANK, GLA_TAU = 4, 64, 128, 16, 16.0
N_BRANCH = 4
BRANCH_ORDER = [0, 1, 3, 2]
GLA_LEVELS = [128, 64, 32, 16, 8, 4, 2, 1]

TWO_PI, PI_F = 2.0 * np.pi, float(np.nextafter(np.float32(np.pi), np.float32(0)))
ROUND = 1.5 * 2.0 ** 23
TWO_PI_PARTS = (6.28125, 0.0019340515136718750, TWO_PI - 6.28125 - 0.0019340515136718750)
ACT_STEPS, DVE_STEPS = 28, 37
WAIT_MARKS = 40

PRE_CHUNKS = 8
EXPERT_CHUNKS = 3
UNROLL = 4
LAYER_CHUNKS = 44
W_IN_CHUNKS = {"nsa_q": 0, "nsa_k": 1, "nsa_v": 2, "cmp": 3, "sb_q": 5, "sb_k": 6, "sb_v": 7}


def columns(*fields):
    at, out = 0, {}
    for name, width in fields:
        out[name] = slice(at, at + width)
        at += width
    return out, at


CONST, CONST_COLS = columns(
    ("ident", 128), ("negmask", 384), ("strict", 128), ("sufneg", 128), ("negstrict", 128),
    ("negtriu", 256), ("gla", 7 * 128), ("rope", 128), ("dup", 256), ("inv", 1), ("cmpmask", 2 * N_CMP),
    ("rowvalid", 2), ("iota8", 8), ("neghalf", 8), ("ones8", 8), ("one", 1), ("bucket", 384))
PRM1, PRM1_COLS = columns(
    ("norm1", 8), ("norm2", 8), ("conv_w", 16), ("conv_b", 4), ("m_norm", 4), ("m_skip", 4), ("da_norm", 1),
    ("b_gate", 8), ("lam", 256), ("w_q", 512), ("w_k", 512), ("w_gate", 96), ("w_r", 288), ("b_r", 36),
    ("rel", 4))
PRM2, PRM2_COLS = columns(
    ("norm_mix", 8), ("norm_ff", 8), ("b_gate", 32), ("pe_k", 32), ("pe_v", 32), ("w_k2", 128), ("w_v2", 128),
    ("w_alpha", 256), ("b_alpha", 2), ("gla_norm", 128), ("fox_b", 8))


def constants():
    c = np.zeros((P, CONST_COLS), np.float32)
    r = np.arange(P)
    row, col = r[:, None], r[None, :]
    c[:, CONST["ident"]] = row == col
    neg = np.where(col > row, -BIG, 0.0)
    c[:, CONST["negmask"]] = np.concatenate([neg, 0 * neg, neg], 1)
    c[:, CONST["strict"]] = row < col
    c[:, CONST["sufneg"]] = -(row >= col).astype(np.float32)
    c[:, CONST["negstrict"]] = np.where(row >= col, -BIG, 0.0)
    c[:, CONST["negtriu"]] = np.concatenate([-(row <= col).astype(np.float32), -np.ones((P, P))], 1)
    levels = []
    for h in GLA_LEVELS[1:]:
        levels.append((row // (2 * h) == col // (2 * h)) & (row % (2 * h) < h) & (col % (2 * h) >= h))
    c[:, CONST["gla"]] = np.concatenate(levels, 1)
    rot = np.zeros((P, P), np.float32)
    inv = np.zeros(P, np.float32)
    freq = (np.float32(ROPE_THETA) ** (-np.arange(0, 2 * ROT_HALF, 2, dtype=np.float32)
                                       / np.float32(2 * ROT_HALF))).astype(np.float32)
    for base in (0, HD):
        for d in range(ROT_HALF):
            rot[base + ROT_HALF + d, base + d] = -1.0
            rot[base + d, base + ROT_HALF + d] = 1.0
            inv[base + d] = inv[base + ROT_HALF + d] = freq[d]
    c[:, CONST["rope"]] = rot
    c[:, CONST["inv"]] = inv[:, None]
    c[:, CONST["dup"]] = np.concatenate([row == g * HD + col % HD for g in range(NSA_GROUPS)], 1)
    ends = np.arange(N_CMP) * CMP_STRIDE + CMP_LEN - 1
    tok = np.arange(S).reshape(TT, P).T
    c[:, CONST["cmpmask"]] = np.where(ends[None, None] <= tok[:, :, None], 0.0, -BIG).reshape(P, -1)
    c[:, CONST["rowvalid"]] = tok >= ends[0]
    c[:, CONST["iota8"]] = np.arange(8)[None]
    c[:, CONST["neghalf"]] = -0.5
    c[:, CONST["ones8"]] = 1.0
    c[:, CONST["one"]] = 1.0
    n = np.maximum(255 - np.arange(384), 0)
    exact = REL_BUCKETS // 2
    large = exact + (np.log(np.maximum(n, 1).astype(np.float32) / np.float32(exact))
                     / np.float32(np.log(REL_MAX_DIST / exact)) * np.float32(REL_BUCKETS - exact)).astype(np.int32)
    bucket = np.where(n < exact, n, np.minimum(large, REL_BUCKETS - 1))
    c[:REL_BUCKETS, CONST["bucket"]] = np.arange(REL_BUCKETS)[:, None] == bucket[None]
    return c


class Job:

    def __init__(self, region, bank, use):
        self.region, self.bank, self.use = region, bank, use

    def count(self, turn=0):
        r = self.region
        return turn * r.uses[self.bank] + (r.base[self.bank] + self.use + 1)


class Region:

    def __init__(self, base, first_bank, turns=1):
        self.base, self.turns = list(base), turns
        self.uses = [0] * BANKS
        self.next = first_bank
        self.jobs = {}

    def add(self, name, count=1):
        for _ in range(count):
            b = self.next % BANKS
            self.next += 1
            self.jobs.setdefault(name, []).append(Job(self, b, self.uses[b]))
            self.uses[b] += 1

    def after(self):
        return [b + self.turns * u for b, u in zip(self.base, self.uses)]

    def __getitem__(self, name):
        return self.jobs[name]


def last_in_bank(jobs, but=None):
    last = {}
    for j in jobs:
        if but is None or j.bank != but.bank:
            if j.bank not in last or last[j.bank].use < j.use:
                last[j.bank] = j
    return list(last.values())


class Steps:

    def __init__(self):
        self.base, self.n, self.turn, self.per = 0, 0, 0, 0

    def next(self):
        self.n += 1
        return self.turn * self.per + (self.base + self.n)

    def enter(self, turn, per):
        self.base, self.n, self.turn, self.per = self.base + self.n, 0, turn, per

    def leave(self, turns):
        assert self.n == self.per, (self.n, self.per)
        self.base, self.n, self.turn = self.base + turns * self.per, 0, 0


def plan_pre():
    r = Region([0] * BANKS, 0)
    for name, count in (("ht", 4), ("c", 2), ("vm", 2), ("z", 2), ("rel", 4), ("mq", 2), ("mk", 2), ("vmt", 2),
                        ("gate", 1), ("qd", 2), ("kd", 2), ("vd", 2), ("negb", 1)):
        r.add(name, count)
    for h in range(ML_HEADS):
        r.add("u")
        r.add("qk")
    for n in range(2 * DA_HEADS):
        r.add("s")
        if n % 2:
            r.add("wt")
    for name, count in (("num", 2), ("at", 4), ("pv", 2), ("hnt", 2), ("ydt", 2), ("out", 4), ("h2", 4),
                        ("router", 1)):
        r.add(name, count)
    return r


def plan_moe(pre):
    r = Region(pre.after(), pre.next, N_EXPERTS // UNROLL)
    for e in range(UNROLL):
        for half in range(2):
            r.add(("g", e))
            r.add(("u", e))
        r.add(("d", e), 4)
    return r


NSA_FILL = [(n, j) for n in ("sb_q", "sb_k", "sb_v") for j in range(2)] + [("gates", j) for j in range(2)]
SB_FILL = [(n, j) for n in ("fox_q", "fox_k", "fox_v") for j in range(2)] + [("gates", j) for j in range(2, 4)]
FOX_FILL = [(n, j) for n in ("gla_qk", "gla_v", "gla_g") for j in range(2)] + [("gates", j) for j in range(4, 6)]
GLA_FILL = [("gates", j) for j in range(6, 16)]
NSA_N, NSA_LAG = 16, 3
SB_N, SB_LAG = 8, 3
FOX_N, FOX_LAG = 8, 3


def nsa_steps():
    out, fill = [], list(NSA_FILL)
    for n in range(NSA_N + NSA_LAG + 2):
        if n < NSA_N:
            out.append(("score", n))
        if 0 <= n - NSA_LAG < NSA_N:
            out.append(("turn", n - NSA_LAG))
        if n % 2 == 1 and fill:
            out.append(("fill", fill.pop(0)))
        k = n - NSA_LAG - 1
        if k >= 0 and k % 4 == 3:
            out.append(("value", k // 4))
    return out + [("fill", f) for f in fill]


def sb_steps():
    out, fill = [], list(SB_FILL)
    for n in range(SB_N + SB_LAG + 2):
        if n < SB_N:
            out.append(("score", n))
        if fill:
            out.append(("fill", fill.pop(0)))
        if 0 <= n - SB_LAG < SB_N:
            out.append(("again", n - SB_LAG))
        k = n - SB_LAG - 1
        if k >= 0 and k % 2 == 1:
            out.append(("value", k // 2))
    return out + [("fill", f) for f in fill]


def fox_steps():
    out, fill = [], list(FOX_FILL)
    for n in range(FOX_N + FOX_LAG + 2):
        if n < FOX_N:
            out.append(("score", n))
        if fill:
            out.append(("fill", fill.pop(0)))
        if 0 <= n - FOX_LAG < FOX_N:
            out.append(("turn", n - FOX_LAG))
        k = n - FOX_LAG - 1
        if k >= 0 and k % 2 == 1:
            out.append(("value", k // 2))
    return out + [("fill", f) for f in fill]


def gla_steps():
    out, fill = [], list(GLA_FILL)
    for n in range(len(GLA_LEVELS) + 1):
        out.append(("level", n))
        if fill:
            out.append(("fill", fill.pop(0)))
    return out + [("fill", f) for f in fill]


def plan_layer(moe):
    r = Region(moe.after(), moe.next, LAYERS)
    for name, count in (("ht", 4), ("nsa_q", 2), ("nsa_k", 2), ("nsa_v", 2), ("gla_a", 1), ("rope_q", 2),
                        ("rope_k", 1), ("dup", 2), ("hid", 2), ("kc", 1), ("vc", 1), ("rope_c", 1), ("gla_la", 1),
                        ("cs", 2), ("ct", 4)):
        r.add(name, count)
    for mixer, steps in (("nsa", nsa_steps()), ("sb", sb_steps()), ("fox", fox_steps()), ("gla", gla_steps())):
        for kind, n in steps:
            if kind == "fill":
                r.add(n[0])
            elif kind == "level":
                r.add((mixer, kind, n), 2)
            else:
                r.add((mixer, kind, n))
    for name, count in (("gla_o", 2), ("gla_t", 2), ("branch", 16), ("out", 4), ("h2", 4), ("ff1", 16), ("ff2", 4)):
        r.add(name, count)
    return r


def program(nc, d):
    sb = lambda name, cols, dt=F32: nc.alloc_sbuf_tensor(name, [P, cols], dt)
    sem = lambda name: nc.alloc_semaphore(name)

    cst = sb("cst", CONST["bucket"].start)
    prm = sb("prm", max(PRM1_COLS - 1024, PRM2_COLS))
    wring = sb("wring", SLOTS * CHUNK_COLS)
    x_mem, xn_mem, ht_mem = sb("x_mem", TT * D), sb("xn_mem", TT * D), sb("ht_mem", KT * S)
    gates_mem = sb("gates_mem", 8 * 1024)
    qkv_a, qkv_b = sb("qkv_a", 3072), sb("qkv_b", 3072)
    p_mem, pt_mem = sb("p_mem", 3072), sb("pt_mem", 3072)
    yt_mem = sb("yt_mem", 4096)
    rope_mem = sb("rope_mem", 512)
    small = sb("small", 480)
    index8 = sb("index8", 32, U32)
    psum = [nc.alloc_psum_tensor(f"bank{b}", [P, 512], F32) for b in range(BANKS)]

    def view(mem, first, *shape):
        n = int(np.prod(shape))
        v = mem[:, first:first + n]
        if len(shape) == 1:
            return v
        names = "abcd"[:len(shape)]
        return v.rearrange(f"p ({' '.join(names)}) -> p {' '.join(names)}", **dict(zip(names, shape)))

    def C(name):
        return cst[:, CONST[name]]

    at_small = [0]

    def stat(n):
        at_small[0] += n
        return small[:, at_small[0] - n:at_small[0]]

    x, xn, hT = view(x_mem, 0, TT, D), view(xn_mem, 0, TT, D), view(ht_mem, 0, KT, S)
    ident, negmask, negtriu = C("ident"), C("negmask"), C("negtriu")
    sumsq, var, rstd = stat(2), stat(2), stat(2)

    c_raw, c_act, v_m = view(gates_mem, 0, 4, S), view(gates_mem, 1024, 4, S), view(gates_mem, 2048, TT, 512)
    v_mT, sig_z, m_q = (view(gates_mem, 1024 * n, 4, S) for n in (3, 4, 5))
    m_k, skip_c = view(gates_mem, 6144, 4, S), view(gates_mem, 7168, 4, S)
    q_d, k_d, v_d = view(qkv_a, 0, 4, S), view(qkv_a, 1024, 4, S), view(qkv_a, 2048, TT, 512)
    w_m, w_mT = view(qkv_b, 0, 4, 384), view(qkv_b, 1536, 4, 384)
    p_d, a_T, rel_row = view(p_mem, 0, 8, 384), view(pt_mem, 0, 4, 384), view(pt_mem, 0, 4, 384)
    square, bucket = view(pt_mem, 1536, TT, 512), pt_mem[0:REL_BUCKETS, 2560:2560 + 384]
    y_T, rel_bias = view(yt_mem, 0, 8, S), view(yt_mem, 2048, 4, S)
    w_mq, w_mk = view(yt_mem, 3072, 4, P), view(yt_mem, 3584, 4, P)
    h_m, y_d = view(xn_mem, 0, TT, 512), view(xn_mem, 1024, TT, 512)
    at1 = {n: prm[:, s.start - (1024 if s.start > PRM1["w_k"].start else 0):
                  s.stop - (1024 if s.start > PRM1["w_k"].start else 0)]
           for n, s in PRM1.items() if n not in ("w_q", "w_k")}
    conv_w = at1["conv_w"].rearrange("p (f w) -> p f w", w=CONV_W)
    lam_in = at1["lam"].rearrange("p (a b) -> p a b", a=4)
    w_gate = at1["w_gate"].rearrange("p (k n) -> p k n", n=8)
    w_r = at1["w_r"].rearrange("p (k n) -> p k n", n=36)
    gate_pre, log_f, lse = stat(16).rearrange("p (i n) -> p i n", i=2), stat(8), stat(8)
    m_max, m_neg, m_den, m_dec, m_abs = stat(8), stat(8), stat(8), stat(8), stat(8)
    neg_b, mean, var8, rstd8 = stat(8), stat(8), stat(8), stat(8)
    lam_two, lam = stat(2), stat(1)
    d_max, d_neg, d_sum, d_inv = stat(16), stat(16), stat(16), stat(16)
    mark = stat(1)
    logits = view(p_mem, 0, TT, 36)
    group8, le8, top8, one_g = (view(p_mem, 128 + 32 * n, TT, 8) for n in range(4))
    pick0, pick1, idx_f = (view(p_mem, 256 + 32 * n, TT, 8) for n in range(3))
    r_stat = view(p_mem, 352, 8, TT)
    gates_moe = view(p_mem, 384, TT, N_EXPERTS)
    sig_g = view(gates_mem, 0, 2, 2, 512)
    hid = view(gates_mem, 2048, 4, S)
    gain_row = view(pt_mem, 0, D)


    at2 = {n: prm[:, s] for n, s in PRM2.items()}
    cos_t, sin_t = rope_mem[:, 0:S], rope_mem[:, S:2 * S]
    gates, hid_ff = view(gates_mem, 0, 32, S), view(gates_mem, 0, 32, S)
    q_n, kv_c, k_sw = view(qkv_a, 0, 4, S), view(qkv_a, 1024, 2, S), view(qkv_a, 1536, 2, S)
    v_n = view(qkv_a, 2048, TT, S)
    k_cT, v_c = qkv_a[:, 2560:2560 + N_CMP], qkv_a[0:N_CMP, 2576:2576 + 2 * HD]
    hid_c, p_c = view(qkv_a, 2704, 2, 2, 2 * N_CMP), view(qkv_a, 2824, TT, HEADS, N_CMP)
    gelu_tmp, rope_tmp = pt_mem[:, 1600:1600 + 8 * N_CMP], view(pt_mem, 0, 6, S)
    rope_tmp_c = pt_mem[:, 1536:1536 + N_CMP]
    dup = view(p_mem, 0, 4, 2 * S)
    pc_T = view(yt_mem, 2048, HEADS, S)
    a_low, b_cum = xn_mem[0:GLA_RANK, 0:S], view(xn_mem, 256, 2, S)
    la_l, la_m = view(xn_mem, 768, 2, S), view(xn_mem, 1280, 2, S)
    p_s, pT_s = view(p_mem, 0, 8, 384), view(pt_mem, 0, 8, 384)
    q_s, k_s, v_s = view(qkv_b, 0, 4, S), view(qkv_b, 1024, 4, S), view(qkv_b, 2048, TT, 512)
    q_f, k_f, v_f = view(qkv_a, 0, 4, S), view(qkv_a, 1024, 4, S), view(qkv_a, 2048, TT, 512)
    q_g, k_g = view(qkv_b, 0, 2, S), view(qkv_b, 512, 2, S)
    v_g, g_g = view(qkv_b, 1024, TT, 512), view(qkv_b, 2048, TT, 512)
    decay, q_lv, k_lv = (view(p_mem, 1024 * n, 2, 2, S) for n in range(3))
    att, att_far = view(pt_mem, 0, 2, 4, P), view(pt_mem, 1024, 2, 2, P)
    o_g, square_g, sig_gg = view(pt_mem, 1536, TT, 512), view(qkv_a, 0, TT, 512), view(qkv_a, 1024, TT, 512)
    yT_all, mixed = view(yt_mem, 0, 16, S), view(xn_mem, 0, KT, S)
    fg = stat(64).rearrange("p (i n) -> p i n", i=TT)
    nsa_gate = fg[:, :, 8:32].rearrange("p i (r m b) -> p i m r b", r=NSA_GROUPS, b=3)
    lf_fox, lse_fox = stat(16), stat(16)
    s_max, s_neg, s_sum, s_inv = stat(32), stat(32), stat(32), stat(32)
    c_max, c_inv = stat(16), stat(16)
    wait_marks = stat(WAIT_MARKS)
    pos_i, ang, turns = p_mem[:, 2048:2304].bitcast(I32), p_mem[:, 2304:2560], p_mem[:, 2560:2816]

    bank_full = [sem(f"bank{b}_full") for b in range(BANKS)]
    bank_read = [sem(f"bank{b}_read") for b in range(BANKS)]
    w_landed = [sem(f"weights{s}_landed") for s in range(SLOTS)]
    x_loaded, const_loaded, params_loaded = sem("x_loaded"), sem("const_loaded"), sem("params_loaded")
    gain_loaded = sem("gain_loaded")
    act_step, dve_step, pool_step = sem("act_step"), sem("dve_step"), sem("pool_step")
    sumsq_ready, var_ready, rstd_ready = sem("sumsq_ready"), sem("var_ready"), sem("rstd_ready")
    xn_ready, x_ready = sem("xn_ready"), sem("x_ready")
    conv_ready, conv_sig, act_ready = sem("conv_ready"), sem("conv_sig"), sem("c_act_ready")
    lam_dots, lam_exp = sem("lam_dots"), sem("lam_exp")
    gates_pre, lse_ready, logf_ready = sem("gates_pre"), sem("lse_ready"), sem("logf_ready")
    rel_saved, rel_loaded = sem("rel_rows_saved"), sem("rel_bias_loaded")
    m_neg_ready, m_exp_ready, m_dec_in, m_dec_out = (sem("m_neg_ready"), sem("m_exp_ready"), sem("m_decay_in"),
                                                     sem("m_decay_out"))
    d_neg_ready, d_exp_ready, a_ready = sem("d_neg_ready"), sem("d_exp_ready"), sem("a_ready")
    centred, squared, var8_ready, rstd8_ready = (sem("centred"), sem("squared"), sem("var8_ready"),
                                                 sem("rstd8_ready"))
    head_norm = sem("head_normed")
    ym_ready, yd_ready = sem("ym_ready"), sem("yd_ready")
    r_neg, r_exp, top_diff, top_exp = sem("router_neg_max"), sem("router_exp"), sem("top_difference"), sem("top_exp")
    sig_ready = sem("expert_sigmoid_ready")
    stored = sem("stored")

    pre = plan_pre()
    moe = plan_moe(pre)
    MOE_TURNS = N_EXPERTS // UNROLL


    pos_loaded, angle_ready, rope_ready = sem("positions_loaded"), sem("angles_ready"), sem("rope_table_ready")
    params2_loaded = sem("layer_params_loaded")
    nsa_gate_ready, fox_sum, fox_lse, lf_ready = sem("nsa_gate_ready"), sem("fox_logit_ready"), sem("fox_lse_ready"), sem("fox_logf_ready")
    roped, dup_ready, gelu_in, gelu_sig, hid_ready = (sem("roped"), sem("windows_ready"), sem("gelu_in"), sem("gelu_sigmoid"),
                                                      sem("cmp_hidden_ready"))
    la_ready = sem("gla_lse_ready")
    c_in, c_exp, c_ready = sem("cmp_scores_ready"), sem("cmp_exp_ready"), sem("cmp_weights_ready")
    s_neg_ready, s_exp_ready, s_inv_ready, p_scaled = (sem("softmax_neg_max"), sem("softmax_exp"), sem("softmax_inverse"),
                                                       sem("softmax_scaled"))
    sb_log, sb_ready = sem("stick_log_ready"), sem("stick_softplus_ready")
    decay_in, decay_out, level_ready = sem("gla_decay_in"), sem("gla_decay_out"), sem("gla_level_ready")
    g_sig, gate_sig, y_gla = sem("gla_gate_sigmoid"), sem("gates_sigmoid"), sem("gla_y_ready")
    mixed_ready, relu_ready, ffh_ready = sem("mixed_ready"), sem("relu_ready"), sem("ff_hidden_ready")
    ff2_chunk = sem("ff2_chunk_used")
    layer = plan_layer(moe)
    LAYER_FIRST = PRE_CHUNKS + N_EXPERTS * EXPERT_CHUNKS
    SOFTMAXES = NSA_N + FOX_N

    def slot(c):
        return wring[:, (c % SLOTS) * CHUNK_COLS:(c % SLOTS + 1) * CHUNK_COLS]

    def landed(first, per, c, turn):
        return turn * (16 * per // SLOTS) + 16 * ((first + c) // SLOTS + 1)

    block = nc.Block()
    block.__enter__()

    @block.sync
    def _(sp):
        sp.dma_start(x, d["x"]).then_inc(x_loaded, 16)
        sp.dma_start(cst[:, :], d["const"][:, 0:CONST["bucket"].start]).then_inc(const_loaded, 16)
        sp.dma_start(prm[:, 0:PRM1["w_q"].start], d["prm1"][:, 0:PRM1["w_q"].start]).then_inc(params_loaded, 16)
        sp.dma_start(pos_i, d["pos"]).then_inc(pos_loaded, 16)
        sp.dma_start(slot(0), d["w1"][0]).then_inc(w_landed[0], 16)
        sp.dma_start(prm[:, PRM1["w_q"].start:PRM1_COLS - 1024],
                     d["prm1"][:, PRM1["w_k"].stop:PRM1_COLS]).then_inc(params_loaded, 16)
        sp.dma_start(yt_mem[:, 3072:4096], d["prm1"][:, PRM1["w_q"].start:PRM1["w_k"].stop]).then_inc(params_loaded, 16)
        sp.dma_start(bucket, d["const"][0:REL_BUCKETS, CONST["bucket"]]).then_inc(params_loaded, 16)
        pre_last = [pre[n][1] for n in ("c", "vm", "z", "qd", "kd", "vd")] + [pre["out"][1], pre["out"][3]]
        for c in range(1, PRE_CHUNKS):
            if c >= SLOTS:
                j = pre_last[c - SLOTS]
                sp.wait_ge(bank_full[j.bank], j.count())
            sp.dma_start(slot(c), d["w1"][c]).then_inc(w_landed[c % SLOTS], 16)
            if c == 3:
                for j in pre["rel"]:
                    sp.wait_ge(bank_read[j.bank], j.count())
                sp.dma_start(d["skew"].rearrange("(h p n) -> p h n", h=4, p=P)[:, :, 0:384], rel_row).then_inc(rel_saved, 16)
                sp.wait_ge(rel_saved, 16)
                sp.dma_start(rel_bias, bass.AP(d["skew"].tensor, 127, [[383, P], [384 * P, 4], [1, S]])).then_inc(rel_loaded, 16)
        for j in pre_last[-SLOTS:]:
            sp.wait_ge(bank_full[j.bank], j.count())
        sp.wait_ge(rel_loaded, 16)
        for j in pre["ydt"]:
            sp.wait_ge(bank_read[j.bank], j.count())
        sp.dma_start(gain_row, d["gain"][0]).then_inc(gain_loaded, 16)
        turn_chunks = UNROLL * EXPERT_CHUNKS
        with sp.Fori(0, MOE_TURNS) as turn:
            for c in range(turn_chunks):
                e, k = divmod((c - SLOTS) % turn_chunks, EXPERT_CHUNKS)
                j = moe["gud"[k], e][-1]
                sp.wait_ge(bank_full[j.bank], j.count(turn - 1 if c < SLOTS else turn))
                sp.dma_start(slot(c), d["w1"][PRE_CHUNKS + c + turn * turn_chunks]).then_inc(w_landed[c % SLOTS], 16)
        for e in range(UNROLL - 2, UNROLL):
            for k in "gud":
                j = moe[k, e][-1]
                sp.wait_ge(bank_full[j.bank], j.count(MOE_TURNS - 1))
        uses = {0: ("nsa_q", 1), 1: ("nsa_k", 1), 2: ("gla_a", 0), 3: ("hid", 0), 4: ("hid", 1), 8: ("gates", 1), 12: ("gates", 3)}
        uses |= {c: (n, 1) for c, n in ((5, "sb_q"), (6, "sb_k"), (7, "sb_v"), (9, "fox_q"), (10, "fox_k"), (11, "fox_v"),
                                        (13, "gla_qk"), (14, "gla_v"), (15, "gla_g"))}
        uses |= {16 + n: ("gates", 5 + 2 * n) for n in range(6)}
        uses |= {22 + n: ("branch", 4 * n + 3) for n in range(N_BRANCH)}
        uses |= {26 + n: ("out", 2 * n + 1) for n in range(2)} | {28 + n: ("ff1", 2 * n + 1) for n in range(8)}
        with sp.Fori(0, LAYERS) as l:
            for j in layer["h2"]:
                sp.wait_ge(bank_read[j.bank], j.count(l - 1))
            sp.dma_start(prm[:, 0:PRM2_COLS], d["prm2"][l]).then_inc(params2_loaded, 16)
            for c in range(LAYER_CHUNKS):
                before = (c - SLOTS) % LAYER_CHUNKS
                turn = l - 1 if c < SLOTS else l
                if before < 36:
                    n, k = uses[before]
                    j = layer[n][k]
                    sp.wait_ge(bank_full[j.bank], j.count(turn))
                elif before < LAYER_CHUNKS - 1 and c >= SLOTS:
                    sp.wait_ge(ff2_chunk, l * 7 + (before - 35))
                elif c < SLOTS:
                    j = layer["ff2"][3]
                    sp.wait_ge(bank_full[j.bank], j.count(turn))
                sp.dma_start(slot(c), d["w2"][c + l * LAYER_CHUNKS]).then_inc(w_landed[c % SLOTS], 16)
        for j in layer["h2"]:
            sp.wait_ge(bank_full[j.bank], j.count(LAYERS - 1))
        sp.dma_start(gain_row, d["gain"][1]).then_inc(gain_loaded, 16)
        sp.wait_ge(x_ready, LAYERS + 2)
        sp.dma_start(d["out"], x).then_inc(stored, 16)
        sp.wait_ge(stored, 16)

    @block.tensor
    def _(pe):
        def free(j, turn=0):
            if not (isinstance(turn, int) and j.count(turn) == 1):
                pe.wait_ge(bank_read[j.bank], j.count(turn) - 1)

        def in_sbuf(jobs, turn=0, then=None):
            for j in last_in_bank(jobs, then):
                pe.wait_ge(bank_read[j.bank], j.count(turn))

        def chunk(c, first, per=0, turn=0):
            pe.wait_ge(w_landed[c % SLOTS], landed(first, per, c, turn))
            return slot(c)

        def turn_x(jobs, turn=0):
            for n, j in enumerate(jobs):
                free(j, turn)
                for t in range(2):
                    for i in range(TT):
                        dt = 2 * n + t
                        mm = pe.transpose(psum[j.bank][:, t * S + i * P:t * S + (i + 1) * P],
                                          xn[:, i, dt * P:(dt + 1) * P], ident)
                mm.then_inc(bank_full[j.bank], 1)

        def project_a(j, w, ft, turn=0, src=hT, kts=KT):
            free(j, turn)
            for t in range(2):
                for k in range(kts):
                    mm = pe.matmul(psum[j.bank][:, t * S:(t + 1) * S], w[:, k, (ft + t) * P:(ft + t + 1) * P],
                                   src[:, k, :], start=(k == 0), stop=(k == kts - 1))
            mm.then_inc(bank_full[j.bank], 1)

        def project_b(j, w, i, n, turn=0, src=hT):
            free(j, turn)
            for k in range(KT):
                mm = pe.matmul(psum[j.bank][:, 0:n], src[:, k, i * P:(i + 1) * P], w[:, k, 0:n],
                               start=(k == 0), stop=(k == KT - 1))
            mm.then_inc(bank_full[j.bank], 1)

        def scores(j, q, k, turn=0):
            free(j, turn)
            pe.matmul(psum[j.bank][:, 0:P], q[:, 0:P], k[:, 0:P], start=True, stop=True)
            mm = pe.matmul(psum[j.bank][:, P:384], q[:, P:S], k[:, 0:S], start=True, stop=True)
            mm.then_inc(bank_full[j.bank], 1)

        def turn_three(j, src, turn=0):
            free(j, turn)
            for b in range(3):
                mm = pe.transpose(psum[j.bank][:, b * P:(b + 1) * P], src[:, b * P:(b + 1) * P], ident)
            mm.then_inc(bank_full[j.bank], 1)

        def mix_heads(j, i, wT, v, turn=0):
            free(j, turn)
            for h in range(4):
                out = psum[j.bank][:, h * P:(h + 1) * P]
                if i == 0:
                    mm = pe.matmul(out, wT[:, h, 0:P], v[:, 0, h * P:(h + 1) * P], start=True, stop=True)
                else:
                    pe.matmul(out, wT[:, h, P:2 * P], v[:, 0, h * P:(h + 1) * P], start=True, stop=False)
                    mm = pe.matmul(out, wT[:, h, 2 * P:384], v[:, 1, h * P:(h + 1) * P], start=False, stop=True)
            mm.then_inc(bank_full[j.bank], 1)

        def turn_four(j, src, turn=0):
            free(j, turn)
            for h in range(4):
                mm = pe.transpose(psum[j.bank][:, h * P:(h + 1) * P], src[:, h * P:(h + 1) * P], ident)
            mm.then_inc(bank_full[j.bank], 1)

        def project_out(jobs, first, c0, per=0, turn=0):
            def run(src):
                for half in range(2):
                    w = chunk(c0 + half, first, per, turn).rearrange("p (k n) -> p k n", k=KT)
                    for i in range(TT):
                        project_b(jobs[2 * half + i], w, i, 512, turn, src)
            return run

        k8 = lambda w: w.rearrange("p (k n) -> p k n", k=KT)

        pe.wait_ge(const_loaded, 16)
        pe.wait_ge(xn_ready, 2)
        turn_x(pre["ht"])
        in_sbuf(pre["ht"])
        for j in range(2):
            project_a(pre["c"][j], k8(chunk(0, 0)), 2 * j)
        for i in range(TT):
            project_b(pre["vm"][i], k8(chunk(1, 0)), i, 512)
        for j in range(2):
            project_a(pre["z"][j], k8(chunk(2, 0)), 2 * j)
        pe.wait_ge(params_loaded, 64)
        for h, j in enumerate(pre["rel"]):
            free(j)
            pe.matmul(psum[j.bank][:, 0:384], at1["rel"][0:REL_BUCKETS, h:h + 1].to_broadcast([REL_BUCKETS, P]),
                      bucket, start=True, stop=True).then_inc(bank_full[j.bank], 1)
        pe.wait_ge(act_ready, 4)
        for name, w in (("mq", w_mq), ("mk", w_mk)):
            for n, j in enumerate(pre[name]):
                free(j)
                for t in range(2):
                    mm = pe.matmul(psum[j.bank][:, t * S:(t + 1) * S], w[:, 2 * n + t, :], c_act[:, 2 * n + t, :],
                                   start=True, stop=True)
                mm.then_inc(bank_full[j.bank], 1)
        in_sbuf(pre["vm"])
        for n, j in enumerate(pre["vmt"]):
            free(j)
            for t in range(2):
                for i in range(TT):
                    ft = 2 * n + t
                    mm = pe.transpose(psum[j.bank][:, t * S + i * P:t * S + (i + 1) * P],
                                      v_m[:, i, ft * P:(ft + 1) * P], ident)
            mm.then_inc(bank_full[j.bank], 1)
        in_sbuf(pre["mq"] + pre["mk"] + pre["vmt"])
        j = pre["gate"][0]
        free(j)
        for i in range(TT):
            for k in range(12):
                src = (m_q, m_k, v_mT)[k // 4]
                mm = pe.matmul(psum[j.bank][:, 8 * i:8 * i + 8], src[:, k % 4, i * P:(i + 1) * P], w_gate[:, k, :],
                               start=(k == 0), stop=(k == 11))
        mm.then_inc(bank_full[j.bank], 1)
        for j in range(2):
            project_a(pre["qd"][j], k8(chunk(3, 0)), 2 * j)
        for j in range(2):
            project_a(pre["kd"][j], k8(chunk(4, 0)), 2 * j)
        for i in range(TT):
            project_b(pre["vd"][i], k8(chunk(5, 0)), i, 512)

        pe.wait_ge(logf_ready, 1)
        lf = log_f.rearrange("p (i n) -> p i n", i=2)
        j = pre["negb"][0]
        free(j)
        pe.matmul(psum[j.bank][:, 0:4], negtriu[:, 0:P], lf[:, 0, :], start=True, stop=True)
        pe.matmul(psum[j.bank][:, 4:8], negtriu[:, P:S], lf[:, 0, :], start=True, stop=False)
        pe.matmul(psum[j.bank][:, 4:8], negtriu[:, 0:P], lf[:, 1, :], start=False, stop=True).then_inc(bank_full[j.bank], 1)
        for h in range(ML_HEADS):
            j = pre["u"][h]
            free(j)
            b = psum[j.bank]
            lf_h = [lf[:, i, h:h + 1].to_broadcast([P, P]) for i in range(TT)]
            ig_h = [gate_pre[:, i, h:h + 1].to_broadcast([P, P]) for i in range(TT)]
            pe.matmul(b[:, 0:S], lf_h[0], negtriu, start=True, stop=False)
            pe.matmul(b[:, P:S], lf_h[1], negtriu[:, 0:P], start=False, stop=False)
            pe.matmul(b[:, 0:P], ig_h[0], ident, start=False, stop=False)
            pe.matmul(b[:, P:S], ig_h[1], ident, start=False, stop=True).then_inc(bank_full[j.bank], 1)
            scores(pre["qk"][h], m_q[:, h, :], m_k[:, h, :])
        in_sbuf(pre["qd"] + pre["kd"])
        for n in range(2 * DA_HEADS):
            h, r = n // 2, slice(DA_QD * (n % 2), DA_QD * (n % 2) + DA_QD)
            scores(pre["s"][n], q_d[r, h, :], k_d[r, h, :])
            if n % 2:
                in_sbuf([pre["qk"][h]])
                turn_three(pre["wt"][h], w_m[:, h, :])
        in_sbuf(pre["wt"])
        for i in range(TT):
            mix_heads(pre["num"][i], i, w_mT, v_m)
        for h in range(DA_HEADS):
            pe.wait_ge(a_ready, h + 1)
            turn_three(pre["at"][h], p_d[:, 2 * h, :])
        in_sbuf(pre["at"] + pre["vd"])
        for i in range(TT):
            mix_heads(pre["pv"][i], i, a_T, v_d)
        pe.wait_ge(head_norm, 1)
        for i in range(TT):
            turn_four(pre["hnt"][i], h_m[:, i, :])
        pe.wait_ge(head_norm, 2)
        for i in range(TT):
            turn_four(pre["ydt"][i], y_d[:, i, :])
        pe.wait_ge(ym_ready, 2)
        in_sbuf(pre["ydt"])
        project_out(pre["out"], 0, 6)(y_T)
        pe.wait_ge(xn_ready, 4)
        turn_x(pre["h2"])
        in_sbuf(pre["h2"])
        j = pre["router"][0]
        free(j)
        for i in range(TT):
            for k in range(KT):
                mm = pe.matmul(psum[j.bank][:, 36 * i:36 * i + 36], hT[:, k, i * P:(i + 1) * P], w_r[:, k, :],
                               start=(k == 0), stop=(k == KT - 1))
        mm.then_inc(bank_full[j.bank], 1)
        with pe.Fori(0, MOE_TURNS) as turn:
            for e in range(UNROLL):
                per = UNROLL * EXPERT_CHUNKS
                wg, wu = (k8(chunk(EXPERT_CHUNKS * e + n, PRE_CHUNKS, per, turn)) for n in range(2))
                for half in range(2):
                    project_a(moe["g", e][half], wg, 2 * half, turn)
                    project_a(moe["u", e][half], wu, 2 * half, turn)
                wd = chunk(EXPERT_CHUNKS * e + 2, PRE_CHUNKS, per, turn).rearrange("p (k n) -> p k n", k=4)
                for ft in range(4):
                    if ft % 2 == 0:
                        in_sbuf([moe["u", e][ft // 2]], turn, moe["d", e][0] if ft == 0 else None)
                    for n, j in enumerate(moe["d", e]):
                        i, half = divmod(n, 2)
                        if ft == 0:
                            free(j, turn)
                        mm = pe.matmul(psum[j.bank][:, :], hid[:, ft, i * P:(i + 1) * P],
                                       wd[:, ft, half * 512:(half + 1) * 512], start=(ft == 0), stop=(ft == 3))
                        if ft == 3:
                            mm.then_inc(bank_full[j.bank], 1)
        def rope(j, tiles, turn, n=S):
            free(j, turn)
            for t, src in enumerate(tiles):
                mm = pe.matmul(psum[j.bank][:, t * S:t * S + n], C("rope"), src, start=True, stop=True)
            mm.then_inc(bank_full[j.bank], 1)

        def heads_out(j, lhs, rhs, turn):
            free(j, turn)
            for r in range(2):
                rows = slice(HD * r, HD * r + HD)
                pe.matmul(psum[j.bank][rows, 0:S], lhs[r][0], rhs[r][:, 0:S], start=True, stop=False)
                mm = pe.matmul(psum[j.bank][rows, P:S], lhs[r][1], rhs[r][:, S:384], start=False, stop=True)
            mm.then_inc(bank_full[j.bank], 1)

        with pe.Fori(0, LAYERS) as l:
            lay = lambda c: chunk(c, LAYER_FIRST, LAYER_CHUNKS, l)
            fill_chunk = {"sb_q": 5, "sb_k": 6, "sb_v": 7, "fox_q": 9, "fox_k": 10, "fox_v": 11, "gla_qk": 13, "gla_v": 14,
                          "gla_g": 15}
            gate_chunk = [8, 12, 16, 17, 18, 19, 20, 21]

            def fill(name, n):
                if name == "gates":
                    project_a(layer[name][n], k8(lay(gate_chunk[n // 2])), 2 * (n % 2), l)
                elif name in ("sb_v", "fox_v", "gla_v", "gla_g"):
                    project_b(layer[name][n], k8(lay(fill_chunk[name])), n, 512, l)
                else:
                    project_a(layer[name][n], k8(lay(fill_chunk[name])), 2 * n, l)

            pe.wait_ge(params2_loaded, 16 * l + 16)
            pe.wait_ge(xn_ready, 4 * l + 8)
            turn_x(layer["ht"], l)
            in_sbuf(layer["ht"], l, layer["nsa_q"][0])
            for n, c in (("nsa_q", 0), ("nsa_k", 1)):
                for j in range(2):
                    project_a(layer[n][j], k8(lay(c)), 2 * j, l)
            w = k8(lay(2))
            for i in range(TT):
                project_b(layer["nsa_v"][i], w, i, 288, l)
            j = layer["gla_a"][0]
            free(j, l)
            for k in range(KT):
                mm = pe.matmul(psum[j.bank][0:GLA_RANK, 0:S], w[:, k, 288:288 + GLA_RANK], hT[:, k, :],
                               start=(k == 0), stop=(k == KT - 1))
            mm.then_inc(bank_full[j.bank], 1)
            in_sbuf(layer["nsa_q"] + layer["nsa_k"] + layer["gla_a"], l, layer["rope_q"][0])
            for n in range(2):
                rope(layer["rope_q"][n], [q_n[:, 2 * n + t, :] for t in range(2)], l)
            rope(layer["rope_k"][0], [k_sw[:, t, :] for t in range(2)], l)
            for n, j in enumerate(layer["dup"]):
                free(j, l)
                for g in range(NSA_GROUPS):
                    mm = pe.matmul(psum[j.bank][:, g * S:(g + 1) * S], C("dup")[:, g * P:(g + 1) * P], kv_c[:, n, :],
                                   start=True, stop=True)
                mm.then_inc(bank_full[j.bank], 1)
            for n, j in enumerate(layer["hid"]):
                w = lay(3 + n).rearrange("p (k n) -> p k n", k=16)
                pe.wait_ge(dup_ready, 8 * l + 4 * n + 4)
                free(j, l)
                for half in range(2):
                    for k in range(16):
                        win = dup[:, 2 * n + k // 8, :].rearrange("p (g c s) -> p g c s", g=2, s=CMP_STRIDE)
                        mm = pe.matmul(psum[j.bank][:, half * 30:half * 30 + 30].rearrange("p (g c) -> p g c", g=2),
                                       w[:, k, half * P:(half + 1) * P],
                                       win[:, :, k // 8:k // 8 + N_CMP, 2 * (k % 8)], start=(k == 0), stop=(k == 15))
                mm.then_inc(bank_full[j.bank], 1)
            pe.wait_ge(hid_ready, l + 1)
            j = layer["kc"][0]
            free(j, l)
            for g in range(NSA_GROUPS):
                for half in range(2):
                    mm = pe.matmul(psum[j.bank][g * HD:(g + 1) * HD, 0:N_CMP], at2["w_k2"][:, half * HD:(half + 1) * HD],
                                   hid_c[:, 0, half, g * N_CMP:(g + 1) * N_CMP], start=(half == 0), stop=(half == 1))
            mm.then_inc(bank_full[j.bank], 1)
            j = layer["vc"][0]
            free(j, l)
            for g in range(NSA_GROUPS):
                for half in range(2):
                    mm = pe.matmul(psum[j.bank][0:N_CMP, g * HD:(g + 1) * HD], hid_c[:, 1, half, g * N_CMP:(g + 1) * N_CMP],
                                   at2["w_v2"][:, half * HD:(half + 1) * HD], start=(half == 0), stop=(half == 1))
            mm.then_inc(bank_full[j.bank], 1)
            in_sbuf(layer["kc"], l, layer["rope_c"][0])
            rope(layer["rope_c"][0], [k_cT], l, N_CMP)
            j = layer["gla_la"][0]
            free(j, l)
            for t in range(2):
                mm = pe.matmul(psum[j.bank][:, t * S:(t + 1) * S], at2["w_alpha"][0:GLA_RANK, t * P:(t + 1) * P], a_low,
                               start=True, stop=True)
            mm.then_inc(bank_full[j.bank], 1)
            pe.wait_ge(roped, 4 * l + 4)
            for r, j in enumerate(layer["cs"]):
                free(j, l)
                rows = slice(HD * r, HD * r + HD)
                for i in range(TT):
                    for m in range(NSA_HPG):
                        at = (NSA_HPG * i + m) * N_CMP
                        mm = pe.matmul(psum[j.bank][:, at:at + N_CMP], q_n[rows, m, i * P:(i + 1) * P], k_cT[rows, :],
                                       start=True, stop=True)
                mm.then_inc(bank_full[j.bank], 1)
            pe.wait_ge(c_ready, l + 1)
            for n, j in enumerate(layer["ct"]):
                free(j, l)
                for r in range(2):
                    for i in range(TT):
                        mm = pe.transpose(psum[j.bank][0:N_CMP, r * S + i * P:r * S + (i + 1) * P], p_c[:, i, 2 * n + r, :], ident)
                mm.then_inc(bank_full[j.bank], 1)
            in_sbuf(layer["nsa_v"] + layer["vc"] + layer["ct"], l, layer["nsa", "score", 0][0])
            for kind, n in nsa_steps():
                if kind == "fill":
                    fill(*n)
                    continue
                j = layer["nsa", kind, n][0]
                if kind == "score":
                    m, r, br = n // 4, n // 2 % 2, n % 2
                    rows = slice(HD * r, HD * r + HD)
                    scores(j, q_n[rows, m, :], k_sw[rows, br, :], l)
                elif kind == "turn":
                    pe.wait_ge(p_scaled, SOFTMAXES * l + n + 1)
                    turn_three(j, p_s[:, n % 8, :], l)
                else:
                    in_sbuf([layer["nsa", "turn", 4 * n + k][0] for k in range(4)], l, j)
                    free(j, l)
                    for r in range(2):
                        out = psum[j.bank][HD * r:HD * r + HD, :]
                        pe.matmul(out[:, 0:S], v_c[:, r * HD:(r + 1) * HD], pc_T[0:N_CMP, 2 * n + r, :], start=True, stop=False)
                        for br in range(2):
                            wT, cols = pT_s[:, (4 * n + 2 * r + br) % 8, :], slice(br * P + r * HD, br * P + r * HD + HD)
                            pe.matmul(out[:, 0:S], v_n[:, 0, cols], wT[:, 0:S], start=False, stop=False)
                            mm = pe.matmul(out[:, P:S], v_n[:, 1, cols], wT[:, S:384], start=False, stop=(br == 1))
                    mm.then_inc(bank_full[j.bank], 1)
            in_sbuf(layer["sb_q"] + layer["sb_k"] + layer["sb_v"], l, layer["sb", "score", 0][0])

            def stick(j, n, stop):
                rows = slice(HD * (n % 2), HD * (n % 2) + HD)
                q, k = q_s[rows, n // 2, :], k_s[rows, n // 2, :]
                near = pe.matmul(psum[j.bank][:, 0:S], k[:, 0:P], q, start=True, stop=stop)
                if stop:
                    return pe.matmul(psum[j.bank][:, S:384], k[:, P:S], q[:, P:S], start=True, stop=True)
                sp_ = p_s[:, n, :]
                b = psum[j.bank]
                pe.matmul(b[:, 0:S], C("sufneg"), sp_[:, 0:S], start=False, stop=False)
                pe.matmul(b[:, P:S], negtriu[:, P:S], sp_[:, S:384], start=False, stop=False)
                pe.matmul(b[:, 0:P], ident, C("negstrict"), start=False, stop=True)
                pe.matmul(b[:, S:384], k[:, P:S], q[:, P:S], start=True, stop=False)
                pe.matmul(b[:, S:384], C("sufneg"), sp_[:, S:384], start=False, stop=False)
                return pe.matmul(b[:, S:384], ident, C("negstrict"), start=False, stop=True)

            for kind, n in sb_steps():
                if kind == "fill":
                    fill(*n)
                    continue
                j = layer["sb", kind, n][0]
                if kind == "score":
                    free(j, l)
                    stick(j, n, True).then_inc(bank_full[j.bank], 1)
                elif kind == "again":
                    pe.wait_ge(sb_ready, 8 * l + n + 1)
                    free(j, l)
                    stick(j, n, False).then_inc(bank_full[j.bank], 1)
                else:
                    in_sbuf([layer["sb", "again", 2 * n + r][0] for r in range(2)], l, j)
                    heads_out(j, [[v_s[:, i, (2 * n + r) * HD:(2 * n + r + 1) * HD] for i in range(TT)] for r in range(2)],
                              [pT_s[:, 2 * n + r, :] for r in range(2)], l)
            in_sbuf(layer["fox_q"] + layer["fox_k"] + layer["fox_v"], l, layer["fox", "score", 0][0])
            pe.wait_ge(lf_ready, l + 1)
            lf2 = lf_fox.rearrange("p (i n) -> p i n", i=2)
            for kind, n in fox_steps():
                if kind == "fill":
                    fill(*n)
                    continue
                j = layer["fox", kind, n][0]
                if kind == "score":
                    free(j, l)
                    rows = slice(HD * (n % 2), HD * (n % 2) + HD)
                    q, k = q_f[rows, n // 2, :], k_f[rows, n // 2, :]
                    lf_h = [lf2[:, i, n:n + 1].to_broadcast([P, P]) for i in range(TT)]
                    b = psum[j.bank]
                    pe.matmul(b[:, 0:P], q[:, 0:P], k[:, 0:P], start=True, stop=False)
                    pe.matmul(b[:, 0:P], lf_h[0], negtriu[:, 0:P], start=False, stop=True)
                    pe.matmul(b[:, P:384], q[:, P:S], k, start=True, stop=False)
                    pe.matmul(b[:, P:384], lf_h[0], negtriu, start=False, stop=False)
                    pe.matmul(b[:, S:384], lf_h[1], negtriu[:, 0:P], start=False, stop=True).then_inc(bank_full[j.bank], 1)
                elif kind == "turn":
                    pe.wait_ge(p_scaled, SOFTMAXES * l + NSA_N + n + 1)
                    turn_three(j, p_s[:, n, :], l)
                else:
                    in_sbuf([layer["fox", "turn", 2 * n + r][0] for r in range(2)], l, j)
                    heads_out(j, [[v_f[:, i, (2 * n + r) * HD:(2 * n + r + 1) * HD] for i in range(TT)] for r in range(2)],
                              [pT_s[:, 2 * n + r, :] for r in range(2)], l)
            in_sbuf(layer["gla_qk"], l, layer["gla", "level", 0][0])
            for kind, n in gla_steps():
                if kind == "fill":
                    fill(*n)
                    continue
                if n < len(GLA_LEVELS):
                    pe.wait_ge(level_ready, 8 * l + n + 1)
                    q, k = q_lv[:, n % 2], k_lv[:, n % 2]
                else:
                    q, k = q_g, k_g
                for r, j in enumerate(layer["gla", kind, n]):
                    free(j, l)
                    rows = slice(HD * r, HD * r + HD)
                    for i in range(1 if n == 0 else TT):
                        for t in range(2):
                            keys, queries = (slice(0, P), slice(P, S)) if n == 0 else (slice(i * P, (i + 1) * P),) * 2
                            mm = pe.matmul(psum[j.bank][:, (2 * i + t) * P:(2 * i + t + 1) * P], k[rows, t, keys],
                                           q[rows, t, queries], start=True, stop=True)
                    mm.then_inc(bank_full[j.bank], 1)
            in_sbuf(layer["gla_v"] + [j for n in range(9) for j in layer["gla", "level", n]], l, layer["gla_o"][0])
            for i, j in enumerate(layer["gla_o"]):
                free(j, l)
                for h in range(GLA_HEADS):
                    out, cols = psum[j.bank][:, h * P:(h + 1) * P], slice(h * P, (h + 1) * P)
                    if i:
                        pe.matmul(out, att_far[:, h % 2, h // 2, :], v_g[:, 0, cols], start=True, stop=False)
                    mm = pe.matmul(out, att[:, h % 2, 2 * i + h // 2, :], v_g[:, i, cols], start=(i == 0), stop=True)
                mm.then_inc(bank_full[j.bank], 1)

            def branch(n):
                w = lay(22 + n).rearrange("p (k n) -> p k n", k=4)
                for k in range(4):
                    project_a(layer["branch"][4 * n + k], w, 2 * k, l, yT_all[:, 4 * n:4 * n + 4, :], 4)

            in_sbuf([layer[mixer, "value", n][0] for mixer in ("nsa", "sb", "fox") for n in range(4)], l, layer["gla_t"][0])
            pe.wait_ge(y_gla, l + 1)
            for i, j in enumerate(layer["gla_t"]):
                turn_four(j, o_g[:, i, :], l)
            for n in range(3):
                branch(n)
            in_sbuf(layer["gla_t"], l, layer["branch"][12])
            branch(3)
            pe.wait_ge(mixed_ready, 4 * l + 4)
            project_out(layer["out"], LAYER_FIRST, 26, LAYER_CHUNKS, l)(mixed)
            pe.wait_ge(xn_ready, 4 * l + 10)
            turn_x(layer["h2"], l)
            in_sbuf(layer["h2"], l, layer["ff1"][0])
            for c in range(8):
                for k in range(2):
                    project_a(layer["ff1"][2 * c + k], k8(lay(28 + c)), 2 * k, l)
            for c in range(8):
                w = lay(36 + c).rearrange("p (k n) -> p k n", k=4)
                pe.wait_ge(ffh_ready, 16 * l + 2 * c + 2)
                for k in range(4):
                    for n, j in enumerate(layer["ff2"]):
                        half, i = divmod(n, 2)
                        first, last = c == 0 and k == 0, c == 7 and k == 3
                        if first:
                            free(j, l)
                        mm = pe.matmul(psum[j.bank][:, :], hid_ff[:, 4 * c + k, i * P:(i + 1) * P],
                                       w[:, k, half * 512:(half + 1) * 512], start=first, stop=last)
                        if last:
                            mm.then_inc(bank_full[j.bank], 1)
                if c < 7:
                    mm.then_inc(ff2_chunk, 1)

    @block.scalar
    def _(act):
        steps = Steps()

        def then(ins):
            ins.then_inc(act_step, 1)
            act.wait_ge(act_step, steps.next())

        def full(j, turn=0):
            act.wait_ge(bank_full[j.bank], j.count(turn))

        def copy(j, out, scale=1.0, turn=0, cols=512):
            full(j, turn)
            act.activation(out, psum[j.bank][:, 0:cols], ACT.Copy, scale=scale).then_inc(bank_read[j.bank], 1)

        def squares():
            for i in range(TT):
                act.activation(xn[:, i, :], x[:, i, :], ACT.Square, accum_out=sumsq[:, i:i + 1]).then_inc(sumsq_ready, 1)

        flat = lambda v: v.rearrange("p a b -> p (a b)")

        act.wait_ge(x_loaded, 16)
        squares()
        act.wait_ge(params_loaded, 64)
        for n, j in enumerate(pre["c"]):
            copy(j, flat(c_raw[:, 2 * n:2 * n + 2, :]))
        act.wait_ge(angle_ready, 1)
        act.activation(rope_mem[:, :], rope_mem[:, :], ACT.Sin).then_inc(rope_ready, 1)
        for i, j in enumerate(pre["vm"]):
            copy(j, v_m[:, i, :])
        act.wait_ge(conv_ready, 4)
        act.activation(flat(c_raw), flat(c_act), ACT.Sigmoid).then_inc(conv_sig, 1)
        for n, j in enumerate(pre["z"]):
            full(j)
            act.activation(flat(sig_z[:, 2 * n:2 * n + 2, :]), psum[j.bank][:, :], ACT.Sigmoid).then_inc(bank_read[j.bank], 1)
        for h, j in enumerate(pre["rel"]):
            copy(j, rel_row[:, h, :], cols=384)
        for name, dst in (("mq", m_q), ("mk", m_k), ("vmt", v_mT)):
            for n, j in enumerate(pre[name]):
                copy(j, flat(dst[:, 2 * n:2 * n + 2, :]))
        for n, j in enumerate(pre["qd"]):
            copy(j, flat(q_d[:, 2 * n:2 * n + 2, :]), scale=DA_QD ** -0.5)
        for n, j in enumerate(pre["kd"]):
            copy(j, flat(k_d[:, 2 * n:2 * n + 2, :]))
        act.wait_ge(gates_pre, 1)
        lse3 = lse.rearrange("p (i n) -> p i n", i=2)
        then(act.activation(lse3, gate_pre[:, :, 4:8], ACT.Abs))
        then(act.activation(lse, lse, ACT.Exp, scale=-1.0))
        act.activation(lse, lse, ACT.Ln, bias=C("one")).then_inc(lse_ready, 1)
        for i, j in enumerate(pre["vd"]):
            copy(j, v_d[:, i, :])
        act.wait_ge(lam_dots, 1)
        act.activation(lam_two, lam_two, ACT.Exp).then_inc(lam_exp, 1)

        def m_exp(h):
            act.wait_ge(m_neg_ready, h + 1)
            act.activation(w_m[:, h, 0:P], w_m[:, h, 0:P], ACT.Exp, bias=m_neg[:, h:h + 1])
            act.activation(w_m[:, h, P:384], w_m[:, h, P:384], ACT.Exp, bias=m_neg[:, 4 + h:5 + h]).then_inc(m_exp_ready, 1)

        def d_exp(n):
            act.wait_ge(d_neg_ready, n + 1)
            act.activation(p_d[:, n, 0:P], p_d[:, n, 0:P], ACT.Exp, bias=d_neg[:, 2 * n:2 * n + 1],
                           accum_out=d_sum[:, 2 * n:2 * n + 1])
            act.activation(p_d[:, n, P:384], p_d[:, n, P:384], ACT.Exp, bias=d_neg[:, 2 * n + 1:2 * n + 2],
                           accum_out=d_sum[:, 2 * n + 1:2 * n + 2]).then_inc(d_exp_ready, 1)

        for h in range(ML_HEADS):
            m_exp(h)
        act.wait_ge(m_dec_in, 1)
        act.activation(m_dec, m_dec, ACT.Exp).then_inc(m_dec_out, 1)
        for n in range(2 * DA_HEADS):
            d_exp(n)
            if n % 2:
                copy(pre["wt"][n // 2], w_mT[:, n // 2, :], cols=384)
        act.wait_ge(centred, 1)
        act.activation(flat(square), flat(h_m), ACT.Square).then_inc(squared, 1)
        for h, j in enumerate(pre["at"]):
            copy(j, a_T[:, h, :], cols=384)
        act.wait_ge(var8_ready, 1)
        for i, j in enumerate(pre["pv"]):
            full(j)
            act.activation(square[:, i, :], psum[j.bank][:, :], ACT.Square).then_inc(squared, 1)
            copy(j, y_d[:, i, :])
        for j in pre["out"]:
            act.wait_ge(bank_read[j.bank], j.count())
        squares()
        for i in range(TT):
            act.wait_ge(r_neg, i + 1)
            act.activation(pick0[:, i, 0:4], logits[:, i, 0:4], ACT.Exp, bias=r_stat[:, 0, i:i + 1],
                           accum_out=r_stat[:, 1, i:i + 1]).then_inc(r_exp, 1)
        for i in range(TT):
            act.wait_ge(top_diff, i + 1)
            act.activation(r_stat[:, 2, i:i + 1], r_stat[:, 2, i:i + 1], ACT.Exp).then_inc(top_exp, 1)
        with act.Fori(0, MOE_TURNS) as turn:
            for e in range(UNROLL):
                for half in range(2):
                    j = moe["g", e][half]
                    full(j, turn)
                    act.activation(sig_g[:, e % 2, half, :], psum[j.bank][:, :], ACT.Sigmoid).then_inc(sig_ready, 1)
        for j in moe["d", UNROLL - 1]:
            act.wait_ge(bank_read[j.bank], j.count(MOE_TURNS - 1))
        squares()
        with act.Fori(0, LAYERS) as l:
            steps.enter(l, ACT_STEPS)
            act.wait_ge(params2_loaded, 16 * l + 16)
            act.wait_ge(x_ready, l + 1)
            squares()

            def fill(name, n):
                j = layer[name][n]
                pair = slice(2 * n, 2 * n + 2)
                if name == "gates":
                    full(j, l)
                    for t in range(2):
                        ins = act.activation(gates[:, 2 * n + t, :], psum[j.bank][:, t * S:(t + 1) * S], ACT.Identity,
                                             bias=at2["b_gate"][:, 2 * n + t:2 * n + t + 1])
                    ins.then_inc(bank_read[j.bank], 1)
                elif name in ("sb_v", "fox_v", "gla_v", "gla_g"):
                    copy(j, {"sb_v": v_s, "fox_v": v_f, "gla_v": v_g, "gla_g": g_g}[name][:, n, :], turn=l)
                elif name == "gla_qk":
                    copy(j, flat((q_g, k_g)[n]), scale=(GLA_DK ** -0.5, 1.0)[n], turn=l)
                else:
                    copy(j, flat({"sb_q": q_s, "sb_k": k_s, "fox_q": q_f, "fox_k": k_f}[name][:, pair, :]),
                         scale=HD ** -0.5 if name[-1] == "q" else 1.0, turn=l)

            for n, j in enumerate(layer["nsa_q"]):
                copy(j, flat(q_n[:, 2 * n:2 * n + 2, :]), scale=HD ** -0.5, turn=l)
            copy(layer["nsa_k"][0], flat(kv_c), turn=l)
            copy(layer["nsa_k"][1], flat(k_sw), turn=l)
            for i, j in enumerate(layer["nsa_v"]):
                full(j, l)
                act.activation(fg[:, i, :], psum[j.bank][:, S:S + 32], ACT.Copy)
                copy(j, v_n[:, i, :], turn=l, cols=S)
            j = layer["gla_a"][0]
            full(j, l)
            act.activation(a_low, psum[j.bank][0:GLA_RANK, 0:S], ACT.Copy).then_inc(bank_read[j.bank], 1)
            for j in last_in_bank(layer["nsa_v"]):
                act.wait_ge(bank_read[j.bank], j.count(l))
            act.activation(fg[:, :, 8:32], fg[:, :, 8:32], ACT.Sigmoid).then_inc(nsa_gate_ready, 1)
            for n, j in enumerate(layer["hid"]):
                full(j, l)
                act.activation(hid_c[:, n].rearrange("p a b -> p (a b)"), psum[j.bank][:, 0:4 * N_CMP], ACT.Copy).then_inc(bank_read[j.bank], 1)
            act.wait_ge(gelu_in, l + 1)
            act.activation(gelu_tmp, gelu_tmp, ACT.Sigmoid, scale=2.0 * float(np.sqrt(2.0 / np.pi))).then_inc(gelu_sig, 1)
            j = layer["kc"][0]
            full(j, l)
            act.activation(k_cT, psum[j.bank][:, 0:N_CMP], ACT.Copy).then_inc(bank_read[j.bank], 1)
            j = layer["vc"][0]
            full(j, l)
            act.activation(v_c, psum[j.bank][0:N_CMP, 0:P], ACT.Copy).then_inc(bank_read[j.bank], 1)
            act.wait_ge(fox_sum, l + 1)
            then(act.activation(lse_fox, lf_fox, ACT.Abs))
            then(act.activation(lse_fox, lse_fox, ACT.Exp, scale=-1.0))
            act.activation(lse_fox, lse_fox, ACT.Ln, bias=C("one")).then_inc(fox_lse, 1)
            j = layer["gla_la"][0]
            act.wait_ge(bank_read[j.bank], j.count(l))
            then(act.activation(flat(la_l), flat(la_m), ACT.Abs))
            then(act.activation(flat(la_l), flat(la_l), ACT.Exp, scale=-1.0))
            act.activation(flat(la_l), flat(la_l), ACT.Ln, bias=C("one")).then_inc(la_ready, 1)
            act.wait_ge(c_in, l + 1)
            act.activation(p_c, p_c, ACT.Exp).then_inc(c_exp, 1)
            for n, j in enumerate(layer["ct"]):
                full(j, l)
                act.activation(flat(pc_T[0:N_CMP, 2 * n:2 * n + 2, :]), psum[j.bank][0:N_CMP, :], ACT.Copy).then_inc(bank_read[j.bank], 1)

            def soft_exp(n, k):
                act.wait_ge(s_neg_ready, SOFTMAXES * l + k + 1)
                for i, cols in enumerate((slice(0, P), slice(P, 384))):
                    at = 2 * (k % NSA_N) + i
                    ins = act.activation(p_s[:, n, cols], p_s[:, n, cols], ACT.Exp, bias=s_neg[:, at:at + 1],
                                         accum_out=s_sum[:, at:at + 1])
                ins.then_inc(s_exp_ready, 1)

            for kind, n in nsa_steps():
                if kind == "fill":
                    fill(*n)
                elif kind == "score":
                    soft_exp(n % 8, n)
                elif kind == "turn":
                    copy(layer["nsa", kind, n][0], pT_s[:, n % 8, :], turn=l, cols=384)
            for kind, n in sb_steps():
                if kind == "fill":
                    fill(*n)
                    continue
                j = layer["sb", kind, n][0]
                if kind == "score":
                    full(j, l)
                    then(act.activation(p_s[:, n, :], psum[j.bank][:, 0:384], ACT.Abs))
                    then(act.activation(p_s[:, n, :], p_s[:, n, :], ACT.Exp, scale=-1.0))
                    act.activation(p_s[:, n, :], p_s[:, n, :], ACT.Ln, bias=C("one")).then_inc(sb_log, 1)
                elif kind == "again":
                    full(j, l)
                    act.activation(pT_s[:, n, :], psum[j.bank][:, 0:384], ACT.Exp).then_inc(bank_read[j.bank], 1)
            for kind, n in fox_steps():
                if kind == "fill":
                    fill(*n)
                elif kind == "score":
                    soft_exp(n, NSA_N + n)
                elif kind == "turn":
                    copy(layer["fox", kind, n][0], pT_s[:, n, :], turn=l, cols=384)
            for kind, n in gla_steps():
                if kind == "fill":
                    fill(*n)
                elif n < len(GLA_LEVELS):
                    act.wait_ge(decay_in, 8 * l + n + 1)
                    dk = decay[:, n % 2].rearrange("p a b -> p (a b)")
                    then(act.activation(dk, dk, ACT.Abs))
                    act.activation(dk, dk, ACT.Exp, scale=-1.0 / GLA_TAU).then_inc(decay_out, 1)
            for j in last_in_bank(layer["gla_g"] + layer["gates"]):
                act.wait_ge(bank_read[j.bank], j.count(l))
            act.activation(flat(sig_gg), flat(g_g), ACT.Sigmoid).then_inc(g_sig, 1)
            for i, j in enumerate(layer["gla_o"]):
                full(j, l)
                act.activation(square_g[:, i, :], psum[j.bank][:, :], ACT.Square).then_inc(squared, 1)
                copy(j, o_g[:, i, :], turn=l)
            for n in range(8):
                act.activation(flat(gates[:, 4 * n:4 * n + 4, :]), flat(gates[:, 4 * n:4 * n + 4, :]), ACT.Sigmoid).then_inc(gate_sig, 1)
                if n == 1:
                    for i, j in enumerate(layer["gla_t"]):
                        full(j, l)
                        act.activation(yT_all[:, 12:16, i * P:(i + 1) * P],
                                       psum[j.bank][:, :].rearrange("p (h t) -> p h t", h=4), ACT.Copy).then_inc(bank_read[j.bank], 1)
            for j in last_in_bank(layer["out"]):
                act.wait_ge(bank_read[j.bank], j.count(l))
            squares()
            for n, j in enumerate(layer["ff1"]):
                full(j, l)
                act.activation(flat(hid_ff[:, 2 * n:2 * n + 2, :]), psum[j.bank][:, :], ACT.Relu).then_inc(bank_read[j.bank], 1)
            steps.leave(LAYERS)
        act.wait_ge(x_ready, LAYERS + 1)
        squares()

    @block.gpsimd
    def _(pool):
        def rsqrt_x(value):
            pool.wait_ge(var_ready, value)
            pool.tensor_tensor(rstd, var, C("neghalf")[:, 0:TT], ALU.pow).then_inc(rstd_ready, 1)

        pool.wait_ge(const_loaded, 16)
        rsqrt_x(1)
        for n in range(2):
            pool.wait_ge(var8_ready, n + 1)
            pool.tensor_tensor(rstd8, var8, C("neghalf"), ALU.pow).then_inc(rstd8_ready, 1)
        rsqrt_x(2)
        rsqrt_x(3)
        with pool.Fori(0, LAYERS) as l:
            rsqrt_x(2 * l + 4)

            def scale(n, k):
                pool.wait_ge(s_inv_ready, SOFTMAXES * l + k + 1)
                for i, cols in enumerate((slice(0, P), slice(P, 384))):
                    at = 2 * (k % NSA_N) + i
                    part = p_s[:, n, cols]
                    ins = pool.tensor_tensor(part, part, s_inv[:, at:at + 1].to_broadcast([P, part.shape[-1]]), ALU.mult)
                ins.then_inc(p_scaled, 1)

            for n in range(NSA_N):
                scale(n % 8, n)
            for n in range(FOX_N):
                scale(n, NSA_N + n)
            pool.wait_ge(var8_ready, l + 3)
            pool.tensor_tensor(rstd8, var8, C("neghalf"), ALU.pow).then_inc(rstd8_ready, 1)
            rsqrt_x(2 * l + 5)
        rsqrt_x(2 * LAYERS + 4)

    @block.vector
    def _(dve):
        steps = Steps()

        def then(ins):
            ins.then_inc(dve_step, 1)
            dve.wait_ge(dve_step, steps.next())

        def full(j, turn=0):
            dve.wait_ge(bank_full[j.bank], j.count(turn))

        def norm_x(n):
            dve.wait_ge(sumsq_ready, n * 2)
            dve.tensor_scalar(var, sumsq, 1.0 / D, EPS, ALU.mult, ALU.add).then_inc(var_ready, 1)
            dve.wait_ge(rstd_ready, n)
            for i in range(TT):
                dve.tensor_scalar(xn[:, i, :], x[:, i, :], rstd[:, i:i + 1], None, ALU.mult).then_inc(xn_ready, 1)

        def gain_x(jobs, gain, turn=0):
            for n, j in enumerate(jobs):
                full(j, turn)
                for t in range(2):
                    dt = 2 * n + t
                    ins = dve.tensor_scalar(hT[:, dt, :], psum[j.bank][:, t * S:(t + 1) * S], gain[:, dt:dt + 1],
                                            None, ALU.mult)
                ins.then_inc(bank_read[j.bank], 1)

        def add_x(jobs, turn=0):
            for n, j in enumerate(jobs):
                half, i = divmod(n, 2)
                xs = x[:, i, half * 512:(half + 1) * 512]
                full(j, turn)
                dve.tensor_tensor(xs, psum[j.bank][:, :], xs, ALU.add).then_inc(bank_read[j.bank], 1)

        def by_head(v):
            return v.rearrange("p (n o) -> p n o", o=1).to_broadcast([P, 8, P])

        heads8 = lambda v: v.rearrange("p i (h e) -> p (i h) e", e=P)

        dve.wait_ge(x_loaded, 16)
        norm_x(1)
        dve.wait_ge(params_loaded, 64)
        gain_x(pre["ht"], at1["norm1"])
        dve.wait_ge(pos_loaded, 16)
        dve.wait_ge(const_loaded, 16)
        then(dve.tensor_copy(ang, pos_i))
        then(dve.tensor_scalar(ang, ang, C("inv"), None, ALU.mult))
        then(dve.tensor_scalar(turns, ang, 1.0 / TWO_PI, ROUND, ALU.mult, ALU.add))
        then(dve.tensor_scalar(turns, turns, -ROUND, None, ALU.add))
        for part in TWO_PI_PARTS:
            then(dve.scalar_tensor_tensor(ang, turns, -part, ang, ALU.mult, ALU.add))
        then(dve.tensor_scalar(sin_t, ang, PI_F, -PI_F, ALU.min, ALU.max))
        then(dve.tensor_scalar(ang, ang, 0.5 * np.pi, None, ALU.add))
        then(dve.tensor_scalar(turns, ang, PI_F, -TWO_PI, ALU.is_gt, ALU.mult))
        then(dve.tensor_tensor(ang, ang, turns, ALU.add))
        dve.tensor_scalar(cos_t, ang, PI_F, -PI_F, ALU.min, ALU.max).then_inc(angle_ready, 1)
        lam_mult = view(p_mem, 0, 2, DA_QD)
        then(dve.tensor_tensor(lam_mult, lam_in[:, 0::2, :], lam_in[:, 1::2, :], ALU.mult))
        dve.tensor_reduce(lam_two, lam_mult, AX.X, ALU.add).then_inc(lam_dots, 1)
        for j in pre["c"]:
            dve.wait_ge(bank_read[j.bank], j.count())
        for w in range(CONV_W - 1, -1, -1):
            back = CONV_W - 1 - w
            for f in range(4):
                if back == 0:
                    ins = dve.tensor_scalar(c_act[:, f, :], c_raw[:, f, :], conv_w[:, f, w:w + 1],
                                            at1["conv_b"][:, f:f + 1], ALU.mult, ALU.add)
                else:
                    ins = dve.scalar_tensor_tensor(c_act[:, f, back:], c_raw[:, f, 0:S - back], conv_w[:, f, w:w + 1],
                                                   c_act[:, f, back:], ALU.mult, ALU.add)
                if w:
                    if f == 3:
                        then(ins)
                else:
                    ins.then_inc(conv_ready, 1)
        dve.wait_ge(conv_sig, 1)
        for f in range(4):
            dve.tensor_tensor(c_act[:, f, :], c_act[:, f, :], c_raw[:, f, :], ALU.mult).then_inc(act_ready, 1)
        dve.wait_ge(act_ready, 4)
        for f in range(4):
            dve.tensor_scalar(skip_c[:, f, :], c_act[:, f, :], at1["m_skip"][:, f:f + 1], None, ALU.mult)
        j = pre["gate"][0]
        full(j)
        b_gate = at1["b_gate"].rearrange("p (o n) -> p o n", o=1).to_broadcast([P, TT, 8])
        dve.tensor_tensor(gate_pre, psum[j.bank][:, 0:16].rearrange("p (i n) -> p i n", i=2), b_gate,
                          ALU.add).then_inc(bank_read[j.bank], 1)
        dve.wait_ge(bank_read[j.bank], j.count())
        lf = log_f.rearrange("p (i n) -> p i n", i=2)
        dve.tensor_scalar(lf, gate_pre[:, :, 4:8], 0.0, None, ALU.min).then_inc(gates_pre, 1)
        dve.wait_ge(gates_pre, 1)
        dve.wait_ge(lse_ready, 1)
        dve.tensor_tensor(log_f, log_f, lse, ALU.subtract).then_inc(logf_ready, 1)
        dve.wait_ge(lam_exp, 1)
        dve.tensor_scalar(lam, lam_two[:, 0:1], lam_two[:, 1:2], LAM_INIT, ALU.subtract, ALU.add)
        dve.wait_ge(rel_loaded, 16)
        then(dve.tensor_tensor(rel_bias[:, :, P:S], rel_bias[:, :, P:S],
                               negmask[:, 0:P].rearrange("p (o n) -> p o n", o=1).to_broadcast([P, 4, P]), ALU.add))
        j = pre["negb"][0]
        full(j)
        dve.tensor_copy(neg_b, psum[j.bank][:, 0:8]).then_inc(bank_read[j.bank], 1)

        def m_weights(h):
            dve.wait_ge(m_exp_ready, h + 1)
            j = pre["qk"][h]
            full(j)
            for i, cols in enumerate((slice(0, P), slice(P, 384))):
                ins = dve.tensor_tensor_reduce(w_m[:, h, cols], w_m[:, h, cols], psum[j.bank][:, cols], ML_HD ** -0.5,
                                               0.0, ALU.mult, ALU.add, m_den[:, 4 * i + h:4 * i + h + 1])
            ins.then_inc(bank_read[j.bank], 1)

        for h in range(ML_HEADS):
            j = pre["u"][h]
            full(j)
            dve.tensor_tensor_reduce(w_m[:, h, 0:P], psum[j.bank][:, 0:P], negmask[:, 0:P], 1.0, -BIG,
                                     ALU.add, ALU.max, m_max[:, h:h + 1])
            dve.tensor_tensor_reduce(w_m[:, h, P:384], psum[j.bank][:, 0:S], negmask[:, P:384], 1.0, -BIG,
                                     ALU.add, ALU.max, m_max[:, 4 + h:5 + h]).then_inc(bank_read[j.bank], 1)
            dve.wait_ge(bank_read[j.bank], j.count())
            dve.tensor_scalar(m_neg[:, h::4], m_max[:, h::4], 0.0, -1.0, ALU.max, ALU.mult).then_inc(m_neg_ready, 1)
            if h:
                m_weights(h - 1)
        m_weights(ML_HEADS - 1)
        dve.wait_ge(m_neg_ready, ML_HEADS)
        j = pre["negb"][0]
        dve.wait_ge(bank_read[j.bank], j.count())
        dve.tensor_tensor(m_dec, m_neg, neg_b, ALU.add).then_inc(m_dec_in, 1)

        def d_scores(n):
            j = pre["s"][n]
            full(j)
            dve.tensor_tensor_reduce(p_d[:, n, 0:P], psum[j.bank][:, 0:P], rel_bias[:, n // 2, P:S], 1.0, -BIG,
                                     ALU.add, ALU.max, d_max[:, 2 * n:2 * n + 1])
            dve.tensor_tensor_reduce(p_d[:, n, P:384], psum[j.bank][:, P:384], rel_bias[:, n // 2, :], 1.0, -BIG,
                                     ALU.add, ALU.max, d_max[:, 2 * n + 1:2 * n + 2]).then_inc(bank_read[j.bank], 1)
            dve.wait_ge(bank_read[j.bank], j.count())
            dve.tensor_scalar(d_neg[:, 2 * n:2 * n + 2], d_max[:, 2 * n:2 * n + 2], -1.0, None,
                              ALU.mult).then_inc(d_neg_ready, 1)

        def d_mix(h):
            dve.wait_ge(d_exp_ready, 2 * h + 2)
            inv = d_inv[:, 4 * h:4 * h + 4]
            then(dve.reciprocal(inv, d_sum[:, 4 * h:4 * h + 4]))
            then(dve.tensor_scalar(inv[:, 2:4], inv[:, 2:4], lam, None, ALU.mult))
            halves = (slice(0, P), slice(P, 384))
            for i, cols in enumerate(halves):
                ins = dve.tensor_scalar(p_d[:, 2 * h + 1, cols], p_d[:, 2 * h + 1, cols], inv[:, 2 + i:3 + i], None, ALU.mult)
            then(ins)
            for i, cols in enumerate(halves):
                ins = dve.scalar_tensor_tensor(p_d[:, 2 * h, cols], p_d[:, 2 * h, cols], inv[:, i:i + 1],
                                               p_d[:, 2 * h + 1, cols], ALU.mult, ALU.subtract)
            ins.then_inc(a_ready, 1)

        for n in range(2 * DA_HEADS):
            d_scores(n)
            if n == 1:
                dve.wait_ge(m_dec_out, 1)
                then(dve.scalar_tensor_tensor(m_abs, m_den, -1.0, m_den, ALU.mult, ALU.max))
                then(dve.tensor_tensor(m_abs, m_abs, m_dec, ALU.max))
                then(dve.reciprocal(m_abs, m_abs))
            if n % 2 and n > 1:
                d_mix(n // 2 - 1)
        for i, j in enumerate(pre["num"]):
            full(j)
            inv = m_abs[:, 4 * i:4 * i + 4].rearrange("p (n o) -> p n o", o=1).to_broadcast([P, 4, P])
            dve.tensor_tensor(h_m[:, i, :].rearrange("p (h e) -> p h e", e=P),
                              psum[j.bank][:, :].rearrange("p (h e) -> p h e", e=P), inv, ALU.mult).then_inc(bank_read[j.bank], 1)
        for j in pre["num"]:
            dve.wait_ge(bank_read[j.bank], j.count())
        then(dve.tensor_reduce(mean, heads8(h_m), AX.X, ALU.add))
        then(dve.tensor_scalar(mean, mean, -1.0 / ML_HD, None, ALU.mult))
        dve.tensor_tensor(heads8(h_m), heads8(h_m), by_head(mean), ALU.add).then_inc(centred, 1)
        d_mix(DA_HEADS - 1)

        def head_rms(n, values, eps, signal):
            dve.wait_ge(squared, (1, 3)[n])
            then(dve.tensor_reduce(mean, heads8(square), AX.X, ALU.add))
            dve.tensor_scalar(var8, mean, 1.0 / P, eps, ALU.mult, ALU.add).then_inc(var8_ready, 1)
            dve.wait_ge(rstd8_ready, n + 1)
            dve.tensor_tensor(heads8(values), heads8(values), by_head(rstd8), ALU.mult).then_inc(signal, 1)

        head_rms(0, h_m, EPS, head_norm)
        for j in pre["pv"]:
            dve.wait_ge(bank_read[j.bank], j.count())
        head_rms(1, y_d, SUBLN_EPS, head_norm)
        for i, j in enumerate(pre["hnt"]):
            cols = slice(i * P, (i + 1) * P)
            full(j)
            for f in range(4):
                ins = dve.scalar_tensor_tensor(y_T[:, f, cols], psum[j.bank][:, f * P:(f + 1) * P],
                                               at1["m_norm"][:, f:f + 1], skip_c[:, f, cols], ALU.mult, ALU.add)
            ins.then_inc(bank_read[j.bank], 1)
            dve.wait_ge(bank_read[j.bank], j.count())
            dve.tensor_tensor(y_T[:, 0:4, cols], y_T[:, 0:4, cols], sig_z[:, :, cols], ALU.mult).then_inc(ym_ready, 1)
        for i, j in enumerate(pre["ydt"]):
            full(j)
            dve.tensor_scalar(y_T[:, 4:8, i * P:(i + 1) * P], psum[j.bank][:, :].rearrange("p (h t) -> p h t", h=4),
                              at1["da_norm"], 1.0 - LAM_INIT, ALU.mult, ALU.mult).then_inc(bank_read[j.bank], 1)
        add_x(pre["out"])
        norm_x(2)
        gain_x(pre["h2"], at1["norm2"])

        j = pre["router"][0]
        full(j)
        b_r = at1["b_r"].rearrange("p (o n) -> p o n", o=1).to_broadcast([P, TT, 36])
        dve.memset(group8, -BIG)
        dve.tensor_tensor(logits, psum[j.bank][:, 0:72].rearrange("p (i n) -> p i n", i=2), b_r,
                          ALU.add).then_inc(bank_read[j.bank], 1)
        dve.wait_ge(bank_read[j.bank], j.count())
        then(dve.tensor_copy(group8[:, :, 0:4], logits[:, :, 0:4]))
        iota8 = C("iota8")
        for i in range(TT):
            found = index8[:, 8 * i:8 * i + 8]
            then(dve.max(top8[:, i, :], group8[:, i, :]))
            dve.tensor_scalar(r_stat[:, 0, i:i + 1], top8[:, i, 0:1], -1.0, None, ALU.mult).then_inc(r_neg, 1)
            then(dve.max_index(found, top8[:, i, :], group8[:, i, :]))
            then(dve.tensor_copy(idx_f[:, i, 0:1], found[:, 0:1]))
            then(dve.tensor_scalar(one_g[:, i, :], iota8, idx_f[:, i, 0:1], None, ALU.is_equal))
            for g in range(N_GROUPS):
                le = logits[:, i, 4 + 8 * g:12 + 8 * g]
                if g == 0:
                    then(dve.tensor_scalar(le8[:, i, :], le, one_g[:, i, 0:1], None, ALU.mult))
                else:
                    then(dve.scalar_tensor_tensor(le8[:, i, :], le, one_g[:, i, g:g + 1], le8[:, i, :], ALU.mult, ALU.add))
            then(dve.max(top8[:, i, :], le8[:, i, :]))
            dve.tensor_tensor(r_stat[:, 2, i:i + 1], top8[:, i, 1:2], top8[:, i, 0:1], ALU.subtract).then_inc(top_diff, 1)
            then(dve.max_index(found, top8[:, i, :], le8[:, i, :]))
            then(dve.tensor_copy(idx_f[:, i, 0:2], found[:, 0:2]))
        for i in range(TT):
            dve.wait_ge(r_exp, i + 1)
            dve.wait_ge(top_exp, i + 1)
            then(dve.tensor_scalar(r_stat[:, 3, i:i + 1], r_stat[:, 2, i:i + 1], 1.0, r_stat[:, 1, i:i + 1], ALU.add, ALU.mult))
            then(dve.reciprocal(r_stat[:, 3, i:i + 1], r_stat[:, 3, i:i + 1]))
            then(dve.tensor_tensor(r_stat[:, 4, i:i + 1], r_stat[:, 3, i:i + 1], r_stat[:, 2, i:i + 1], ALU.mult))
            then(dve.tensor_scalar(pick1[:, i, :], iota8, idx_f[:, i, 1:2], r_stat[:, 4, i:i + 1], ALU.is_equal, ALU.mult))
            then(dve.tensor_scalar(pick0[:, i, :], iota8, idx_f[:, i, 0:1], r_stat[:, 3, i:i + 1], ALU.is_equal, ALU.mult))
            then(dve.tensor_tensor(pick0[:, i, :], pick0[:, i, :], pick1[:, i, :], ALU.add))
            for g in range(N_GROUPS):
                then(dve.tensor_scalar(gates_moe[:, i, 8 * g:8 * g + 8], pick0[:, i, :], one_g[:, i, g:g + 1], None, ALU.mult))
        with dve.Fori(0, MOE_TURNS) as turn:
            steps.enter(turn, 2 * UNROLL)
            for e in range(UNROLL):
                for half in range(2):
                    sg = sig_g[:, e % 2, half, :]
                    jg, ju = moe["g", e][half], moe["u", e][half]
                    dve.wait_ge(sig_ready, turn * (2 * UNROLL) + 2 * e + half + 1)
                    full(jg, turn)
                    dve.tensor_tensor(sg, psum[jg.bank][:, :], sg, ALU.mult).then_inc(bank_read[jg.bank], 1)
                    dve.wait_ge(bank_read[jg.bank], jg.count(turn))
                    full(ju, turn)
                    dve.tensor_tensor(hid[:, 2 * half:2 * half + 2, :].rearrange("p a b -> p (a b)"),
                                      psum[ju.bank][:, :], sg, ALU.mult).then_inc(bank_read[ju.bank], 1)
                for i in range(TT):
                    then(dve.tensor_copy(r_stat[:, 5, i:i + 1], gates_moe[:, i, bass.ds(turn * UNROLL + e, 1)]))
                for n, j in enumerate(moe["d", e]):
                    i, half = divmod(n, 2)
                    xs = x[:, i, half * 512:(half + 1) * 512]
                    full(j, turn)
                    dve.scalar_tensor_tensor(xs, psum[j.bank][:, :], r_stat[:, 5, i:i + 1], xs, ALU.mult,
                                             ALU.add).then_inc(bank_read[j.bank], 1)
            steps.leave(MOE_TURNS)
        norm_x(3)
        dve.wait_ge(xn_ready, 6)
        dve.wait_ge(gain_loaded, 16)
        for i in range(TT):
            ins = dve.tensor_tensor(x[:, i, :], xn[:, i, :], gain_row, ALU.mult)
        ins.then_inc(x_ready, 1)
        with dve.Fori(0, LAYERS) as l:
            steps.enter(l, DVE_STEPS)
            norm_x(2 * l + 4)
            dve.wait_ge(params2_loaded, 16 * l + 16)
            gain_x(layer["ht"], at2["norm_mix"], l)

            marks = iter(range(WAIT_MARKS))

            def apart():
                n = next(marks)
                dve.memset(wait_marks[:, n:n + 1], 0.0)

            def rotate(j, v, tmp, cos, sin):
                full(j, l)
                n = v.shape[-1]
                tiles = v.shape[1] if len(v.shape) == 3 else 1
                if tiles > 1:
                    cos, sin = (c.rearrange("p (o n) -> p o n", o=1).to_broadcast([P, tiles, n]) for c in (cos, sin))
                    swapped = psum[j.bank][:, 0:tiles * S].rearrange("p (a n) -> p a n", a=tiles)
                else:
                    swapped = psum[j.bank][:, 0:n]
                dve.tensor_tensor(tmp, swapped, sin, ALU.mult).then_inc(bank_read[j.bank], 1)
                then(dve.tensor_tensor(v, v, cos, ALU.mult))
                dve.wait_ge(bank_read[j.bank], j.count(l))
                dve.tensor_tensor(v, v, tmp, ALU.add).then_inc(roped, 1)

            for j in last_in_bank(layer["nsa_v"]):
                dve.wait_ge(bank_read[j.bank], j.count(l))
            lf2 = lf_fox.rearrange("p (i n) -> p i n", i=2)
            dve.tensor_tensor(lf2, fg[:, :, 0:8], at2["fox_b"].rearrange("p (o n) -> p o n", o=1).to_broadcast([P, TT, 8]),
                              ALU.add).then_inc(fox_sum, 1)
            for n, j in enumerate(layer["rope_q"]):
                rotate(j, q_n[:, 2 * n:2 * n + 2, :], rope_tmp[:, 2 * n:2 * n + 2, :], cos_t, sin_t)
            rotate(layer["rope_k"][0], k_sw, rope_tmp[:, 4:6, :], cos_t, sin_t)
            even = lambda v, w: v.rearrange("p (b s w) -> p b s w", s=CMP_STRIDE // 2, w=2)[:, :, :, w]
            for n, j in enumerate(layer["dup"]):
                full(j, l)
                for late in range(2):
                    for w in range(2):
                        rows = slice(HD * w, HD * w + HD)
                        pe_ = at2["pe_" + "kv"[n]][rows, 16 * late:16 * late + 16:2]
                        ins = dve.tensor_tensor(even(dup[rows, 2 * n + late, :], 0), even(psum[j.bank][rows, :], w),
                                                pe_.rearrange("p (o s) -> p o s", o=1).to_broadcast([HD, 32, 8]), ALU.add)
                        ins.then_inc(dup_ready, 1)
                dve.wait_ge(dup_ready, 8 * l + 4 * n + 4)
                dve.memset(mark, 0.0).then_inc(bank_read[j.bank], 1)
            for j in last_in_bank(layer["hid"]):
                dve.wait_ge(bank_read[j.bank], j.count(l))
            hx = hid_c.rearrange("p a b c -> p (a b c)")
            then(dve.tensor_tensor(gelu_tmp, hx, hx, ALU.mult))
            then(dve.tensor_scalar(gelu_tmp, gelu_tmp, 0.044715, 1.0, ALU.mult, ALU.add))
            dve.tensor_tensor(gelu_tmp, gelu_tmp, hx, ALU.mult).then_inc(gelu_in, 1)
            dve.wait_ge(gelu_sig, l + 1)
            dve.tensor_tensor(hx, hx, gelu_tmp, ALU.mult).then_inc(hid_ready, 1)
            j = layer["kc"][0]
            dve.wait_ge(bank_read[j.bank], j.count(l))
            ends = slice(CMP_LEN - 1, S, CMP_STRIDE)
            rotate(layer["rope_c"][0], k_cT, rope_tmp_c, cos_t[:, ends], sin_t[:, ends])
            j = layer["gla_la"][0]
            full(j, l)
            for t in range(2):
                ins = dve.tensor_scalar(la_m[:, t, :], psum[j.bank][:, t * S:(t + 1) * S], at2["b_alpha"][:, t:t + 1], None, ALU.add)
            ins.then_inc(bank_read[j.bank], 1)
            cmask = C("cmpmask").rearrange("p (i o c) -> p i o c", i=TT, o=1).to_broadcast([P, TT, NSA_HPG, N_CMP])
            for r, j in enumerate(layer["cs"]):
                full(j, l)
                got = psum[j.bank][:, 0:TT * NSA_HPG * N_CMP].rearrange("p (i m c) -> p i m c", i=TT, m=NSA_HPG)
                dve.tensor_tensor(p_c.rearrange("p i (m r) c -> p i m r c", r=2)[:, :, :, r, :], got, cmask,
                                  ALU.add).then_inc(bank_read[j.bank], 1)
            for j in last_in_bank(layer["cs"]):
                dve.wait_ge(bank_read[j.bank], j.count(l))
            pc16 = p_c.rearrange("p i h c -> p (i h) c")
            wide16 = lambda v: v.rearrange("p (n o) -> p n o", o=1).to_broadcast([P, 16, N_CMP])
            then(dve.tensor_reduce(c_max, pc16, AX.X, ALU.max))
            dve.tensor_tensor(pc16, pc16, wide16(c_max), ALU.subtract).then_inc(c_in, 1)
            dve.wait_ge(fox_lse, l + 1)
            then(dve.tensor_scalar(lf_fox, lf_fox, 0.0, None, ALU.min))
            dve.tensor_tensor(lf_fox, lf_fox, lse_fox, ALU.subtract).then_inc(lf_ready, 1)
            dve.wait_ge(la_ready, l + 1)
            then(dve.tensor_scalar(la_m, la_m, 0.0, None, ALU.min))
            for t in range(2):
                ins = dve.tensor_tensor_scan(b_cum[:, t, :], la_m[:, t, :], la_l[:, t, :], 0.0, ALU.add, ALU.subtract)
            then(ins)
            dve.wait_ge(c_exp, l + 1)
            then(dve.tensor_reduce(c_inv, pc16, AX.X, ALU.add))
            then(dve.reciprocal(c_inv, c_inv))
            c_inv3 = c_inv.rearrange("p (i h) -> p i h", i=TT)
            then(dve.tensor_tensor(c_inv3, c_inv3, C("rowvalid").rearrange("p (i o) -> p i o", o=1).to_broadcast([P, TT, HEADS]), ALU.mult))
            dve.wait_ge(nsa_gate_ready, l + 1)
            c_inv4 = c_inv.rearrange("p (i m r) -> p i m r", i=TT, r=2)
            then(dve.tensor_tensor(c_inv4, c_inv4, nsa_gate[:, :, :, :, 0], ALU.mult))
            dve.tensor_tensor(pc16, pc16, wide16(c_inv), ALU.mult).then_inc(c_ready, 1)

            def soft_max(j, n, k):
                full(j, l)
                apart()
                at = 2 * (k % NSA_N)
                dve.tensor_tensor_reduce(p_s[:, n, 0:P], psum[j.bank][:, 0:P], negmask[:, 0:P], 1.0, -BIG,
                                         ALU.add, ALU.max, s_max[:, at:at + 1])
                dve.tensor_tensor_reduce(p_s[:, n, P:384], psum[j.bank][:, P:384], negmask[:, P:384], 1.0, -BIG,
                                         ALU.add, ALU.max, s_max[:, at + 1:at + 2]).then_inc(bank_read[j.bank], 1)
                dve.wait_ge(bank_read[j.bank], j.count(l))
                dve.tensor_scalar(s_neg[:, at:at + 2], s_max[:, at:at + 2], -1.0, None, ALU.mult).then_inc(s_neg_ready, 1)

            def soft_inverse(k, gate=None):
                at = 2 * (k % NSA_N)
                dve.wait_ge(s_exp_ready, SOFTMAXES * l + k + 1)
                if gate is None:
                    dve.reciprocal(s_inv[:, at:at + 2], s_sum[:, at:at + 2]).then_inc(s_inv_ready, 1)
                else:
                    then(dve.reciprocal(s_inv[:, at:at + 2], s_sum[:, at:at + 2]))
                    dve.tensor_tensor(s_inv[:, at:at + 2], s_inv[:, at:at + 2], gate, ALU.mult).then_inc(s_inv_ready, 1)

            def value(j, tile):
                full(j, l)
                dve.tensor_copy(yT_all[:, tile, :], psum[j.bank][:, 0:S]).then_inc(bank_read[j.bank], 1)

            gate_of = lambda n: nsa_gate[:, :, n // 4, n // 2 % 2, 1 + n % 2]
            for kind, n in nsa_steps():
                if kind == "score":
                    soft_max(layer["nsa", kind, n][0], n % 8, n)
                    if n:
                        soft_inverse(n - 1, gate_of(n - 1))
                elif kind == "turn" and n == NSA_N - NSA_LAG:
                    soft_inverse(NSA_N - 1, gate_of(NSA_N - 1))
                elif kind == "value":
                    value(layer["nsa", kind, n][0], n)
            for kind, n in sb_steps():
                if kind == "score":
                    j = layer["sb", kind, n][0]
                    dve.wait_ge(sb_log, 8 * l + n + 1)
                    dve.scalar_tensor_tensor(p_s[:, n, :], psum[j.bank][:, 0:384], 0.0, p_s[:, n, :], ALU.max,
                                             ALU.add).then_inc(bank_read[j.bank], 1)
                    dve.wait_ge(bank_read[j.bank], j.count(l))
                    diag = p_s[:, n, :].rearrange("p (b c) -> p b c", b=3)[:, 0::2, :]
                    dve.tensor_tensor(diag, diag, C("strict").rearrange("p (o n) -> p o n", o=1).to_broadcast([P, 2, P]),
                                      ALU.mult).then_inc(sb_ready, 1)
                elif kind == "value":
                    value(layer["sb", kind, n][0], 4 + n)
            for kind, n in fox_steps():
                if kind == "score":
                    soft_max(layer["fox", kind, n][0], n, NSA_N + n)
                    if n:
                        soft_inverse(NSA_N + n - 1)
                elif kind == "turn" and n == FOX_N - FOX_LAG:
                    soft_inverse(NSA_N + FOX_N - 1)
                elif kind == "value":
                    value(layer["fox", kind, n][0], 8 + n)
            for j in last_in_bank(layer["gla_qk"]):
                dve.wait_ge(bank_read[j.bank], j.count(l))
            then(dve.memset(att, 0.0))

            def level_decay(n):
                h = GLA_LEVELS[n]
                blocks = lambda v: v.rearrange("p a (b s) -> p (a b) s", s=2 * h)
                b = blocks(b_cum)
                if n >= 2:
                    dve.wait_ge(level_ready, 8 * l + n - 1)
                dve.tensor_tensor(blocks(decay[:, n % 2]), b, b[:, :, h - 1:h].to_broadcast([P, S // h, 2 * h]),
                                  ALU.subtract).then_inc(decay_in, 1)

            def level_read(n):
                for r, j in enumerate(layer["gla", "level", n]):
                    full(j, l)
                    got = psum[j.bank][:, :].rearrange("p (h t) -> p h t", h=4)
                    if n == 0:
                        ins = dve.tensor_copy(att_far[:, r], got[:, 0:2, :])
                    else:
                        before = layer["gla", "level", n - 1][r]
                        dve.wait_ge(bank_read[before.bank], before.count(l))
                        apart()
                        mask = C("gla")[:, (n - 1) * P:n * P] if n < len(GLA_LEVELS) else ident
                        mask = mask.bitcast(U32).rearrange("p (o t) -> p o t", o=1).to_broadcast([P, 4, P])
                        ins = dve.copy_predicated(att[:, r], mask, got)
                    ins.then_inc(bank_read[j.bank], 1)

            level_decay(0)
            for n in range(len(GLA_LEVELS)):
                if n + 1 < len(GLA_LEVELS):
                    level_decay(n + 1)
                dve.wait_ge(decay_out, 8 * l + n + 1)
                dve.tensor_tensor(q_lv[:, n % 2], q_g, decay[:, n % 2], ALU.mult)
                dve.tensor_tensor(k_lv[:, n % 2], k_g, decay[:, n % 2], ALU.mult).then_inc(level_ready, 1)
                if n:
                    level_read(n - 1)
            for n in range(len(GLA_LEVELS) - 1, len(GLA_LEVELS) + 1):
                level_read(n)
            dve.wait_ge(g_sig, l + 1)
            then(dve.tensor_tensor(sig_gg, sig_gg, g_g, ALU.mult))
            then(dve.tensor_tensor(heads8(sig_gg), heads8(sig_gg),
                                   at2["gla_norm"].rearrange("p (o e) -> p o e", o=1).to_broadcast([P, 8, P]), ALU.mult))
            dve.wait_ge(squared, 2 * l + 5)
            then(dve.tensor_reduce(mean, heads8(square_g), AX.X, ALU.add))
            dve.tensor_scalar(var8, mean, 1.0 / GLA_DV, EPS, ALU.mult, ALU.add).then_inc(var8_ready, 1)
            for j in last_in_bank(layer["gla_o"]):
                dve.wait_ge(bank_read[j.bank], j.count(l))
            dve.wait_ge(rstd8_ready, l + 3)
            then(dve.tensor_tensor(heads8(o_g), heads8(o_g), by_head(rstd8), ALU.mult))
            dve.tensor_tensor(o_g, o_g, sig_gg, ALU.mult).then_inc(y_gla, 1)
            for n, j in enumerate(layer["branch"]):
                br, k = divmod(n, 4)
                dve.wait_ge(gate_sig, 8 * l + n // 2 + 1)
                full(j, l)
                got = psum[j.bank][:, :].rearrange("p (a t) -> p a t", a=2)
                g, m = gates[:, 2 * n:2 * n + 2, :], mixed[:, 2 * k:2 * k + 2, :]
                dve.tensor_tensor(m if br == 0 else g, got, g, ALU.mult).then_inc(bank_read[j.bank], 1)
                if br:
                    dve.wait_ge(bank_read[j.bank], j.count(l))
                    ins = dve.tensor_tensor(m, m, g, ALU.add)
                    if br == N_BRANCH - 1:
                        ins.then_inc(mixed_ready, 1)
                    elif k == 3:
                        then(ins)
            add_x(layer["out"], l)
            norm_x(2 * l + 5)
            gain_x(layer["h2"], at2["norm_ff"], l)
            for n, j in enumerate(layer["ff1"]):
                dve.wait_ge(bank_read[j.bank], j.count(l))
                hf = hid_ff[:, 2 * n:2 * n + 2, :]
                dve.tensor_tensor(hf, hf, hf, ALU.mult).then_inc(ffh_ready, 1)
            add_x(layer["ff2"], l)
            for j in last_in_bank(layer["ff2"]):
                dve.wait_ge(bank_read[j.bank], j.count(l))
            dve.memset(mark, 0.0).then_inc(x_ready, 1)
            steps.leave(LAYERS)
        norm_x(2 * LAYERS + 4)
        dve.wait_ge(xn_ready, 2 * (2 * LAYERS + 4))
        dve.wait_ge(gain_loaded, 32)
        for i in range(TT):
            ins = dve.tensor_tensor(x[:, i, :], xn[:, i, :], gain_row, ALU.mult)
        ins.then_inc(x_ready, 1)

    block.__exit__(None, None, None)


def k_tiles(w):
    k, n = w.shape[0] // P, w.shape[1]
    return np.ascontiguousarray(w.reshape(k, P, n).transpose(1, 0, 2)).reshape(P, k * n)


def column(v):
    return v.reshape(-1, P).T


def wide(v):
    return np.broadcast_to(v.reshape(1, -1), (P, v.size))


def fill_chunk(out, w):
    out[:, 0:w.shape[1]] = w


def layout(a):
    f = np.float32
    w1 = np.zeros((PRE_CHUNKS + N_EXPERTS * EXPERT_CHUNKS, P, CHUNK_COLS), f)
    for c in range(6):
        fill_chunk(w1[c], k_tiles(a["w_in"][0][:, 512 * c:512 * c + 512]))
    for c in range(2):
        fill_chunk(w1[6 + c], k_tiles(a["w_out"][0][:, 512 * c:512 * c + 512]))
    for e in range(N_EXPERTS):
        for n, name in enumerate(("w_eg", "w_eu", "w_ed")):
            fill_chunk(w1[PRE_CHUNKS + EXPERT_CHUNKS * e + n], k_tiles(a[name][0, e]))
    prm1 = np.zeros((P, PRM1_COLS), f)

    def put1(name, v):
        prm1[:v.shape[0], PRM1[name]] = v

    put1("norm1", column(a["norm1_g"][0]))
    put1("norm2", column(a["norm2_g"][0]))
    put1("conv_w", a["conv_w"][0].reshape(CONV_W, 4, P).transpose(2, 1, 0).reshape(P, 16))
    put1("conv_b", column(a["conv_b"][0]))
    put1("m_norm", column(a["m_norm_g"][0]))
    put1("m_skip", column(a["m_skip"][0]))
    put1("da_norm", column(a["da_norm_g"][0]))
    put1("b_gate", wide(a["b_mgate"][0]))
    put1("lam", wide(a["lambda_qk"][0]))
    put1("w_q", a["w_mq"][0].transpose(1, 0, 2).reshape(P, 512))
    put1("w_k", a["w_mk"][0].transpose(1, 0, 2).reshape(P, 512))
    put1("w_gate", k_tiles(a["w_mgate"][0]))
    w_r = np.concatenate([a["w_rg"][0], a["w_re"][0].reshape(D, N_EXPERTS)], 1)
    put1("w_r", k_tiles(w_r))
    put1("b_r", wide(np.concatenate([a["b_rg"][0], a["b_re"][0].reshape(-1)])))
    put1("rel", a["rel_bias"])
    gain = np.stack([wide(a["normf_g"]), wide(a["norm_final_2"])])

    w2 = np.zeros((LAYERS * LAYER_CHUNKS, P, CHUNK_COLS), f)
    prm2 = np.zeros((LAYERS, P, PRM2_COLS), f)
    head_pairs = [h for m in range(NSA_HPG) for h in (m, NSA_HPG + m)]
    pair_cols = np.concatenate([np.arange(h * HD, h * HD + HD) for h in head_pairs])
    gate_cols = np.concatenate([np.arange(n * D, n * D + D) for n in BRANCH_ORDER])
    for l in range(LAYERS):
        w = a["w_in_2"][l]
        at, o = {}, 0
        for name, n in (("q", 512), ("kc", 128), ("vc", 128), ("ks", 128), ("vs", 128), ("kw", 128), ("vw", 128),
                        ("g", 24), ("sbq", 512), ("sbk", 512), ("sbv", 512), ("gq", 256), ("gk", 256), ("gv", 512),
                        ("ga", 16), ("gg", 512), ("fq", 512), ("fk", 512), ("fv", 512), ("ff", 8), ("gates", 4096)):
            at[name] = w[:, o:o + n]
            o += n
        cat = lambda *names: np.concatenate([at[n] for n in names], 1)
        narrow = np.zeros((D, 512), f)
        v_cols = cat("vs", "vw", "ff", "g", "ga")
        narrow[:, 0:v_cols.shape[1]] = v_cols
        seq = [at["q"][:, pair_cols], cat("kc", "vc", "ks", "kw"), narrow]
        seq = [k_tiles(v) for v in seq]
        seq += [k_tiles(a[n][l]) for n in ("nsa_cmp_wk1_2", "nsa_cmp_wv1_2")]
        gates = at["gates"][:, gate_cols]
        gate_chunk = lambda n: k_tiles(gates[:, 512 * n:512 * n + 512])
        seq += [k_tiles(at[n]) for n in ("sbq", "sbk", "sbv")] + [gate_chunk(0)]
        seq += [k_tiles(at[n]) for n in ("fq", "fk", "fv")] + [gate_chunk(1)]
        seq += [k_tiles(cat("gq", "gk")), k_tiles(at["gv"]), k_tiles(at["gg"])] + [gate_chunk(n) for n in range(2, 8)]
        for n in range(N_BRANCH):
            wb = a["w_branch_2"][l, BRANCH_ORDER[n]]
            seq.append(k_tiles(wb[pair_cols] if n == 0 else wb))
        seq += [k_tiles(a["w_out_2"][l][:, 512 * c:512 * c + 512]) for c in range(2)]
        seq += [k_tiles(a["w_ff1_2"][l][:, 512 * c:512 * c + 512]) for c in range(8)]
        seq += [k_tiles(a["w_ff2_2"][l][512 * c:512 * c + 512]) for c in range(8)]
        assert len(seq) == LAYER_CHUNKS
        for c, v in enumerate(seq):
            fill_chunk(w2[l * LAYER_CHUNKS + c], v)

        def put2(name, v):
            prm2[l, :v.shape[0], PRM2[name]] = v

        put2("norm_mix", column(a["norm_mix_2"][l]))
        put2("norm_ff", column(a["norm_ff_2"][l]))
        put2("b_gate", column(a["b_gate_2"][l][gate_cols]))
        for name in ("k", "v"):
            pe = a[f"nsa_cmp_pos_{name}_2"][l]
            put2(f"pe_{name}", np.concatenate([np.repeat(pe[0::2].T, 2, 1), np.repeat(pe[1::2].T, 2, 1)], 0))
            put2(f"w_{name}2", k_tiles(a[f"nsa_cmp_w{name}2_2"][l]))
        put2("w_alpha", a["gla_w_alpha_2"][l])
        put2("b_alpha", column(a["gla_b_alpha_2"][l]))
        put2("gla_norm", wide(a["gla_norm_2"][l]))
        put2("fox_b", wide(a["fox_b_f_2"][l]))
    x = np.ascontiguousarray(a["x"][0].reshape(TT, P, D).transpose(1, 0, 2))
    pos = np.ascontiguousarray(np.broadcast_to(a["positions_2"].reshape(1, S), (P, S)))
    return {"x": x, "const": constants(), "prm1": prm1, "gain": gain, "w1": w1, "prm2": prm2, "w2": w2, "pos": pos}


def kernel(**inputs):
    import concourse.bacc as bacc
    from concourse.bass_utils import run_bass_kernel_spmd as run

    arrays = layout({n: np.asarray(v) for n, v in inputs.items()})
    nc = bacc.Bacc("TRN2", target_bir_lowering=False, num_devices=1)
    d = {n: nc.dram_tensor(f"in_{n}", a.shape, mybir.dt.from_np(a.dtype), kind="ExternalInput").ap()
         for n, a in arrays.items()}
    d["skew"] = nc.dram_tensor("rel_skew", (4 * P * 384,), F32, kind="Internal").ap()
    d["out"] = nc.dram_tensor("out_x", (P, TT, D), F32, kind="ExternalOutput").ap()
    program(nc, d)
    r = run(nc, [{f"in_{n}": a for n, a in arrays.items()}], core_ids=[0])
    out = np.asarray(r.results[0]["out_x"])
    return np.ascontiguousarray(out.transpose(1, 0, 2)).reshape(1, S, D)
```

```python
import numpy as np
import concourse.bass as bass
from concourse import mybir

F32 = mybir.dt.float32
F32R = mybir.dt.float32r
I32 = mybir.dt.int32
U32 = mybir.dt.uint32
ALU = mybir.AluOpType
ACT = mybir.ActivationFunctionType
AX = mybir.AxisListType

P = 128
S = 256
TT = S // P
D = 1024
KT = D // P
CHUNK_COLS = 4096
BANKS = 8
SLOTS = 4
BIG = 1.0e30

ML_HEADS, ML_HD = 4, 128
DA_HEADS, DA_QD, DA_VD = 4, 64, 128
CONV_W = 4
N_GROUPS, EXP_PER_GROUP = 4, 8
N_EXPERTS = N_GROUPS * EXP_PER_GROUP
D_FF_EXP = 512
REL_BUCKETS, REL_MAX_DIST = 32, 128
LAM_INIT = 0.8 - 0.6 * float(np.exp(-0.3 * 0))
EPS, SUBLN_EPS = 1e-6, 1e-5
LAYERS = 2
HEADS, HD = 8, 64
NSA_GROUPS, NSA_HPG = 2, 4
CMP_LEN, CMP_STRIDE, CMP_HIDDEN = 32, 16, 256
N_CMP = (S - CMP_LEN) // CMP_STRIDE + 1
ROT_HALF = HD // 8
ROPE_THETA = 500000.0
GLA_HEADS, GLA_DK, GLA_DV, GLA_RANK, GLA_TAU = 4, 64, 128, 16, 16.0
N_BRANCH = 4
BRANCH_ORDER = [0, 1, 3, 2]
GLA_LEVELS = [128, 64, 32, 16, 8, 4, 2, 1]

TWO_PI, PI_F = 2.0 * np.pi, float(np.nextafter(np.float32(np.pi), np.float32(0)))
ROUND = 1.5 * 2.0 ** 23
TWO_PI_PARTS = (6.28125, 0.0019340515136718750, TWO_PI - 6.28125 - 0.0019340515136718750)
ACT_STEPS, DVE_STEPS = 28, 77
WAIT_MARKS = 40
FF2_SIGNALS = 7

PRE_CHUNKS = 8
PAIR_CHUNKS = 6
PAIRS = 2
MOE_TURNS = N_EXPERTS // (2 * PAIRS)
CAP = P // 2
PASSES = S // CAP
FAR = 4096.0
LAYER_CHUNKS = 44
RING = 3
LAYER_SLOTS = LAYER_CHUNKS + 1
SPLIT_CHUNKS = [0, 1, 2] + list(range(5, LAYER_CHUNKS))
LATE = 2 * SPLIT_CHUNKS.index(22)
HALVES = 2 * len(SPLIT_CHUNKS)
HALF = CHUNK_COLS // 2
AHEAD = 3
W_IN_CHUNKS = {"nsa_q": 0, "nsa_k": 1, "nsa_v": 2, "cmp": 3, "sb_q": 5, "sb_k": 6, "sb_v": 7}


def columns(*fields):
    at, out = 0, {}
    for name, width in fields:
        out[name] = slice(at, at + width)
        at += width
    return out, at


CONST, CONST_COLS = columns(
    ("ident", 128), ("negmask", 384), ("strict", 128), ("sufneg", 128), ("negstrict", 128),
    ("negtriu", 256), ("gla", 7 * 128), ("rope", 128), ("dup", 256), ("inv", 1), ("cmpmask", 2 * N_CMP),
    ("rowvalid", 2), ("iota", CAP), ("neghalf", 8), ("ones8", 8), ("one", 1), ("bucket", 384))
PRM1, PRM1_COLS = columns(
    ("norm1", 8), ("norm2", 8), ("conv_w", 16), ("conv_b", 4), ("m_norm", 4), ("m_skip", 4), ("da_norm", 1),
    ("b_gate", 8), ("lam", 256), ("w_q", 512), ("w_k", 512), ("w_gate", 96), ("w_r", 288), ("b_r", 36),
    ("rel", 4))
PRM2, PRM2_COLS = columns(
    ("norm_mix", 8), ("norm_ff", 8), ("b_gate", 32), ("pe_k", 32), ("pe_v", 32), ("w_k2", 128), ("w_v2", 128),
    ("w_alpha", 256), ("b_alpha", 2), ("gla_norm", 128), ("fox_b", 8))


def constants():
    c = np.zeros((P, CONST_COLS), np.float32)
    r = np.arange(P)
    row, col = r[:, None], r[None, :]
    c[:, CONST["ident"]] = row == col
    neg = np.where(col > row, -BIG, 0.0)
    c[:, CONST["negmask"]] = np.concatenate([neg, 0 * neg, neg], 1)
    c[:, CONST["strict"]] = row < col
    c[:, CONST["sufneg"]] = -(row >= col).astype(np.float32)
    c[:, CONST["negstrict"]] = np.where(row >= col, -BIG, 0.0)
    c[:, CONST["negtriu"]] = np.concatenate([-(row <= col).astype(np.float32), -np.ones((P, P))], 1)
    levels = []
    for h in GLA_LEVELS[1:]:
        levels.append((row // (2 * h) == col // (2 * h)) & (row % (2 * h) < h) & (col % (2 * h) >= h))
    c[:, CONST["gla"]] = np.concatenate(levels, 1)
    rot = np.zeros((P, P), np.float32)
    inv = np.zeros(P, np.float32)
    freq = (np.float32(ROPE_THETA) ** (-np.arange(0, 2 * ROT_HALF, 2, dtype=np.float32)
                                       / np.float32(2 * ROT_HALF))).astype(np.float32)
    for base in (0, HD):
        for d in range(ROT_HALF):
            rot[base + ROT_HALF + d, base + d] = -1.0
            rot[base + d, base + ROT_HALF + d] = 1.0
            inv[base + d] = inv[base + ROT_HALF + d] = freq[d]
    c[:, CONST["rope"]] = rot
    c[:, CONST["inv"]] = inv[:, None]
    c[:, CONST["dup"]] = np.concatenate([row == g * HD + col % HD for g in range(NSA_GROUPS)], 1)
    ends = np.arange(N_CMP) * CMP_STRIDE + CMP_LEN - 1
    tok = np.arange(S).reshape(TT, P).T
    c[:, CONST["cmpmask"]] = np.where(ends[None, None] <= tok[:, :, None], 0.0, -BIG).reshape(P, -1)
    c[:, CONST["rowvalid"]] = tok >= ends[0]
    c[:, CONST["iota"]] = np.arange(CAP)[None]
    c[:, CONST["neghalf"]] = -0.5
    c[:, CONST["ones8"]] = 1.0
    c[:, CONST["one"]] = 1.0
    n = np.maximum(255 - np.arange(384), 0)
    exact = REL_BUCKETS // 2
    large = exact + (np.log(np.maximum(n, 1).astype(np.float32) / np.float32(exact))
                     / np.float32(np.log(REL_MAX_DIST / exact)) * np.float32(REL_BUCKETS - exact)).astype(np.int32)
    bucket = np.where(n < exact, n, np.minimum(large, REL_BUCKETS - 1))
    c[:REL_BUCKETS, CONST["bucket"]] = np.arange(REL_BUCKETS)[:, None] == bucket[None]
    return c


class Job:

    def __init__(self, region, bank, use):
        self.region, self.bank, self.use = region, bank, use

    def count(self, turn=0):
        r = self.region
        return turn * r.uses[self.bank] + (r.base[self.bank] + self.use + 1)


class Region:

    def __init__(self, base, first_bank, turns=1):
        self.base, self.turns = list(base), turns
        self.uses = [0] * BANKS
        self.next = first_bank
        self.jobs = {}

    def add(self, name, count=1):
        for _ in range(count):
            b = self.next % BANKS
            self.next += 1
            self.jobs.setdefault(name, []).append(Job(self, b, self.uses[b]))
            self.uses[b] += 1

    def after(self):
        return [b + self.turns * u for b, u in zip(self.base, self.uses)]

    def __getitem__(self, name):
        return self.jobs[name]


def last_in_bank(jobs, but=None):
    last = {}
    for j in jobs:
        if but is None or j.bank != but.bank:
            if j.bank not in last or last[j.bank].use < j.use:
                last[j.bank] = j
    return list(last.values())


class Steps:

    def __init__(self):
        self.base, self.n, self.turn, self.per = 0, 0, 0, 0

    def next(self):
        self.n += 1
        return self.turn * self.per + (self.base + self.n)

    def enter(self, turn, per):
        self.base, self.n, self.turn, self.per = self.base + self.n, 0, turn, per

    def leave(self, turns):
        assert self.n == self.per, (self.n, self.per)
        self.base, self.n, self.turn = self.base + turns * self.per, 0, 0


def plan_pre():
    r = Region([0] * BANKS, 0)
    for name, count in (("ht", 4), ("c", 2), ("vm", 2), ("z", 2), ("rel", 4), ("mq", 2), ("mk", 2), ("vmt", 2),
                        ("gate", 1), ("qd", 2), ("kd", 2), ("vd", 2), ("negb", 1)):
        r.add(name, count)
    for h in range(ML_HEADS):
        r.add("u")
        r.add("qk")
    for n in range(2 * DA_HEADS):
        r.add("s")
        if n % 2:
            r.add("wt")
    for name, count in (("num", 2), ("at", 4), ("pv", 2), ("hnt", 2), ("ydt", 2), ("out", 4), ("h2", 4),
                        ("router", 1), ("rank", 1)):
        r.add(name, count)
    return r


MOE_STEPS = [("pick", 0), ("turn", 0), ("gate", 0), ("up", 0), ("pick", 1), ("flip", 0), ("turn", 1), ("down", 0),
             ("gate", 1), ("up", 1), ("spread", 0), ("flip", 1), ("down", 1), ("spread", 1)]
MOE_JOBS = {"pick": 2, "down": 2, "spread": 4}


def plan_moe(base, first_bank, turns):
    r = Region(base, first_bank, turns)
    for step in MOE_STEPS:
        r.add(step, MOE_JOBS.get(step[0], 1))
    return r


NSA_FILL = [(n, j) for n in ("sb_q", "sb_k", "sb_v") for j in range(2)] + [("gates", j) for j in range(2)]
SB_FILL = [(n, j) for n in ("fox_q", "fox_k", "fox_v") for j in range(2)] + [("gates", j) for j in range(2, 4)]
FOX_FILL = [(n, j) for n in ("gla_qk", "gla_v", "gla_g") for j in range(2)] + [("gates", j) for j in range(4, 6)]
GLA_FILL = [("gates", j) for j in range(6, 16)]
NSA_N, NSA_LAG = 16, 3
SB_N, SB_LAG = 8, 3
FOX_N, FOX_LAG = 8, 3


def nsa_steps():
    out, fill = [], list(NSA_FILL)
    for n in range(NSA_N + NSA_LAG + 2):
        if n < NSA_N:
            out.append(("score", n))
        if 0 <= n - NSA_LAG < NSA_N:
            out.append(("turn", n - NSA_LAG))
        if n % 2 == 1 and fill:
            out.append(("fill", fill.pop(0)))
        k = n - NSA_LAG - 1
        if k >= 0 and k % 4 == 3:
            out.append(("value", k // 4))
    return out + [("fill", f) for f in fill]


def sb_steps():
    out, fill = [], list(SB_FILL)
    for n in range(SB_N + SB_LAG + 2):
        if n < SB_N:
            out.append(("score", n))
        if fill:
            out.append(("fill", fill.pop(0)))
        if 0 <= n - SB_LAG < SB_N:
            out.append(("again", n - SB_LAG))
        k = n - SB_LAG - 1
        if k >= 0 and k % 2 == 1:
            out.append(("value", k // 2))
    return out + [("fill", f) for f in fill]


def fox_steps():
    out, fill = [], list(FOX_FILL)
    for n in range(FOX_N + FOX_LAG + 2):
        if n < FOX_N:
            out.append(("score", n))
        if fill:
            out.append(("fill", fill.pop(0)))
        if 0 <= n - FOX_LAG < FOX_N:
            out.append(("turn", n - FOX_LAG))
        k = n - FOX_LAG - 1
        if k >= 0 and k % 2 == 1:
            out.append(("value", k // 2))
    return out + [("fill", f) for f in fill]


def gla_steps():
    out, fill = [], list(GLA_FILL)
    for n in range(len(GLA_LEVELS) + 1):
        out.append(("level", n))
        if fill:
            out.append(("fill", fill.pop(0)))
    return out + [("fill", f) for f in fill]


def plan_layer(moe):
    r = Region(moe.after(), moe.next, LAYERS)
    for name, count in (("ht", 4), ("nsa_q", 2), ("nsa_k", 2), ("nsa_v", 1), ("nsa_f", 1), ("gla_a", 1), ("rope_q", 2),
                        ("rope_k", 1), ("dup", 2), ("hid", 2), ("kc", 1), ("vc", 1), ("rope_c", 1), ("gla_la", 1),
                        ("cs", 2), ("ct", 4)):
        r.add(name, count)
    for mixer, steps in (("nsa", nsa_steps()), ("sb", sb_steps()), ("fox", fox_steps()), ("gla", gla_steps())):
        for kind, n in steps:
            if kind == "fill":
                r.add(n[0])
            elif kind == "level":
                r.add((mixer, kind, n), 2)
            else:
                r.add((mixer, kind, n))
    for name, count in (("gla_o", 2), ("gla_t", 2), ("branch", 16), ("out", 4), ("h2", 4), ("ff1", 16), ("ff2", 4)):
        r.add(name, count)
    return r


def program(nc, d):
    start = {}

    def sb(name, cols, dt=F32):
        start[name] = -(-nc.sbuf_base // 32) * 32
        return nc.alloc_sbuf_tensor(name, [P, cols], dt)

    def parts(name, of, first, cols):
        return nc.alloc_sbuf_tensor_at(name, [P, cols], F32R, offset=start[of] + 4 * first)

    sem = lambda name: nc.alloc_semaphore(name)

    cst = sb("cst", CONST["bucket"].start)
    prm1, prm2 = sb("prm1", PRM1_COLS - 1024), sb("prm2", PRM2_COLS)
    wring = sb("wring", SLOTS * CHUNK_COLS)
    x_mem, xn_mem, ht_mem = sb("x_mem", TT * D), sb("xn_mem", TT * D), sb("ht_mem", KT * S)
    gates_mem = sb("gates_mem", 8 * 1024)
    work_mem = sb("work_mem", 16384)
    qkv_a, qkv_b, p_mem, pt_mem = (work_mem[:, 3072 * n:3072 * (n + 1)] for n in range(4))
    yt_mem = work_mem[:, 12288:]
    rope_mem = sb("rope_mem", 512)
    small = sb("small", 480)
    index8 = sb("index8", 32, U32)
    psum = [nc.alloc_psum_tensor(f"bank{b}", [P, 512], F32) for b in range(BANKS)]

    def view(mem, first, *shape):
        n = int(np.prod(shape))
        v = mem[:, first:first + n]
        if len(shape) == 1:
            return v
        names = "abcd"[:len(shape)]
        return v.rearrange(f"p ({' '.join(names)}) -> p {' '.join(names)}", **dict(zip(names, shape)))

    def C(name):
        return cst[:, CONST[name]]

    at_small = [0]

    def stat(n):
        at_small[0] += n
        return small[:, at_small[0] - n:at_small[0]]

    x, xn, hT = view(x_mem, 0, TT, D), view(xn_mem, 0, TT, D), view(ht_mem, 0, KT, S)
    ident, negmask, negtriu = C("ident"), C("negmask"), C("negtriu")
    sumsq, var, rstd = stat(2), stat(2), stat(2)

    c_raw, c_act, v_m = view(gates_mem, 0, 4, S), view(gates_mem, 1024, 4, S), view(gates_mem, 2048, TT, 512)
    v_mT, sig_z, m_q = (view(gates_mem, 1024 * n, 4, S) for n in (3, 4, 5))
    m_k, skip_c = view(gates_mem, 6144, 4, S), view(gates_mem, 7168, 4, S)
    q_d, k_d, v_d = view(qkv_a, 0, 4, S), view(qkv_a, 1024, 4, S), view(qkv_a, 2048, TT, 512)
    w_m, w_mT = view(qkv_b, 0, 4, 384), view(qkv_b, 1536, 4, 384)
    p_d, a_T, rel_row = view(p_mem, 0, 8, 384), view(pt_mem, 0, 4, 384), view(pt_mem, 0, 4, 384)
    square, bucket = view(pt_mem, 1536, TT, 512), pt_mem[0:REL_BUCKETS, 2560:2560 + 384]
    y_T, rel_bias = view(yt_mem, 0, 8, S), view(yt_mem, 2048, 4, S)
    w_mq, w_mk = view(yt_mem, 3072, 4, P), view(yt_mem, 3584, 4, P)
    h_m, y_d = view(xn_mem, 0, TT, 512), view(xn_mem, 1024, TT, 512)
    at1 = {n: prm1[:, s.start - (1024 if s.start > PRM1["w_k"].start else 0):
                  s.stop - (1024 if s.start > PRM1["w_k"].start else 0)]
           for n, s in PRM1.items() if n not in ("w_q", "w_k")}
    conv_w = at1["conv_w"].rearrange("p (f w) -> p f w", w=CONV_W)
    lam_in = at1["lam"].rearrange("p (a b) -> p a b", a=4)
    w_gate = at1["w_gate"].rearrange("p (k n) -> p k n", n=8)
    w_r = at1["w_r"].rearrange("p (k n) -> p k n", n=36)
    gate_pre, log_f, lse = stat(16).rearrange("p (i n) -> p i n", i=2), stat(8), stat(8)
    m_max, m_neg, m_den, m_dec, m_abs = stat(8), stat(8), stat(8), stat(8), stat(8)
    neg_b, mean, var8, rstd8 = stat(8), stat(8), stat(8), stat(8)
    lam_two, lam = stat(2), stat(1)
    d_max, d_neg, d_sum, d_inv = stat(16), stat(16), stat(16), stat(16)
    mark = stat(1)
    logits = view(p_mem, 0, TT, 36)
    group8, le8, top8, one_g = (view(p_mem, 128 + 32 * n, TT, 8) for n in range(4))
    pick0, pick1, idx_f = (view(p_mem, 256 + 32 * n, TT, 8) for n in range(3))
    r_stat = view(p_mem, 352, 8, TT)
    gates_moe, rank = (view(p_mem, at, TT, N_EXPERTS + 2 * PAIRS) for at in (384, 456))
    member, most, crowded = view(p_mem, 528, TT, N_EXPERTS), p_mem[:, 592:593], p_mem[:, 593:594].bitcast(I32)
    x_e, hid_b, hid_t = view(gates_mem, 0, PAIRS, KT, P), view(gates_mem, 2048, PAIRS, 512), view(gates_mem, 3072, PAIRS, 4, P)
    y_b, spread_w = view(gates_mem, 4096, PAIRS, D), view(gates_mem, 6144, PAIRS, S)
    one_hot, weighted = (view(gates_mem, at, TT, 2 * PAIRS, CAP) for at in (6656, 7168))
    gain_row = view(pt_mem, 0, D)


    at2 = {n: prm2[:, s] for n, s in PRM2.items()}
    cos_t, sin_t = rope_mem[:, 0:S], rope_mem[:, S:2 * S]
    gates, hid_ff = view(gates_mem, 0, 32, S), view(work_mem, 6144, 32, S)
    q_n, kv_c, k_sw = view(qkv_a, 0, 4, S), view(qkv_a, 1024, 2, S), view(qkv_a, 1536, 2, S)
    v_n = view(qkv_a, 2048, TT, S)
    k_cT, v_c = qkv_a[:, 2560:2560 + N_CMP], qkv_a[0:N_CMP, 2576:2576 + 2 * HD]
    hid_c, p_c = view(qkv_a, 2704, 2, 2, 2 * N_CMP), view(qkv_a, 2824, TT, HEADS, N_CMP)
    gelu_tmp, rope_tmp = pt_mem[:, 1600:1600 + 8 * N_CMP], view(pt_mem, 0, 6, S)
    rope_tmp_c = pt_mem[:, 1536:1536 + N_CMP]
    dup = view(p_mem, 0, 4, 2 * S)
    pc_T = view(gates_mem, 6144, HEADS, S)
    a_low, b_cum = gates_mem[0:GLA_RANK, 4096:4096 + S], view(yt_mem, 3072, 2, S)
    la_l, la_m = view(gates_mem, 4352, 2, S), view(gates_mem, 4864, 2, S)
    xn_a = view(work_mem, 10240, TT, D)
    p_s, pT_s = view(p_mem, 0, 8, 384), view(pt_mem, 0, 8, 384)
    q_s, k_s, v_s = view(qkv_b, 0, 4, S), view(qkv_b, 1024, 4, S), view(qkv_b, 2048, TT, 512)
    q_f, k_f, v_f = view(qkv_a, 0, 4, S), view(qkv_a, 1024, 4, S), view(qkv_a, 2048, TT, 512)
    q_g, k_g = view(qkv_b, 0, 2, S), view(qkv_b, 512, 2, S)
    v_g, g_g = view(qkv_b, 1024, TT, 512), view(qkv_b, 2048, TT, 512)
    decay, q_lv, k_lv = (view(p_mem, 1024 * n, 2, 2, S) for n in range(3))
    att, att_far = view(pt_mem, 0, 2, 4, P), view(pt_mem, 1024, 2, 2, P)
    o_g, square_g, sig_gg = view(pt_mem, 1536, TT, 512), view(qkv_a, 0, TT, 512), view(qkv_a, 1024, TT, 512)
    yT_all, mixed = view(yt_mem, 0, 16, S), view(xn_mem, 0, KT, S)
    w_lo = parts("w_lo", "wring", 0, RING * CHUNK_COLS)
    w_hi_early = view(parts("w_hi_early", "wring", RING * CHUNK_COLS, CHUNK_COLS), 0, 2, HALF)
    w_hi = view(parts("w_hi", "work_mem", 0, AHEAD * HALF), 0, AHEAD, HALF)
    y_hi, y_lo = view(parts("y_hi", "work_mem", 6144, 4096), 0, 16, S), view(parts("y_lo", "work_mem", 12288, 4096), 0, 16, S)
    mixed_hi, mixed_lo = (view(parts(f"mixed_{n}", of, 0, KT * S), 0, KT, S) for n, of in (("hi", "ht_mem"), ("lo", "xn_mem")))
    h_hi, h_lo = mixed_hi, mixed_lo
    h2_hi, h2_lo = mixed_hi, view(parts("h2_lo", "work_mem", 14336, KT * S), 0, KT, S)
    hid_hi, hid_lo = (view(parts(f"hid_{n}", of, first, 32 * S), 0, 32, S)
                      for n, of, first in (("hi", "gates_mem", 0), ("lo", "work_mem", 6144)))
    last_gain = view(ht_mem, 0, D)
    fg = stat(64).rearrange("p (i n) -> p i n", i=TT)
    nsa_gate = fg[:, :, 8:32].rearrange("p i (r m b) -> p i m r b", r=NSA_GROUPS, b=3)
    lf_fox, lse_fox = stat(16), stat(16)
    s_max, s_neg, s_sum, s_inv = stat(32), stat(32), stat(32), stat(32)
    c_max, c_inv = stat(16), stat(16)
    wait_marks = stat(WAIT_MARKS)
    pos_i, ang, turns = p_mem[:, 2048:2304].bitcast(I32), p_mem[:, 2304:2560], p_mem[:, 2560:2816]

    bank_full = [sem(f"bank{b}_full") for b in range(BANKS)]
    bank_read = [sem(f"bank{b}_read") for b in range(BANKS)]
    w_landed = [sem(f"weights{s}_landed") for s in range(SLOTS)]
    x_loaded, const_loaded, params_loaded = sem("x_loaded"), sem("const_loaded"), sem("params_loaded")
    gain_loaded = sem("gain_loaded")
    act_step, dve_step, pool_step = sem("act_step"), sem("dve_step"), sem("pool_step")
    sumsq_ready, var_ready, rstd_ready = sem("sumsq_ready"), sem("var_ready"), sem("rstd_ready")
    xn_ready, x_ready = sem("xn_ready"), sem("x_ready")
    conv_ready, conv_sig, act_ready = sem("conv_ready"), sem("conv_sig"), sem("c_act_ready")
    lam_dots, lam_exp = sem("lam_dots"), sem("lam_exp")
    gates_pre, lse_ready, logf_ready = sem("gates_pre"), sem("lse_ready"), sem("logf_ready")
    rel_saved, rel_loaded = sem("rel_rows_saved"), sem("rel_bias_loaded")
    m_neg_ready, m_exp_ready, m_dec_in, m_dec_out = (sem("m_neg_ready"), sem("m_exp_ready"), sem("m_decay_in"),
                                                     sem("m_decay_out"))
    d_neg_ready, d_exp_ready, a_ready = sem("d_neg_ready"), sem("d_exp_ready"), sem("a_ready")
    centred, squared, var8_ready, rstd8_ready = (sem("centred"), sem("squared"), sem("var8_ready"),
                                                 sem("rstd8_ready"))
    head_norm = sem("head_normed")
    ym_ready, yd_ready = sem("ym_ready"), sem("yd_ready")
    r_neg, r_exp, top_diff, top_exp = sem("router_neg_max"), sem("router_exp"), sem("top_difference"), sem("top_exp")
    member_ready, crowded_ready, moe_done = sem("members_ready"), sem("crowded_ready"), sem("experts_done")

    class Passes:

        def __init__(self, region, name, full, read, landed):
            self.region, self.bank_full, self.bank_read, self.w_landed = region, full, read, landed
            self.slots_ready, self.sig_ready = sem(f"{name}_slots_ready"), sem(f"{name}_sigmoid_ready")
            self.hot_ready = sem(f"{name}_one_hot_ready")
            self.rank_ready, self.turn_done = sem(f"{name}_rank_ready"), sem(f"{name}_turn_done")

        def __getitem__(self, name):
            return self.region[name]

    stored = sem("stored")

    pre = plan_pre()
    moe = plan_moe(pre.after(), pre.next, MOE_TURNS)
    first_pass = Passes(moe, "moe", bank_full, bank_read, w_landed)
    more = plan_moe([0] * BANKS, 0, MOE_TURNS * (PASSES - 1))
    more_passes = Passes(more, "more", [sem(f"more_bank{b}_full") for b in range(BANKS)],
                         [sem(f"more_bank{b}_read") for b in range(BANKS)],
                         [sem(f"more_weights{s}_landed") for s in range(SLOTS)])
    SLOTS_MADE = MOE_TURNS + 1
    turn_chunks = PAIRS * PAIR_CHUNKS
    chunk_users = [(("gate", "up", "down")[c % PAIR_CHUNKS // 2], c // PAIR_CHUNKS) for c in range(turn_chunks)]


    pos_loaded, angle_ready, rope_ready = sem("positions_loaded"), sem("angles_ready"), sem("rope_table_ready")
    params2_loaded = sem("layer_params_loaded")
    nsa_gate_ready, fox_sum, fox_lse, lf_ready = sem("nsa_gate_ready"), sem("fox_logit_ready"), sem("fox_lse_ready"), sem("fox_logf_ready")
    roped, dup_ready, gelu_in, gelu_sig, hid_ready = (sem("roped"), sem("windows_ready"), sem("gelu_in"), sem("gelu_sigmoid"),
                                                      sem("cmp_hidden_ready"))
    la_ready = sem("gla_lse_ready")
    c_in, c_exp, c_ready = sem("cmp_scores_ready"), sem("cmp_exp_ready"), sem("cmp_weights_ready")
    s_neg_ready, s_exp_ready, s_inv_ready, p_scaled = (sem("softmax_neg_max"), sem("softmax_exp"), sem("softmax_inverse"),
                                                       sem("softmax_scaled"))
    sb_log, sb_ready = sem("stick_log_ready"), sem("stick_softplus_ready")
    decay_in, decay_out, level_ready = sem("gla_decay_in"), sem("gla_decay_out"), sem("gla_level_ready")
    g_sig, gate_sig, y_gla = sem("gla_gate_sigmoid"), sem("gates_sigmoid"), sem("gla_y_ready")
    mixed_ready, relu_ready, ffh_ready = sem("mixed_ready"), sem("relu_ready"), sem("ff_hidden_ready")
    ff2_chunk = sem("ff2_chunk_used")
    hi_ready, lo_ready, half_used = sem("weight_high_ready"), sem("weight_low_ready"), sem("weight_half_used")
    y_hi_ready, y_lo_ready, h2_hi_ready = sem("branch_high_ready"), sem("branch_low_ready"), sem("h2_high_ready")
    layer = plan_layer(moe)
    LAYER_FIRST = PRE_CHUNKS + N_EXPERTS // 2 * PAIR_CHUNKS
    SOFTMAXES = NSA_N + FOX_N

    def layer_slot(c):
        return wring[:, (c % RING) * CHUNK_COLS:(c % RING + 1) * CHUNK_COLS]

    def layer_landed(c, l):
        return l * (16 * LAYER_SLOTS // RING) + (16 * (LAYER_FIRST // SLOTS) + 16 * (c // RING + 1))

    def weight_half(h):
        c, second = SPLIT_CHUNKS[h // 2], h % 2
        if c < 22 or 28 <= c < 36:
            k, n, kts, cols = 8, 512, slice(0, 8), slice(second * 256, second * 256 + 256)
        elif c < 26:
            k, n, kts, cols = 4, 1024, slice(0, 4), slice(second * 512, second * 512 + 512)
        elif c < 28:
            k, n, kts, cols = 8, 512, slice(4 * second, 4 * second + 4), slice(0, 512)
        else:
            k, n, kts, cols = 4, 1024, slice(2 * second, 2 * second + 2), slice(0, 1024)
        w, lo = (view(mem, c % RING * CHUNK_COLS, k, n)[:, kts, cols] for mem in (wring, w_lo))
        hi = w_hi_early[:, h % 2, :] if h < LATE else w_hi[:, (h - LATE + 1) % AHEAD, :]
        return c, w, view(hi, 0, kts.stop - kts.start, cols.stop - cols.start), lo

    FILLERS = NSA_FILL + SB_FILL + FOX_FILL + GLA_FILL
    filler_half = {f: 6 + n for n, f in enumerate(FILLERS)}

    def slot(c):
        return wring[:, (c % SLOTS) * CHUNK_COLS:(c % SLOTS + 1) * CHUNK_COLS]

    def landed(first, per, c, turn):
        return turn * (16 * per // SLOTS) + 16 * ((first + c) // SLOTS + 1)

    block = nc.Block()
    block.__enter__()

    @block.sync
    def _(sp):
        sp.dma_start(x, d["x"]).then_inc(x_loaded, 16)
        sp.dma_start(cst[:, :], d["const"][:, 0:CONST["bucket"].start]).then_inc(const_loaded, 16)
        sp.dma_start(prm1[:, 0:PRM1["w_q"].start], d["prm1"][:, 0:PRM1["w_q"].start]).then_inc(params_loaded, 16)
        sp.dma_start(pos_i, d["pos"]).then_inc(pos_loaded, 16)
        sp.dma_start(slot(0), d["w1"][0]).then_inc(w_landed[0], 16)
        sp.dma_start(prm1[:, PRM1["w_q"].start:PRM1_COLS - 1024],
                     d["prm1"][:, PRM1["w_k"].stop:PRM1_COLS]).then_inc(params_loaded, 16)
        sp.dma_start(yt_mem[:, 3072:4096], d["prm1"][:, PRM1["w_q"].start:PRM1["w_k"].stop]).then_inc(params_loaded, 16)
        sp.dma_start(bucket, d["const"][0:REL_BUCKETS, CONST["bucket"]]).then_inc(params_loaded, 16)
        pre_last = [pre[n][1] for n in ("c", "vm", "z", "qd", "kd", "vd")] + [pre["out"][1], pre["out"][3]]
        for c in range(1, PRE_CHUNKS):
            if c >= SLOTS:
                j = pre_last[c - SLOTS]
                sp.wait_ge(bank_full[j.bank], j.count())
            sp.dma_start(slot(c), d["w1"][c]).then_inc(w_landed[c % SLOTS], 16)
            if c == SLOTS:
                sp.dma_start(prm2[:, :], d["prm2"][0]).then_inc(params2_loaded, 16)
            if c == 3:
                for j in pre["rel"]:
                    sp.wait_ge(bank_read[j.bank], j.count())
                sp.dma_start(d["skew"].rearrange("(h p n) -> p h n", h=4, p=P)[:, :, 0:384], rel_row).then_inc(rel_saved, 16)
                sp.wait_ge(rel_saved, 16)
                sp.dma_start(rel_bias, bass.AP(d["skew"].tensor, 127, [[383, P], [384 * P, 4], [1, S]])).then_inc(rel_loaded, 16)
        for j in pre_last[-SLOTS:]:
            sp.wait_ge(bank_full[j.bank], j.count())
        sp.wait_ge(rel_loaded, 16)
        for j in pre["ydt"]:
            sp.wait_ge(bank_read[j.bank], j.count())
        sp.dma_start(gain_row, d["gain"][0]).then_inc(gain_loaded, 16)
        with sp.Fori(0, MOE_TURNS) as turn:
            for c in range(turn_chunks):
                j = moe[chunk_users[c - SLOTS]][-1]
                sp.wait_ge(bank_full[j.bank], j.count(turn - 1 if c < SLOTS else turn))
                sp.dma_start(slot(c), d["w1"][PRE_CHUNKS + c + turn * turn_chunks]).then_inc(w_landed[c % SLOTS], 16)
        for c in range(turn_chunks - SLOTS, turn_chunks):
            j = moe[chunk_users[c]][-1]
            sp.wait_ge(bank_full[j.bank], j.count(MOE_TURNS - 1))
        sp.wait_ge(crowded_ready, 1)
        with sp.If(sp.value_load(crowded[0:1, :], min_val=0, max_val=1) > 0):
            with sp.Fori(0, PASSES - 1) as again:
                with sp.Fori(0, MOE_TURNS) as turn:
                    at = again * MOE_TURNS + turn
                    sp.wait_ge(more_passes.turn_done, at + 1)
                    for c in range(turn_chunks):
                        if c >= SLOTS:
                            j = more[chunk_users[c - SLOTS]][-1]
                            sp.wait_ge(more_passes.bank_full[j.bank], j.count(at))
                        sp.dma_start(slot(c), d["w1"][PRE_CHUNKS + c + turn * turn_chunks]).then_inc(
                            more_passes.w_landed[c % SLOTS], 16)
            sp.wait_ge(more_passes.turn_done, MOE_TURNS * (PASSES - 1) + 1)
        sp.end_ifs()
        uses = {0: ("nsa_q", 1), 1: ("nsa_k", 1), 2: ("gla_a", 0), 3: ("hid", 0), 4: ("hid", 1), 8: ("gates", 1), 12: ("gates", 3)}
        uses |= {c: (n, 1) for c, n in ((5, "sb_q"), (6, "sb_k"), (7, "sb_v"), (9, "fox_q"), (10, "fox_k"), (11, "fox_v"),
                                        (13, "gla_qk"), (14, "gla_v"), (15, "gla_g"))}
        uses |= {16 + n: ("gates", 5 + 2 * n) for n in range(6)}
        uses |= {22 + n: ("branch", 4 * n + 3) for n in range(N_BRANCH)}
        uses |= {26 + n: ("out", 2 * n + 1) for n in range(2)} | {28 + n: ("ff1", 2 * n + 1) for n in range(8)}
        with sp.Fori(0, LAYERS) as l:
            for c in range(LAYER_SLOTS):
                if c == LAYER_CHUNKS - SLOTS:
                    j = layer["h2"][-1]
                    sp.wait_ge(bank_read[j.bank], j.count(l))
                    sp.dma_start(prm2[:, :], d["prm2"][l + 1]).then_inc(params2_loaded, 16)
                before = (c - RING) % LAYER_SLOTS
                turn = l - 1 if c < RING else l
                if before < 36:
                    n, k = uses[before]
                    j = layer[n][k]
                    sp.wait_ge(bank_full[j.bank], j.count(turn))
                elif before < LAYER_CHUNKS - 1:
                    sp.wait_ge(ff2_chunk, (turn + 1) * FF2_SIGNALS + (before - 35))
                elif before == LAYER_CHUNKS - 1:
                    j = layer["ff2"][3]
                    sp.wait_ge(bank_full[j.bank], j.count(turn))
                else:
                    sp.wait_ge(w_landed[before % RING], layer_landed(before, turn))
                if c < LAYER_CHUNKS:
                    sp.dma_start(layer_slot(c), d["w2"][c + l * LAYER_CHUNKS]).then_inc(w_landed[c % RING], 16)
                else:
                    sp.dma_start(layer_slot(c)[:, 0:8], d["w2"][l * LAYER_CHUNKS][:, 0:8]).then_inc(w_landed[c % RING], 16)
        j = layer["ff1"][-1]
        sp.wait_ge(bank_full[j.bank], j.count(LAYERS - 1))
        sp.dma_start(last_gain, d["gain"][1]).then_inc(gain_loaded, 16)
        sp.wait_ge(params2_loaded, 16 * LAYERS + 16)
        sp.wait_ge(w_landed[LAYER_CHUNKS % RING], layer_landed(LAYER_CHUNKS, LAYERS - 1))
        sp.wait_ge(x_ready, LAYERS + 2)
        sp.dma_start(d["out"], x).then_inc(stored, 16)
        sp.wait_ge(stored, 16)

    @block.tensor
    def _(pe):
        def free(j, turn=0):
            if not (isinstance(turn, int) and j.count(turn) == 1):
                pe.wait_ge(bank_read[j.bank], j.count(turn) - 1)

        def in_sbuf(jobs, turn=0, then=None):
            for j in last_in_bank(jobs, then):
                pe.wait_ge(bank_read[j.bank], j.count(turn))

        def chunk(c, first, per=0, turn=0):
            pe.wait_ge(w_landed[c % SLOTS], landed(first, per, c, turn))
            return slot(c)

        def turn_x(jobs, turn=0, src=xn):
            for n, j in enumerate(jobs):
                free(j, turn)
                for t in range(2):
                    for i in range(TT):
                        dt = 2 * n + t
                        mm = pe.transpose(psum[j.bank][:, t * S + i * P:t * S + (i + 1) * P],
                                          src[:, i, dt * P:(dt + 1) * P], ident)
                mm.then_inc(bank_full[j.bank], 1)

        def project_a(j, w, ft, turn=0, src=hT, kts=KT):
            free(j, turn)
            for t in range(2):
                for k in range(kts):
                    mm = pe.matmul(psum[j.bank][:, t * S:(t + 1) * S], w[:, k, (ft + t) * P:(ft + t + 1) * P],
                                   src[:, k, :], start=(k == 0), stop=(k == kts - 1))
            mm.then_inc(bank_full[j.bank], 1)

        def project_b(j, w, i, n, turn=0, src=hT):
            free(j, turn)
            for k in range(KT):
                mm = pe.matmul(psum[j.bank][:, 0:n], src[:, k, i * P:(i + 1) * P], w[:, k, 0:n],
                               start=(k == 0), stop=(k == KT - 1))
            mm.then_inc(bank_full[j.bank], 1)

        def scores(j, q, k, turn=0):
            free(j, turn)
            pe.matmul(psum[j.bank][:, 0:P], q[:, 0:P], k[:, 0:P], start=True, stop=True)
            mm = pe.matmul(psum[j.bank][:, P:384], q[:, P:S], k[:, 0:S], start=True, stop=True)
            mm.then_inc(bank_full[j.bank], 1)

        def turn_three(j, src, turn=0):
            free(j, turn)
            for b in range(3):
                mm = pe.transpose(psum[j.bank][:, b * P:(b + 1) * P], src[:, b * P:(b + 1) * P], ident)
            mm.then_inc(bank_full[j.bank], 1)

        def mix_heads(j, i, wT, v, turn=0):
            free(j, turn)
            for h in range(4):
                out = psum[j.bank][:, h * P:(h + 1) * P]
                if i == 0:
                    mm = pe.matmul(out, wT[:, h, 0:P], v[:, 0, h * P:(h + 1) * P], start=True, stop=True)
                else:
                    pe.matmul(out, wT[:, h, P:2 * P], v[:, 0, h * P:(h + 1) * P], start=True, stop=False)
                    mm = pe.matmul(out, wT[:, h, 2 * P:384], v[:, 1, h * P:(h + 1) * P], start=False, stop=True)
            mm.then_inc(bank_full[j.bank], 1)

        def turn_four(j, src, turn=0):
            free(j, turn)
            for h in range(4):
                mm = pe.transpose(psum[j.bank][:, h * P:(h + 1) * P], src[:, h * P:(h + 1) * P], ident)
            mm.then_inc(bank_full[j.bank], 1)

        def project_out(jobs, first, c0, per=0, turn=0):
            def run(src):
                for half in range(2):
                    w = chunk(c0 + half, first, per, turn).rearrange("p (k n) -> p k n", k=KT)
                    for i in range(TT):
                        project_b(jobs[2 * half + i], w, i, 512, turn, src)
            return run

        k8 = lambda w: w.rearrange("p (k n) -> p k n", k=KT)

        pe.wait_ge(const_loaded, 16)
        pe.wait_ge(xn_ready, 2)
        turn_x(pre["ht"])
        in_sbuf(pre["ht"])
        for j in range(2):
            project_a(pre["c"][j], k8(chunk(0, 0)), 2 * j)
        for i in range(TT):
            project_b(pre["vm"][i], k8(chunk(1, 0)), i, 512)
        for j in range(2):
            project_a(pre["z"][j], k8(chunk(2, 0)), 2 * j)
        pe.wait_ge(params_loaded, 64)
        for h, j in enumerate(pre["rel"]):
            free(j)
            pe.matmul(psum[j.bank][:, 0:384], at1["rel"][0:REL_BUCKETS, h:h + 1].to_broadcast([REL_BUCKETS, P]),
                      bucket, start=True, stop=True).then_inc(bank_full[j.bank], 1)
        pe.wait_ge(act_ready, 4)
        for name, w in (("mq", w_mq), ("mk", w_mk)):
            for n, j in enumerate(pre[name]):
                free(j)
                for t in range(2):
                    mm = pe.matmul(psum[j.bank][:, t * S:(t + 1) * S], w[:, 2 * n + t, :], c_act[:, 2 * n + t, :],
                                   start=True, stop=True)
                mm.then_inc(bank_full[j.bank], 1)
        in_sbuf(pre["vm"])
        for n, j in enumerate(pre["vmt"]):
            free(j)
            for t in range(2):
                for i in range(TT):
                    ft = 2 * n + t
                    mm = pe.transpose(psum[j.bank][:, t * S + i * P:t * S + (i + 1) * P],
                                      v_m[:, i, ft * P:(ft + 1) * P], ident)
            mm.then_inc(bank_full[j.bank], 1)
        in_sbuf(pre["mq"] + pre["mk"] + pre["vmt"])
        j = pre["gate"][0]
        free(j)
        for i in range(TT):
            for k in range(12):
                src = (m_q, m_k, v_mT)[k // 4]
                mm = pe.matmul(psum[j.bank][:, 8 * i:8 * i + 8], src[:, k % 4, i * P:(i + 1) * P], w_gate[:, k, :],
                               start=(k == 0), stop=(k == 11))
        mm.then_inc(bank_full[j.bank], 1)
        for j in range(2):
            project_a(pre["qd"][j], k8(chunk(3, 0)), 2 * j)
        for j in range(2):
            project_a(pre["kd"][j], k8(chunk(4, 0)), 2 * j)
        for i in range(TT):
            project_b(pre["vd"][i], k8(chunk(5, 0)), i, 512)

        pe.wait_ge(logf_ready, 1)
        lf = log_f.rearrange("p (i n) -> p i n", i=2)
        j = pre["negb"][0]
        free(j)
        pe.matmul(psum[j.bank][:, 0:4], negtriu[:, 0:P], lf[:, 0, :], start=True, stop=True)
        pe.matmul(psum[j.bank][:, 4:8], negtriu[:, P:S], lf[:, 0, :], start=True, stop=False)
        pe.matmul(psum[j.bank][:, 4:8], negtriu[:, 0:P], lf[:, 1, :], start=False, stop=True).then_inc(bank_full[j.bank], 1)
        for h in range(ML_HEADS):
            j = pre["u"][h]
            free(j)
            b = psum[j.bank]
            lf_h = [lf[:, i, h:h + 1].to_broadcast([P, P]) for i in range(TT)]
            ig_h = [gate_pre[:, i, h:h + 1].to_broadcast([P, P]) for i in range(TT)]
            pe.matmul(b[:, 0:S], lf_h[0], negtriu, start=True, stop=False)
            pe.matmul(b[:, P:S], lf_h[1], negtriu[:, 0:P], start=False, stop=False)
            pe.matmul(b[:, 0:P], ig_h[0], ident, start=False, stop=False)
            pe.matmul(b[:, P:S], ig_h[1], ident, start=False, stop=True).then_inc(bank_full[j.bank], 1)
            scores(pre["qk"][h], m_q[:, h, :], m_k[:, h, :])
        in_sbuf(pre["qd"] + pre["kd"])
        for n in range(2 * DA_HEADS):
            h, r = n // 2, slice(DA_QD * (n % 2), DA_QD * (n % 2) + DA_QD)
            scores(pre["s"][n], q_d[r, h, :], k_d[r, h, :])
            if n % 2:
                in_sbuf([pre["qk"][h]])
                turn_three(pre["wt"][h], w_m[:, h, :])
        in_sbuf(pre["wt"])
        for i in range(TT):
            mix_heads(pre["num"][i], i, w_mT, v_m)
        for h in range(DA_HEADS):
            pe.wait_ge(a_ready, h + 1)
            turn_three(pre["at"][h], p_d[:, 2 * h, :])
        in_sbuf(pre["at"] + pre["vd"])
        for i in range(TT):
            mix_heads(pre["pv"][i], i, a_T, v_d)
        pe.wait_ge(head_norm, 1)
        for i in range(TT):
            turn_four(pre["hnt"][i], h_m[:, i, :])
        pe.wait_ge(head_norm, 2)
        for i in range(TT):
            turn_four(pre["ydt"][i], y_d[:, i, :])
        pe.wait_ge(ym_ready, 2)
        in_sbuf(pre["ydt"])
        project_out(pre["out"], 0, 6)(y_T)
        pe.wait_ge(xn_ready, 4)
        turn_x(pre["h2"])
        in_sbuf(pre["h2"])
        j = pre["router"][0]
        free(j)
        for i in range(TT):
            for k in range(KT):
                mm = pe.matmul(psum[j.bank][:, 36 * i:36 * i + 36], hT[:, k, i * P:(i + 1) * P], w_r[:, k, :],
                               start=(k == 0), stop=(k == KT - 1))
        mm.then_inc(bank_full[j.bank], 1)
        pe.wait_ge(member_ready, 1)
        j = pre["rank"][0]
        free(j)
        n = N_EXPERTS
        ones = C("one").to_broadcast([P, P])
        pe.matmul(psum[j.bank][:, 0:n], C("strict"), member[:, 0, :], start=True, stop=True).then_inc(ff2_chunk, FF2_SIGNALS)
        pe.matmul(psum[j.bank][:, n:2 * n], ones, member[:, 0, :], start=True, stop=False)
        pe.matmul(psum[j.bank][:, n:2 * n], C("strict"), member[:, 1, :], start=False, stop=True)
        pe.matmul(psum[j.bank][:, 2 * n:3 * n], ones, member[:, 0, :], start=True, stop=False)
        pe.matmul(psum[j.bank][:, 2 * n:3 * n], ones, member[:, 1, :], start=False, stop=True).then_inc(bank_full[j.bank], 1)

        def experts(r, turn, at, slots_before, chunks_before):
            def ready(j):
                if r is first_pass or j.use > 0:
                    pe.wait_ge(r.bank_read[j.bank], j.count(at) - 1)

            def copied(jobs, then):
                for j in last_in_bank(jobs, then):
                    pe.wait_ge(r.bank_read[j.bank], j.count(at))

            def weights(pair, n):
                cs = [PAIR_CHUNKS * pair + 2 * n + e for e in range(2)]
                for c in cs:
                    pe.wait_ge(r.w_landed[c % SLOTS], landed(chunks_before, turn_chunks, c, at))
                return [slot(c).rearrange("p (k n) -> p k n", k=(KT, KT, 4)[n]) for c in cs]

            for step, pair in MOE_STEPS:
                jobs = r[step, pair]
                j = jobs[0]
                out = psum[j.bank]
                two = slice(2 * pair, 2 * pair + 2)
                if step == "pick":
                    if pair == 0:
                        pe.wait_ge(r.slots_ready, slots_before + turn + 1)
                    for n, j in enumerate(jobs):
                        ready(j)
                        for k in range(4):
                            for i in range(TT):
                                mm = pe.matmul(psum[j.bank][:, k * P:(k + 1) * P], xn[:, i, (4 * n + k) * P:(4 * n + k + 1) * P],
                                               one_hot[:, i, two, :], start=(i == 0), stop=(i == TT - 1))
                        if n == 0:
                            mm.then_inc(r.bank_full[j.bank], 1)
                elif step == "turn":
                    ready(j)
                    for i in range(TT):
                        mm = pe.transpose(out[:, i * P:(i + 1) * P], weighted[:, i, two, :], ident)
                elif step in ("gate", "up"):
                    if step == "gate":
                        copied(r["pick", pair], j)
                    ready(j)
                    w = weights(pair, ("gate", "up").index(step))
                    for k in range(KT):
                        for e in range(2):
                            half = slice(e * CAP, (e + 1) * CAP)
                            mm = pe.matmul(out[half, :], x_e[:, pair, k, half], w[e][:, k, :], start=(k == 0), stop=(k == KT - 1))
                elif step == "flip":
                    copied(r["up", pair], j)
                    ready(j)
                    for ft in range(4):
                        mm = pe.transpose(out[:, ft * P:(ft + 1) * P], hid_b[:, pair, ft * P:(ft + 1) * P], ident)
                elif step == "down":
                    copied(r["flip", pair], j)
                    w = weights(pair, 2)
                    for n, j in enumerate(jobs):
                        ready(j)
                        for ft in range(4):
                            for e in range(2):
                                half = slice(e * CAP, (e + 1) * CAP)
                                mm = pe.matmul(psum[j.bank][half, :], hid_t[:, pair, ft, half],
                                               w[e][:, ft, n * 512:(n + 1) * 512], start=(ft == 0), stop=(ft == 3))
                        if n == 0:
                            mm.then_inc(r.bank_full[j.bank], 1)
                else:
                    copied(r["down", pair] + r["turn", pair], j)
                    for n, j in enumerate(jobs):
                        half, i = divmod(n, 2)
                        ready(j)
                        mm = pe.matmul(psum[j.bank][:, :], spread_w[:, pair, i * P:(i + 1) * P],
                                       y_b[:, pair, half * 512:(half + 1) * 512], start=True, stop=True)
                        if n < 3:
                            mm.then_inc(r.bank_full[j.bank], 1)
                mm.then_inc(r.bank_full[j.bank], 1)

        with pe.Fori(0, MOE_TURNS) as turn:
            experts(first_pass, turn, turn, 0, PRE_CHUNKS)
        for j in last_in_bank([j for step in MOE_STEPS for j in moe[step]]):
            pe.wait_ge(bank_read[j.bank], j.count(MOE_TURNS - 1))
        pe.wait_ge(crowded_ready, 1)
        with pe.If(pe.value_load(crowded[0:1, :], min_val=0, max_val=1) > 0):
            with pe.Fori(0, PASSES - 1) as again:
                with pe.Fori(0, MOE_TURNS) as turn:
                    at = again * MOE_TURNS + turn
                    pe.wait_ge(more_passes.turn_done, at + 1)
                    experts(more_passes, turn, at, again * SLOTS_MADE, 0)
        pe.end_ifs()
        pe.wait_ge(moe_done, 1)
        def rope(j, tiles, turn, n=S):
            free(j, turn)
            for t, src in enumerate(tiles):
                mm = pe.matmul(psum[j.bank][:, t * S:t * S + n], C("rope"), src, start=True, stop=True)
            mm.then_inc(bank_full[j.bank], 1)

        def heads_out(j, lhs, rhs, turn):
            free(j, turn)
            for r in range(2):
                rows = slice(HD * r, HD * r + HD)
                pe.matmul(psum[j.bank][rows, 0:S], lhs[r][0], rhs[r][:, 0:S], start=True, stop=False)
                mm = pe.matmul(psum[j.bank][rows, P:S], lhs[r][1], rhs[r][:, S:384], start=False, stop=True)
            mm.then_inc(bank_full[j.bank], 1)

        with pe.Fori(0, LAYERS) as l:
            h_parts = (h_hi, h_lo)

            def half_ready(h):
                pe.wait_ge(lo_ready, HALVES * l + h + 1)
                return weight_half(h)[2:]

            def split_a(j, w, first, x, used):
                free(j, l)
                kts = w[0].shape[1]
                for t in range(2):
                    out, cols = psum[j.bank][:, t * S:(t + 1) * S], slice(first + t * P, first + (t + 1) * P)
                    for k in range(kts):
                        pe.matmul(out, w[0][:, k, cols], x[0][:, k, :], start=(k == 0), stop=False)
                        mm = pe.matmul(out, w[0][:, k, cols], x[1][:, k, :], start=False, stop=False)
                    if used and t == 1:
                        mm.then_inc(half_used, 1)
                    for k in range(kts):
                        mm = pe.matmul(out, w[1][:, k, cols], x[0][:, k, :], start=False, stop=(k == kts - 1))
                mm.then_inc(bank_full[j.bank], 1)

            def split_b(out, w, k, kt, i, x, first, last):
                rows = slice(i * P, (i + 1) * P)
                if last is None:
                    pe.matmul(out, x[0][:, kt, rows], w[0][:, k, :], start=first, stop=False)
                    return pe.matmul(out, x[1][:, kt, rows], w[0][:, k, :], start=False, stop=False)
                return pe.matmul(out, x[0][:, kt, rows], w[1][:, k, :], start=False, stop=last)

            def split_tokens(j, w, first, cols, used=True):
                free(j, l)
                for i in range(TT):
                    out, rows = psum[j.bank][:, i * cols:(i + 1) * cols], slice(i * P, (i + 1) * P)
                    for k in range(KT):
                        pe.matmul(out, h_hi[:, k, rows], w[0][:, k, first:first + cols], start=(k == 0), stop=False)
                        mm = pe.matmul(out, h_lo[:, k, rows], w[0][:, k, first:first + cols], start=False, stop=False)
                    if used and i == TT - 1:
                        mm.then_inc(half_used, 1)
                    for k in range(KT):
                        mm = pe.matmul(out, h_hi[:, k, rows], w[1][:, k, first:first + cols], start=False, stop=(k == KT - 1))
                mm.then_inc(bank_full[j.bank], 1)

            def fill(name, n):
                w, j = half_ready(filler_half[name, n]), layer[name][n]
                if name in ("sb_v", "fox_v", "gla_v", "gla_g"):
                    split_tokens(j, w, 0, S)
                else:
                    split_a(j, w, 0, h_parts, True)

            pe.wait_ge(params2_loaded, 16 * l + 16)
            pe.wait_ge(xn_ready, 4 * l + 8)
            turn_x(layer["ht"], l, xn_a)
            in_sbuf(layer["ht"], l, layer["nsa_q"][0])
            for n in range(2):
                split_a(layer["nsa_q"][n], half_ready(n), 0, h_parts, True)
            for n in range(2):
                split_a(layer["nsa_k"][n], half_ready(2 + n), 0, h_parts, True)
            split_tokens(layer["nsa_v"][0], half_ready(4), 0, S)
            w = half_ready(5)
            split_tokens(layer["nsa_f"][0], w, 0, 32, used=False)
            j = layer["gla_a"][0]
            free(j, l)
            for part, x_parts in ((w[0], h_parts), (w[1], h_parts[:1])):
                for k in range(KT):
                    for x_part in x_parts:
                        mm = pe.matmul(psum[j.bank][0:GLA_RANK, 0:S], part[:, k, 32:32 + GLA_RANK], x_part[:, k, :],
                                       start=(part is w[0] and k == 0 and x_part is h_hi), stop=(part is w[1] and k == KT - 1))
                if part is w[0]:
                    mm.then_inc(half_used, 1)
            mm.then_inc(bank_full[j.bank], 1)
            in_sbuf(layer["nsa_q"] + layer["nsa_k"] + layer["gla_a"], l, layer["rope_q"][0])
            for n in range(2):
                rope(layer["rope_q"][n], [q_n[:, 2 * n + t, :] for t in range(2)], l)
            rope(layer["rope_k"][0], [k_sw[:, t, :] for t in range(2)], l)
            for n, j in enumerate(layer["dup"]):
                free(j, l)
                for g in range(NSA_GROUPS):
                    mm = pe.matmul(psum[j.bank][:, g * S:(g + 1) * S], C("dup")[:, g * P:(g + 1) * P], kv_c[:, n, :],
                                   start=True, stop=True)
                mm.then_inc(bank_full[j.bank], 1)
            for n, j in enumerate(layer["hid"]):
                pe.wait_ge(w_landed[(3 + n) % RING], layer_landed(3 + n, l))
                w = layer_slot(3 + n).rearrange("p (k n) -> p k n", k=16)
                pe.wait_ge(dup_ready, 8 * l + 4 * n + 4)
                free(j, l)
                for half in range(2):
                    for k in range(16):
                        win = dup[:, 2 * n + k // 8, :].rearrange("p (g c s) -> p g c s", g=2, s=CMP_STRIDE)
                        mm = pe.matmul(psum[j.bank][:, half * 30:half * 30 + 30].rearrange("p (g c) -> p g c", g=2),
                                       w[:, k, half * P:(half + 1) * P],
                                       win[:, :, k // 8:k // 8 + N_CMP, 2 * (k % 8)], start=(k == 0), stop=(k == 15))
                mm.then_inc(bank_full[j.bank], 1)
            pe.wait_ge(hid_ready, l + 1)
            j = layer["kc"][0]
            free(j, l)
            for g in range(NSA_GROUPS):
                for half in range(2):
                    mm = pe.matmul(psum[j.bank][g * HD:(g + 1) * HD, 0:N_CMP], at2["w_k2"][:, half * HD:(half + 1) * HD],
                                   hid_c[:, 0, half, g * N_CMP:(g + 1) * N_CMP], start=(half == 0), stop=(half == 1))
            mm.then_inc(bank_full[j.bank], 1)
            j = layer["vc"][0]
            free(j, l)
            for g in range(NSA_GROUPS):
                for half in range(2):
                    mm = pe.matmul(psum[j.bank][0:N_CMP, g * HD:(g + 1) * HD], hid_c[:, 1, half, g * N_CMP:(g + 1) * N_CMP],
                                   at2["w_v2"][:, half * HD:(half + 1) * HD], start=(half == 0), stop=(half == 1))
            mm.then_inc(bank_full[j.bank], 1)
            in_sbuf(layer["kc"], l, layer["rope_c"][0])
            rope(layer["rope_c"][0], [k_cT], l, N_CMP)
            j = layer["gla_la"][0]
            free(j, l)
            for t in range(2):
                mm = pe.matmul(psum[j.bank][:, t * S:(t + 1) * S], at2["w_alpha"][0:GLA_RANK, t * P:(t + 1) * P], a_low,
                               start=True, stop=True)
            mm.then_inc(bank_full[j.bank], 1)
            pe.wait_ge(roped, 4 * l + 4)
            for r, j in enumerate(layer["cs"]):
                free(j, l)
                rows = slice(HD * r, HD * r + HD)
                for i in range(TT):
                    for m in range(NSA_HPG):
                        at = (NSA_HPG * i + m) * N_CMP
                        mm = pe.matmul(psum[j.bank][:, at:at + N_CMP], q_n[rows, m, i * P:(i + 1) * P], k_cT[rows, :],
                                       start=True, stop=True)
                mm.then_inc(bank_full[j.bank], 1)
            pe.wait_ge(c_ready, l + 1)
            for n, j in enumerate(layer["ct"]):
                free(j, l)
                for r in range(2):
                    for i in range(TT):
                        mm = pe.transpose(psum[j.bank][0:N_CMP, r * S + i * P:r * S + (i + 1) * P], p_c[:, i, 2 * n + r, :], ident)
                mm.then_inc(bank_full[j.bank], 1)
            in_sbuf(layer["nsa_v"] + layer["vc"] + layer["ct"], l, layer["nsa", "score", 0][0])
            for kind, n in nsa_steps():
                if kind == "fill":
                    fill(*n)
                    continue
                j = layer["nsa", kind, n][0]
                if kind == "score":
                    m, r, br = n // 4, n // 2 % 2, n % 2
                    rows = slice(HD * r, HD * r + HD)
                    scores(j, q_n[rows, m, :], k_sw[rows, br, :], l)
                elif kind == "turn":
                    pe.wait_ge(p_scaled, SOFTMAXES * l + n + 1)
                    turn_three(j, p_s[:, n % 8, :], l)
                else:
                    in_sbuf([layer["nsa", "turn", 4 * n + k][0] for k in range(4)], l, j)
                    free(j, l)
                    for r in range(2):
                        out = psum[j.bank][HD * r:HD * r + HD, :]
                        pe.matmul(out[:, 0:S], v_c[:, r * HD:(r + 1) * HD], pc_T[0:N_CMP, 2 * n + r, :], start=True, stop=False)
                        for br in range(2):
                            wT, cols = pT_s[:, (4 * n + 2 * r + br) % 8, :], slice(br * P + r * HD, br * P + r * HD + HD)
                            pe.matmul(out[:, 0:S], v_n[:, 0, cols], wT[:, 0:S], start=False, stop=False)
                            mm = pe.matmul(out[:, P:S], v_n[:, 1, cols], wT[:, S:384], start=False, stop=(br == 1))
                    mm.then_inc(bank_full[j.bank], 1)
            in_sbuf(layer["sb_q"] + layer["sb_k"] + layer["sb_v"], l, layer["sb", "score", 0][0])

            def stick(j, n, stop):
                rows = slice(HD * (n % 2), HD * (n % 2) + HD)
                q, k = q_s[rows, n // 2, :], k_s[rows, n // 2, :]
                near = pe.matmul(psum[j.bank][:, 0:S], k[:, 0:P], q, start=True, stop=stop)
                if stop:
                    return pe.matmul(psum[j.bank][:, S:384], k[:, P:S], q[:, P:S], start=True, stop=True)
                sp_ = p_s[:, n, :]
                b = psum[j.bank]
                pe.matmul(b[:, 0:S], C("sufneg"), sp_[:, 0:S], start=False, stop=False)
                pe.matmul(b[:, P:S], negtriu[:, P:S], sp_[:, S:384], start=False, stop=False)
                pe.matmul(b[:, 0:P], ident, C("negstrict"), start=False, stop=True)
                pe.matmul(b[:, S:384], k[:, P:S], q[:, P:S], start=True, stop=False)
                pe.matmul(b[:, S:384], C("sufneg"), sp_[:, S:384], start=False, stop=False)
                return pe.matmul(b[:, S:384], ident, C("negstrict"), start=False, stop=True)

            for kind, n in sb_steps():
                if kind == "fill":
                    fill(*n)
                    continue
                j = layer["sb", kind, n][0]
                if kind == "score":
                    free(j, l)
                    stick(j, n, True).then_inc(bank_full[j.bank], 1)
                elif kind == "again":
                    pe.wait_ge(sb_ready, 8 * l + n + 1)
                    free(j, l)
                    stick(j, n, False).then_inc(bank_full[j.bank], 1)
                else:
                    in_sbuf([layer["sb", "again", 2 * n + r][0] for r in range(2)], l, j)
                    heads_out(j, [[v_s[:, i, (2 * n + r) * HD:(2 * n + r + 1) * HD] for i in range(TT)] for r in range(2)],
                              [pT_s[:, 2 * n + r, :] for r in range(2)], l)
            in_sbuf(layer["fox_q"] + layer["fox_k"] + layer["fox_v"], l, layer["fox", "score", 0][0])
            pe.wait_ge(lf_ready, l + 1)
            lf2 = lf_fox.rearrange("p (i n) -> p i n", i=2)
            for kind, n in fox_steps():
                if kind == "fill":
                    fill(*n)
                    continue
                j = layer["fox", kind, n][0]
                if kind == "score":
                    free(j, l)
                    rows = slice(HD * (n % 2), HD * (n % 2) + HD)
                    q, k = q_f[rows, n // 2, :], k_f[rows, n // 2, :]
                    lf_h = [lf2[:, i, n:n + 1].to_broadcast([P, P]) for i in range(TT)]
                    b = psum[j.bank]
                    pe.matmul(b[:, 0:P], q[:, 0:P], k[:, 0:P], start=True, stop=False)
                    pe.matmul(b[:, 0:P], lf_h[0], negtriu[:, 0:P], start=False, stop=True)
                    pe.matmul(b[:, P:384], q[:, P:S], k, start=True, stop=False)
                    pe.matmul(b[:, P:384], lf_h[0], negtriu, start=False, stop=False)
                    pe.matmul(b[:, S:384], lf_h[1], negtriu[:, 0:P], start=False, stop=True).then_inc(bank_full[j.bank], 1)
                elif kind == "turn":
                    pe.wait_ge(p_scaled, SOFTMAXES * l + NSA_N + n + 1)
                    turn_three(j, p_s[:, n, :], l)
                else:
                    in_sbuf([layer["fox", "turn", 2 * n + r][0] for r in range(2)], l, j)
                    heads_out(j, [[v_f[:, i, (2 * n + r) * HD:(2 * n + r + 1) * HD] for i in range(TT)] for r in range(2)],
                              [pT_s[:, 2 * n + r, :] for r in range(2)], l)
            in_sbuf(layer["gla_qk"], l, layer["gla", "level", 0][0])
            for kind, n in gla_steps():
                if kind == "fill":
                    fill(*n)
                    continue
                if n < len(GLA_LEVELS):
                    pe.wait_ge(level_ready, 8 * l + n + 1)
                    q, k = q_lv[:, n % 2], k_lv[:, n % 2]
                else:
                    q, k = q_g, k_g
                for r, j in enumerate(layer["gla", kind, n]):
                    free(j, l)
                    rows = slice(HD * r, HD * r + HD)
                    for i in range(1 if n == 0 else TT):
                        for t in range(2):
                            keys, queries = (slice(0, P), slice(P, S)) if n == 0 else (slice(i * P, (i + 1) * P),) * 2
                            mm = pe.matmul(psum[j.bank][:, (2 * i + t) * P:(2 * i + t + 1) * P], k[rows, t, keys],
                                           q[rows, t, queries], start=True, stop=True)
                    mm.then_inc(bank_full[j.bank], 1)
            in_sbuf(layer["gla_v"] + [j for n in range(9) for j in layer["gla", "level", n]], l, layer["gla_o"][0])
            for i, j in enumerate(layer["gla_o"]):
                free(j, l)
                for h in range(GLA_HEADS):
                    out, cols = psum[j.bank][:, h * P:(h + 1) * P], slice(h * P, (h + 1) * P)
                    if i:
                        pe.matmul(out, att_far[:, h % 2, h // 2, :], v_g[:, 0, cols], start=True, stop=False)
                    mm = pe.matmul(out, att[:, h % 2, 2 * i + h // 2, :], v_g[:, i, cols], start=(i == 0), stop=True)
                mm.then_inc(bank_full[j.bank], 1)

            def branch(n):
                pe.wait_ge(y_lo_ready, 5 * l + (n + 1 if n < 3 else 5))
                tiles = slice(4 * n, 4 * n + 4)
                for second in range(2):
                    w = half_ready(LATE + 2 * n + second)
                    for k in range(2):
                        split_a(layer["branch"][4 * n + 2 * second + k], w, 256 * k, (y_hi[:, tiles, :], y_lo[:, tiles, :]), k == 1)

            pe.wait_ge(y_gla, l + 1)
            for i, j in enumerate(layer["gla_t"]):
                turn_four(j, o_g[:, i, :], l)
            for n in range(N_BRANCH):
                branch(n)
            for h in range(4):
                half, second = divmod(h, 2)
                w = half_ready(LATE + 8 + h)
                pe.wait_ge(mixed_ready, 4 * l + (2 if h == 0 else 4))
                for i in range(TT):
                    j = layer["out"][2 * half + i]
                    if second == 0:
                        free(j, l)
                    for k in range(4):
                        mm = split_b(psum[j.bank][:, :], w, k, 4 * second + k, i, (mixed_hi, mixed_lo), h % 2 == 0 and k == 0, None)
                    if i == 1:
                        mm.then_inc(half_used, 1)
                    for k in range(4):
                        mm = split_b(psum[j.bank][:, :], w, k, 4 * second + k, i, (mixed_hi, mixed_lo), False,
                                     second == 1 and k == 3)
                    if second == 1:
                        mm.then_inc(bank_full[j.bank], 1)
            pe.wait_ge(xn_ready, 4 * l + 10)
            turn_x(layer["h2"], l)
            in_sbuf(layer["h2"], l, layer["ff1"][0])
            for n in range(16):
                split_a(layer["ff1"][n], half_ready(LATE + 12 + n), 0, (h2_hi, h2_lo), True)
            for h in range(16):
                w = half_ready(LATE + 28 + h)
                pe.wait_ge(ffh_ready, 16 * l + h + 1)
                for k in range(2):
                    for n, j in enumerate(layer["ff2"]):
                        if h == 0 and k == 0:
                            free(j, l)
                        half, i = divmod(n, 2)
                        part = [v[:, :, half * 512:(half + 1) * 512] for v in w]
                        mm = split_b(psum[j.bank][:, :], part, k, 2 * h + k, i, (hid_hi, hid_lo), h == 0 and k == 0, None)
                mm.then_inc(half_used, 1)
                for k in range(2):
                    for n, j in enumerate(layer["ff2"]):
                        half, i = divmod(n, 2)
                        part = [v[:, :, half * 512:(half + 1) * 512] for v in w]
                        mm = split_b(psum[j.bank][:, :], part, k, 2 * h + k, i, (hid_hi, hid_lo), False, h == 15 and k == 1)
                        if h == 15 and k == 1:
                            mm.then_inc(bank_full[j.bank], 1)
                if h % 2 and h // 2 < FF2_SIGNALS:
                    mm.then_inc(ff2_chunk, 1)

    @block.scalar
    def _(act):
        steps = Steps()

        def then(ins):
            ins.then_inc(act_step, 1)
            act.wait_ge(act_step, steps.next())

        def full(j, turn=0):
            act.wait_ge(bank_full[j.bank], j.count(turn))

        def copy(j, out, scale=1.0, turn=0, cols=512):
            full(j, turn)
            act.activation(out, psum[j.bank][:, 0:cols], ACT.Copy, scale=scale).then_inc(bank_read[j.bank], 1)

        def squares():
            for i in range(TT):
                act.activation(xn[:, i, :], x[:, i, :], ACT.Square, accum_out=sumsq[:, i:i + 1]).then_inc(sumsq_ready, 1)

        flat = lambda v: v.rearrange("p a b -> p (a b)")

        act.wait_ge(x_loaded, 16)
        squares()
        act.wait_ge(params_loaded, 64)
        for n, j in enumerate(pre["c"]):
            copy(j, flat(c_raw[:, 2 * n:2 * n + 2, :]))
        act.wait_ge(angle_ready, 1)
        act.activation(rope_mem[:, :], rope_mem[:, :], ACT.Sin).then_inc(rope_ready, 1)
        for i, j in enumerate(pre["vm"]):
            copy(j, v_m[:, i, :])
        act.wait_ge(conv_ready, 4)
        act.activation(flat(c_raw), flat(c_act), ACT.Sigmoid).then_inc(conv_sig, 1)
        for n, j in enumerate(pre["z"]):
            full(j)
            act.activation(flat(sig_z[:, 2 * n:2 * n + 2, :]), psum[j.bank][:, :], ACT.Sigmoid).then_inc(bank_read[j.bank], 1)
        for h, j in enumerate(pre["rel"]):
            copy(j, rel_row[:, h, :], cols=384)
        for name, dst in (("mq", m_q), ("mk", m_k), ("vmt", v_mT)):
            for n, j in enumerate(pre[name]):
                copy(j, flat(dst[:, 2 * n:2 * n + 2, :]))
        for n, j in enumerate(pre["qd"]):
            copy(j, flat(q_d[:, 2 * n:2 * n + 2, :]), scale=DA_QD ** -0.5)
        for n, j in enumerate(pre["kd"]):
            copy(j, flat(k_d[:, 2 * n:2 * n + 2, :]))
        act.wait_ge(gates_pre, 1)
        lse3 = lse.rearrange("p (i n) -> p i n", i=2)
        then(act.activation(lse3, gate_pre[:, :, 4:8], ACT.Abs))
        then(act.activation(lse, lse, ACT.Exp, scale=-1.0))
        act.activation(lse, lse, ACT.Ln, bias=C("one")).then_inc(lse_ready, 1)
        for i, j in enumerate(pre["vd"]):
            copy(j, v_d[:, i, :])
        act.wait_ge(lam_dots, 1)
        act.activation(lam_two, lam_two, ACT.Exp).then_inc(lam_exp, 1)

        def m_exp(h):
            act.wait_ge(m_neg_ready, h + 1)
            act.activation(w_m[:, h, 0:P], w_m[:, h, 0:P], ACT.Exp, bias=m_neg[:, h:h + 1])
            act.activation(w_m[:, h, P:384], w_m[:, h, P:384], ACT.Exp, bias=m_neg[:, 4 + h:5 + h]).then_inc(m_exp_ready, 1)

        def d_exp(n):
            act.wait_ge(d_neg_ready, n + 1)
            act.activation(p_d[:, n, 0:P], p_d[:, n, 0:P], ACT.Exp, bias=d_neg[:, 2 * n:2 * n + 1],
                           accum_out=d_sum[:, 2 * n:2 * n + 1])
            act.activation(p_d[:, n, P:384], p_d[:, n, P:384], ACT.Exp, bias=d_neg[:, 2 * n + 1:2 * n + 2],
                           accum_out=d_sum[:, 2 * n + 1:2 * n + 2]).then_inc(d_exp_ready, 1)

        for h in range(ML_HEADS):
            m_exp(h)
        act.wait_ge(m_dec_in, 1)
        act.activation(m_dec, m_dec, ACT.Exp).then_inc(m_dec_out, 1)
        for n in range(2 * DA_HEADS):
            d_exp(n)
            if n % 2:
                copy(pre["wt"][n // 2], w_mT[:, n // 2, :], cols=384)
        act.wait_ge(centred, 1)
        act.activation(flat(square), flat(h_m), ACT.Square).then_inc(squared, 1)
        for h, j in enumerate(pre["at"]):
            copy(j, a_T[:, h, :], cols=384)
        act.wait_ge(var8_ready, 1)
        for i, j in enumerate(pre["pv"]):
            full(j)
            act.activation(square[:, i, :], psum[j.bank][:, :], ACT.Square).then_inc(squared, 1)
            copy(j, y_d[:, i, :])
        for j in pre["out"]:
            act.wait_ge(bank_read[j.bank], j.count())
        squares()
        for i in range(TT):
            act.wait_ge(r_neg, i + 1)
            act.activation(pick0[:, i, 0:4], logits[:, i, 0:4], ACT.Exp, bias=r_stat[:, 0, i:i + 1],
                           accum_out=r_stat[:, 1, i:i + 1]).then_inc(r_exp, 1)
        for i in range(TT):
            act.wait_ge(top_diff, i + 1)
            act.activation(r_stat[:, 2, i:i + 1], r_stat[:, 2, i:i + 1], ACT.Exp).then_inc(top_exp, 1)
        def experts(r, at):
            for step, pair in MOE_STEPS:
                if step not in ("turn", "gate", "flip", "down"):
                    continue
                for n, j in enumerate(r[step, pair]):
                    got = psum[j.bank]
                    act.wait_ge(r.bank_full[j.bank], j.count(at))
                    if step == "gate":
                        act.activation(hid_b[:, pair, :], got[:, :], ACT.Sigmoid).then_inc(r.sig_ready, 1)
                        continue
                    if step == "turn":
                        ins = act.activation(spread_w[:, pair, :], got[:, 0:S], ACT.Copy)
                    elif step == "flip":
                        ins = act.activation(hid_t[:, pair].rearrange("p f s -> p (f s)"), got[:, :], ACT.Copy)
                    else:
                        ins = act.activation(y_b[:, pair, n * 512:(n + 1) * 512], got[:, :], ACT.Copy)
                    ins.then_inc(r.bank_read[j.bank], 1)

        with act.Fori(0, MOE_TURNS) as turn:
            experts(first_pass, turn)
        act.wait_ge(crowded_ready, 1)
        with act.If(act.value_load(crowded[0:1, :], min_val=0, max_val=1) > 0):
            with act.Fori(0, PASSES - 1) as again:
                with act.Fori(0, MOE_TURNS) as turn:
                    experts(more_passes, again * MOE_TURNS + turn)
        act.end_ifs()
        act.wait_ge(moe_done, 1)
        squares()
        with act.Fori(0, LAYERS) as l:
            steps.enter(l, ACT_STEPS)
            act.wait_ge(x_ready, l + 1)
            squares()
            act.wait_ge(params2_loaded, 16 * l + 16)

            def split_hi(h):
                if h >= HALVES:
                    return
                c, w, hi, lo = weight_half(h)
                if h % 2 == 0:
                    act.wait_ge(w_landed[c % RING], layer_landed(c, l))
                ahead, first = (2, 0) if h < LATE else (AHEAD, LATE)
                if h - first >= ahead:
                    act.wait_ge(half_used, HALVES * l + (h - ahead + 1))
                act.activation(hi, w, ACT.Copy).then_inc(hi_ready, 1)

            def high_x(jobs, gain):
                for n, j in enumerate(jobs):
                    full(j, l)
                    for t in range(2):
                        dt = 2 * n + t
                        ins = act.activation(h_hi[:, dt, :], psum[j.bank][:, t * S:(t + 1) * S], ACT.Copy, scale=gain[:, dt:dt + 1])
                    ins.then_inc(h2_hi_ready, 1)

            split_hi(0)
            high_x(layer["ht"], at2["norm_mix"])
            split_hi(1)

            def next_hi(h):
                if h + 2 < LATE:
                    split_hi(h + 2)

            def fill(name, n):
                next_hi(filler_half[name, n])
                j = layer[name][n]
                pair = slice(2 * n, 2 * n + 2)
                if name == "gates":
                    full(j, l)
                    for t in range(2):
                        ins = act.activation(gates[:, 2 * n + t, :], psum[j.bank][:, t * S:(t + 1) * S], ACT.Identity,
                                             bias=at2["b_gate"][:, 2 * n + t:2 * n + t + 1])
                    ins.then_inc(bank_read[j.bank], 1)
                elif name in ("sb_v", "fox_v", "gla_v", "gla_g"):
                    full(j, l)
                    dst = {"sb_v": v_s, "fox_v": v_f, "gla_v": v_g, "gla_g": g_g}[name][:, :, n * S:(n + 1) * S]
                    act.activation(dst, psum[j.bank][:, :].rearrange("p (i c) -> p i c", i=TT), ACT.Copy).then_inc(bank_read[j.bank], 1)
                elif name == "gla_qk":
                    copy(j, flat((q_g, k_g)[n]), scale=(GLA_DK ** -0.5, 1.0)[n], turn=l)
                else:
                    copy(j, flat({"sb_q": q_s, "sb_k": k_s, "fox_q": q_f, "fox_k": k_f}[name][:, pair, :]),
                         scale=HD ** -0.5 if name[-1] == "q" else 1.0, turn=l)

            for n, j in enumerate(layer["nsa_q"]):
                next_hi(n)
                copy(j, flat(q_n[:, 2 * n:2 * n + 2, :]), scale=HD ** -0.5, turn=l)
            next_hi(2)
            copy(layer["nsa_k"][0], flat(kv_c), turn=l)
            next_hi(3)
            copy(layer["nsa_k"][1], flat(k_sw), turn=l)
            next_hi(4)
            copy(layer["nsa_v"][0], flat(v_n), turn=l)
            copy(layer["nsa_f"][0], flat(fg), turn=l, cols=64)
            j = layer["gla_a"][0]
            full(j, l)
            act.activation(a_low, psum[j.bank][0:GLA_RANK, 0:S], ACT.Copy).then_inc(bank_read[j.bank], 1)
            next_hi(5)
            j = layer["nsa_f"][0]
            act.wait_ge(bank_read[j.bank], j.count(l))
            act.activation(fg[:, :, 8:32], fg[:, :, 8:32], ACT.Sigmoid).then_inc(nsa_gate_ready, 1)
            for n, j in enumerate(layer["hid"]):
                full(j, l)
                act.activation(hid_c[:, n].rearrange("p a b -> p (a b)"), psum[j.bank][:, 0:4 * N_CMP], ACT.Copy).then_inc(bank_read[j.bank], 1)
            act.wait_ge(gelu_in, l + 1)
            act.activation(gelu_tmp, gelu_tmp, ACT.Sigmoid, scale=2.0 * float(np.sqrt(2.0 / np.pi))).then_inc(gelu_sig, 1)
            j = layer["kc"][0]
            full(j, l)
            act.activation(k_cT, psum[j.bank][:, 0:N_CMP], ACT.Copy).then_inc(bank_read[j.bank], 1)
            j = layer["vc"][0]
            full(j, l)
            act.activation(v_c, psum[j.bank][0:N_CMP, 0:P], ACT.Copy).then_inc(bank_read[j.bank], 1)
            act.wait_ge(fox_sum, l + 1)
            then(act.activation(lse_fox, lf_fox, ACT.Abs))
            then(act.activation(lse_fox, lse_fox, ACT.Exp, scale=-1.0))
            act.activation(lse_fox, lse_fox, ACT.Ln, bias=C("one")).then_inc(fox_lse, 1)
            j = layer["gla_la"][0]
            act.wait_ge(bank_read[j.bank], j.count(l))
            then(act.activation(flat(la_l), flat(la_m), ACT.Abs))
            then(act.activation(flat(la_l), flat(la_l), ACT.Exp, scale=-1.0))
            act.activation(flat(la_l), flat(la_l), ACT.Ln, bias=C("one")).then_inc(la_ready, 1)
            act.wait_ge(c_in, l + 1)
            act.activation(p_c, p_c, ACT.Exp).then_inc(c_exp, 1)
            for n, j in enumerate(layer["ct"]):
                full(j, l)
                act.activation(flat(pc_T[0:N_CMP, 2 * n:2 * n + 2, :]), psum[j.bank][0:N_CMP, :], ACT.Copy).then_inc(bank_read[j.bank], 1)

            def soft_exp(n, k):
                act.wait_ge(s_neg_ready, SOFTMAXES * l + k + 1)
                for i, cols in enumerate((slice(0, P), slice(P, 384))):
                    at = 2 * (k % NSA_N) + i
                    ins = act.activation(p_s[:, n, cols], p_s[:, n, cols], ACT.Exp, bias=s_neg[:, at:at + 1],
                                         accum_out=s_sum[:, at:at + 1])
                ins.then_inc(s_exp_ready, 1)

            for kind, n in nsa_steps():
                if kind == "fill":
                    fill(*n)
                elif kind == "score":
                    soft_exp(n % 8, n)
                elif kind == "turn":
                    copy(layer["nsa", kind, n][0], pT_s[:, n % 8, :], turn=l, cols=384)
            for kind, n in sb_steps():
                if kind == "fill":
                    fill(*n)
                    continue
                j = layer["sb", kind, n][0]
                if kind == "score":
                    full(j, l)
                    then(act.activation(p_s[:, n, :], psum[j.bank][:, 0:384], ACT.Abs))
                    then(act.activation(p_s[:, n, :], p_s[:, n, :], ACT.Exp, scale=-1.0))
                    act.activation(p_s[:, n, :], p_s[:, n, :], ACT.Ln, bias=C("one")).then_inc(sb_log, 1)
                elif kind == "again":
                    full(j, l)
                    act.activation(pT_s[:, n, :], psum[j.bank][:, 0:384], ACT.Exp).then_inc(bank_read[j.bank], 1)
            for kind, n in fox_steps():
                if kind == "fill":
                    fill(*n)
                elif kind == "score":
                    soft_exp(n, NSA_N + n)
                elif kind == "turn":
                    copy(layer["fox", kind, n][0], pT_s[:, n, :], turn=l, cols=384)

            def level(n):
                if n < len(GLA_LEVELS):
                    act.wait_ge(decay_in, 8 * l + n + 1)
                    dk = decay[:, n % 2].rearrange("p a b -> p (a b)")
                    then(act.activation(dk, dk, ACT.Abs))
                    act.activation(dk, dk, ACT.Exp, scale=-1.0 / GLA_TAU).then_inc(decay_out, 1)

            level(0)
            for kind, n in gla_steps():
                if kind == "fill":
                    fill(*n)
                else:
                    level(n + 1)
            for j in last_in_bank(layer["gla_g"] + layer["gates"]):
                act.wait_ge(bank_read[j.bank], j.count(l))
            act.activation(flat(sig_gg), flat(g_g), ACT.Sigmoid).then_inc(g_sig, 1)

            full(layer["gla", "level", len(GLA_LEVELS)][-1], l)
            for n, mixer in enumerate(("nsa", "sb", "fox")):
                j = layer[mixer, "value", 3][0]
                act.wait_ge(bank_read[j.bank], j.count(l))
                act.activation(y_hi[:, 4 * n:4 * n + 4, :], yT_all[:, 4 * n:4 * n + 4, :], ACT.Copy).then_inc(y_hi_ready, 1)
            for i, j in enumerate(layer["gla_o"]):
                full(j, l)
                act.activation(square_g[:, i, :], psum[j.bank][:, :], ACT.Square).then_inc(squared, 1)
                copy(j, o_g[:, i, :], turn=l)

            def gate_sigmoid(n):
                if n < 8:
                    act.activation(flat(gates[:, 4 * n:4 * n + 4, :]), flat(gates[:, 4 * n:4 * n + 4, :]), ACT.Sigmoid).then_inc(gate_sig, 1)

            split_hi(LATE + 0)
            gate_sigmoid(0)
            act.wait_ge(var8_ready, l + 3)
            split_hi(LATE + 1)
            act.wait_ge(y_gla, l + 1)
            split_hi(LATE + 2)
            gate_sigmoid(1)
            for i, j in enumerate(layer["gla_t"]):
                full(j, l)
                act.activation(y_hi[:, 12:16, i * P:(i + 1) * P],
                               psum[j.bank][:, :].rearrange("p (h t) -> p h t", h=4), ACT.Copy).then_inc(y_hi_ready, 1)
            for h in range(12):
                split_hi(LATE + h + AHEAD)
                gate_sigmoid(h + 2)
            for j in last_in_bank(layer["out"]):
                act.wait_ge(bank_read[j.bank], j.count(l))
            squares()
            high_x(layer["h2"], at2["norm_ff"])
            for n, j in enumerate(layer["ff1"]):
                split_hi(LATE + 12 + n + AHEAD)
                full(j, l)
                act.activation(flat(hid_ff[:, 2 * n:2 * n + 2, :]), psum[j.bank][:, :], ACT.Relu).then_inc(bank_read[j.bank], 1)
            for h in range(LATE + 28, HALVES - AHEAD):
                split_hi(h + AHEAD)
            steps.leave(LAYERS)
        act.wait_ge(x_ready, LAYERS + 1)
        squares()

    @block.gpsimd
    def _(pool):
        def rsqrt_x(value):
            pool.wait_ge(var_ready, value)
            pool.tensor_tensor(rstd, var, C("neghalf")[:, 0:TT], ALU.pow).then_inc(rstd_ready, 1)

        pool.wait_ge(const_loaded, 16)
        rsqrt_x(1)
        for n in range(2):
            pool.wait_ge(var8_ready, n + 1)
            pool.tensor_tensor(rstd8, var8, C("neghalf"), ALU.pow).then_inc(rstd8_ready, 1)
        rsqrt_x(2)
        rsqrt_x(3)
        with pool.Fori(0, LAYERS) as l:
            rsqrt_x(2 * l + 4)

            def scale(n, k):
                pool.wait_ge(s_inv_ready, SOFTMAXES * l + k + 1)
                for i, cols in enumerate((slice(0, P), slice(P, 384))):
                    at = 2 * (k % NSA_N) + i
                    part = p_s[:, n, cols]
                    ins = pool.tensor_tensor(part, part, s_inv[:, at:at + 1].to_broadcast([P, part.shape[-1]]), ALU.mult)
                ins.then_inc(p_scaled, 1)

            for n in range(NSA_N):
                scale(n % 8, n)
            for n in range(FOX_N):
                scale(n, NSA_N + n)
            pool.wait_ge(var8_ready, l + 3)
            pool.tensor_tensor(rstd8, var8, C("neghalf"), ALU.pow).then_inc(rstd8_ready, 1)
            rsqrt_x(2 * l + 5)
        rsqrt_x(2 * LAYERS + 4)

    @block.vector
    def _(dve):
        steps = Steps()

        def then(ins):
            ins.then_inc(dve_step, 1)
            dve.wait_ge(dve_step, steps.next())

        def full(j, turn=0):
            dve.wait_ge(bank_full[j.bank], j.count(turn))

        def norm_x(n, to=xn):
            dve.wait_ge(sumsq_ready, n * 2)
            dve.tensor_scalar(var, sumsq, 1.0 / D, EPS, ALU.mult, ALU.add).then_inc(var_ready, 1)
            dve.wait_ge(rstd_ready, n)
            for i in range(TT):
                dve.tensor_scalar(to[:, i, :], x[:, i, :], rstd[:, i:i + 1], None, ALU.mult).then_inc(xn_ready, 1)

        def gain_x(jobs, gain, turn=0):
            for n, j in enumerate(jobs):
                full(j, turn)
                for t in range(2):
                    dt = 2 * n + t
                    ins = dve.tensor_scalar(hT[:, dt, :], psum[j.bank][:, t * S:(t + 1) * S], gain[:, dt:dt + 1],
                                            None, ALU.mult)
                ins.then_inc(bank_read[j.bank], 1)

        def add_x(jobs, turn=0, first_half=0):
            for n, j in enumerate(jobs):
                half, i = first_half + n // 2, n % 2
                xs = x[:, i, half * 512:(half + 1) * 512]
                full(j, turn)
                dve.tensor_tensor(xs, psum[j.bank][:, :], xs, ALU.add).then_inc(bank_read[j.bank], 1)

        def by_head(v):
            return v.rearrange("p (n o) -> p n o", o=1).to_broadcast([P, 8, P])

        heads8 = lambda v: v.rearrange("p i (h e) -> p (i h) e", e=P)

        dve.wait_ge(x_loaded, 16)
        norm_x(1)
        dve.wait_ge(params_loaded, 64)
        gain_x(pre["ht"], at1["norm1"])
        dve.wait_ge(pos_loaded, 16)
        dve.wait_ge(const_loaded, 16)
        then(dve.tensor_copy(ang, pos_i))
        then(dve.tensor_scalar(ang, ang, C("inv"), None, ALU.mult))
        then(dve.tensor_scalar(turns, ang, 1.0 / TWO_PI, ROUND, ALU.mult, ALU.add))
        then(dve.tensor_scalar(turns, turns, -ROUND, None, ALU.add))
        for part in TWO_PI_PARTS:
            then(dve.scalar_tensor_tensor(ang, turns, -part, ang, ALU.mult, ALU.add))
        then(dve.tensor_scalar(sin_t, ang, PI_F, -PI_F, ALU.min, ALU.max))
        then(dve.tensor_scalar(ang, ang, 0.5 * np.pi, None, ALU.add))
        then(dve.tensor_scalar(turns, ang, PI_F, -TWO_PI, ALU.is_gt, ALU.mult))
        then(dve.tensor_tensor(ang, ang, turns, ALU.add))
        dve.tensor_scalar(cos_t, ang, PI_F, -PI_F, ALU.min, ALU.max).then_inc(angle_ready, 1)
        lam_mult = view(p_mem, 0, 2, DA_QD)
        then(dve.tensor_tensor(lam_mult, lam_in[:, 0::2, :], lam_in[:, 1::2, :], ALU.mult))
        dve.tensor_reduce(lam_two, lam_mult, AX.X, ALU.add).then_inc(lam_dots, 1)
        for j in pre["c"]:
            dve.wait_ge(bank_read[j.bank], j.count())
        for w in range(CONV_W - 1, -1, -1):
            back = CONV_W - 1 - w
            for f in range(4):
                if back == 0:
                    ins = dve.tensor_scalar(c_act[:, f, :], c_raw[:, f, :], conv_w[:, f, w:w + 1],
                                            at1["conv_b"][:, f:f + 1], ALU.mult, ALU.add)
                else:
                    ins = dve.scalar_tensor_tensor(c_act[:, f, back:], c_raw[:, f, 0:S - back], conv_w[:, f, w:w + 1],
                                                   c_act[:, f, back:], ALU.mult, ALU.add)
                if w:
                    if f == 3:
                        then(ins)
                else:
                    ins.then_inc(conv_ready, 1)
        dve.wait_ge(conv_sig, 1)
        for f in range(4):
            dve.tensor_tensor(c_act[:, f, :], c_act[:, f, :], c_raw[:, f, :], ALU.mult).then_inc(act_ready, 1)
        dve.wait_ge(act_ready, 4)
        for f in range(4):
            dve.tensor_scalar(skip_c[:, f, :], c_act[:, f, :], at1["m_skip"][:, f:f + 1], None, ALU.mult)
        j = pre["gate"][0]
        full(j)
        b_gate = at1["b_gate"].rearrange("p (o n) -> p o n", o=1).to_broadcast([P, TT, 8])
        dve.tensor_tensor(gate_pre, psum[j.bank][:, 0:16].rearrange("p (i n) -> p i n", i=2), b_gate,
                          ALU.add).then_inc(bank_read[j.bank], 1)
        dve.wait_ge(bank_read[j.bank], j.count())
        lf = log_f.rearrange("p (i n) -> p i n", i=2)
        dve.tensor_scalar(lf, gate_pre[:, :, 4:8], 0.0, None, ALU.min).then_inc(gates_pre, 1)
        dve.wait_ge(gates_pre, 1)
        dve.wait_ge(lse_ready, 1)
        dve.tensor_tensor(log_f, log_f, lse, ALU.subtract).then_inc(logf_ready, 1)
        dve.wait_ge(lam_exp, 1)
        dve.tensor_scalar(lam, lam_two[:, 0:1], lam_two[:, 1:2], LAM_INIT, ALU.subtract, ALU.add)
        dve.wait_ge(rel_loaded, 16)
        then(dve.tensor_tensor(rel_bias[:, :, P:S], rel_bias[:, :, P:S],
                               negmask[:, 0:P].rearrange("p (o n) -> p o n", o=1).to_broadcast([P, 4, P]), ALU.add))
        j = pre["negb"][0]
        full(j)
        dve.tensor_copy(neg_b, psum[j.bank][:, 0:8]).then_inc(bank_read[j.bank], 1)

        def m_weights(h):
            dve.wait_ge(m_exp_ready, h + 1)
            j = pre["qk"][h]
            full(j)
            for i, cols in enumerate((slice(0, P), slice(P, 384))):
                ins = dve.tensor_tensor_reduce(w_m[:, h, cols], w_m[:, h, cols], psum[j.bank][:, cols], ML_HD ** -0.5,
                                               0.0, ALU.mult, ALU.add, m_den[:, 4 * i + h:4 * i + h + 1])
            ins.then_inc(bank_read[j.bank], 1)

        for h in range(ML_HEADS):
            j = pre["u"][h]
            full(j)
            dve.tensor_tensor_reduce(w_m[:, h, 0:P], psum[j.bank][:, 0:P], negmask[:, 0:P], 1.0, -BIG,
                                     ALU.add, ALU.max, m_max[:, h:h + 1])
            dve.tensor_tensor_reduce(w_m[:, h, P:384], psum[j.bank][:, 0:S], negmask[:, P:384], 1.0, -BIG,
                                     ALU.add, ALU.max, m_max[:, 4 + h:5 + h]).then_inc(bank_read[j.bank], 1)
            dve.wait_ge(bank_read[j.bank], j.count())
            dve.tensor_scalar(m_neg[:, h::4], m_max[:, h::4], 0.0, -1.0, ALU.max, ALU.mult).then_inc(m_neg_ready, 1)
            if h:
                m_weights(h - 1)
        m_weights(ML_HEADS - 1)
        dve.wait_ge(m_neg_ready, ML_HEADS)
        j = pre["negb"][0]
        dve.wait_ge(bank_read[j.bank], j.count())
        dve.tensor_tensor(m_dec, m_neg, neg_b, ALU.add).then_inc(m_dec_in, 1)

        def d_scores(n):
            j = pre["s"][n]
            full(j)
            dve.tensor_tensor_reduce(p_d[:, n, 0:P], psum[j.bank][:, 0:P], rel_bias[:, n // 2, P:S], 1.0, -BIG,
                                     ALU.add, ALU.max, d_max[:, 2 * n:2 * n + 1])
            dve.tensor_tensor_reduce(p_d[:, n, P:384], psum[j.bank][:, P:384], rel_bias[:, n // 2, :], 1.0, -BIG,
                                     ALU.add, ALU.max, d_max[:, 2 * n + 1:2 * n + 2]).then_inc(bank_read[j.bank], 1)
            dve.wait_ge(bank_read[j.bank], j.count())
            dve.tensor_scalar(d_neg[:, 2 * n:2 * n + 2], d_max[:, 2 * n:2 * n + 2], -1.0, None,
                              ALU.mult).then_inc(d_neg_ready, 1)

        def d_mix(h):
            dve.wait_ge(d_exp_ready, 2 * h + 2)
            inv = d_inv[:, 4 * h:4 * h + 4]
            then(dve.reciprocal(inv, d_sum[:, 4 * h:4 * h + 4]))
            then(dve.tensor_scalar(inv[:, 2:4], inv[:, 2:4], lam, None, ALU.mult))
            halves = (slice(0, P), slice(P, 384))
            for i, cols in enumerate(halves):
                ins = dve.tensor_scalar(p_d[:, 2 * h + 1, cols], p_d[:, 2 * h + 1, cols], inv[:, 2 + i:3 + i], None, ALU.mult)
            then(ins)
            for i, cols in enumerate(halves):
                ins = dve.scalar_tensor_tensor(p_d[:, 2 * h, cols], p_d[:, 2 * h, cols], inv[:, i:i + 1],
                                               p_d[:, 2 * h + 1, cols], ALU.mult, ALU.subtract)
            ins.then_inc(a_ready, 1)

        for n in range(2 * DA_HEADS):
            d_scores(n)
            if n == 1:
                dve.wait_ge(m_dec_out, 1)
                then(dve.scalar_tensor_tensor(m_abs, m_den, -1.0, m_den, ALU.mult, ALU.max))
                then(dve.tensor_tensor(m_abs, m_abs, m_dec, ALU.max))
                then(dve.reciprocal(m_abs, m_abs))
            if n % 2 and n > 1:
                d_mix(n // 2 - 1)
        for i, j in enumerate(pre["num"]):
            full(j)
            inv = m_abs[:, 4 * i:4 * i + 4].rearrange("p (n o) -> p n o", o=1).to_broadcast([P, 4, P])
            dve.tensor_tensor(h_m[:, i, :].rearrange("p (h e) -> p h e", e=P),
                              psum[j.bank][:, :].rearrange("p (h e) -> p h e", e=P), inv, ALU.mult).then_inc(bank_read[j.bank], 1)
        for j in pre["num"]:
            dve.wait_ge(bank_read[j.bank], j.count())
        then(dve.tensor_reduce(mean, heads8(h_m), AX.X, ALU.add))
        then(dve.tensor_scalar(mean, mean, -1.0 / ML_HD, None, ALU.mult))
        dve.tensor_tensor(heads8(h_m), heads8(h_m), by_head(mean), ALU.add).then_inc(centred, 1)
        d_mix(DA_HEADS - 1)

        def head_rms(n, values, eps, signal):
            dve.wait_ge(squared, (1, 3)[n])
            then(dve.tensor_reduce(mean, heads8(square), AX.X, ALU.add))
            dve.tensor_scalar(var8, mean, 1.0 / P, eps, ALU.mult, ALU.add).then_inc(var8_ready, 1)
            dve.wait_ge(rstd8_ready, n + 1)
            dve.tensor_tensor(heads8(values), heads8(values), by_head(rstd8), ALU.mult).then_inc(signal, 1)

        head_rms(0, h_m, EPS, head_norm)
        for j in pre["pv"]:
            dve.wait_ge(bank_read[j.bank], j.count())
        head_rms(1, y_d, SUBLN_EPS, head_norm)
        for i, j in enumerate(pre["hnt"]):
            cols = slice(i * P, (i + 1) * P)
            full(j)
            for f in range(4):
                ins = dve.scalar_tensor_tensor(y_T[:, f, cols], psum[j.bank][:, f * P:(f + 1) * P],
                                               at1["m_norm"][:, f:f + 1], skip_c[:, f, cols], ALU.mult, ALU.add)
            ins.then_inc(bank_read[j.bank], 1)
            dve.wait_ge(bank_read[j.bank], j.count())
            dve.tensor_tensor(y_T[:, 0:4, cols], y_T[:, 0:4, cols], sig_z[:, :, cols], ALU.mult).then_inc(ym_ready, 1)
        for i, j in enumerate(pre["ydt"]):
            full(j)
            dve.tensor_scalar(y_T[:, 4:8, i * P:(i + 1) * P], psum[j.bank][:, :].rearrange("p (h t) -> p h t", h=4),
                              at1["da_norm"], 1.0 - LAM_INIT, ALU.mult, ALU.mult).then_inc(bank_read[j.bank], 1)
        add_x(pre["out"])
        norm_x(2)
        gain_x(pre["h2"], at1["norm2"])

        j = pre["router"][0]
        full(j)
        b_r = at1["b_r"].rearrange("p (o n) -> p o n", o=1).to_broadcast([P, TT, 36])
        dve.memset(group8, -BIG)
        dve.tensor_tensor(logits, psum[j.bank][:, 0:72].rearrange("p (i n) -> p i n", i=2), b_r,
                          ALU.add).then_inc(bank_read[j.bank], 1)
        dve.wait_ge(bank_read[j.bank], j.count())
        then(dve.tensor_copy(group8[:, :, 0:4], logits[:, :, 0:4]))
        iota8 = C("iota")[:, 0:EXP_PER_GROUP]
        for i in range(TT):
            found = index8[:, 8 * i:8 * i + 8]
            then(dve.max(top8[:, i, :], group8[:, i, :]))
            dve.tensor_scalar(r_stat[:, 0, i:i + 1], top8[:, i, 0:1], -1.0, None, ALU.mult).then_inc(r_neg, 1)
            then(dve.max_index(found, top8[:, i, :], group8[:, i, :]))
            then(dve.tensor_copy(idx_f[:, i, 0:1], found[:, 0:1]))
            then(dve.tensor_scalar(one_g[:, i, :], iota8, idx_f[:, i, 0:1], None, ALU.is_equal))
            for g in range(N_GROUPS):
                le = logits[:, i, 4 + 8 * g:12 + 8 * g]
                if g == 0:
                    then(dve.tensor_scalar(le8[:, i, :], le, one_g[:, i, 0:1], None, ALU.mult))
                else:
                    then(dve.scalar_tensor_tensor(le8[:, i, :], le, one_g[:, i, g:g + 1], le8[:, i, :], ALU.mult, ALU.add))
            then(dve.max(top8[:, i, :], le8[:, i, :]))
            dve.tensor_tensor(r_stat[:, 2, i:i + 1], top8[:, i, 1:2], top8[:, i, 0:1], ALU.subtract).then_inc(top_diff, 1)
            then(dve.max_index(found, top8[:, i, :], le8[:, i, :]))
            then(dve.tensor_copy(idx_f[:, i, 0:2], found[:, 0:2]))
        for i in range(TT):
            dve.wait_ge(r_exp, i + 1)
            dve.wait_ge(top_exp, i + 1)
            then(dve.tensor_scalar(r_stat[:, 3, i:i + 1], r_stat[:, 2, i:i + 1], 1.0, r_stat[:, 1, i:i + 1], ALU.add, ALU.mult))
            then(dve.reciprocal(r_stat[:, 3, i:i + 1], r_stat[:, 3, i:i + 1]))
            then(dve.tensor_tensor(r_stat[:, 4, i:i + 1], r_stat[:, 3, i:i + 1], r_stat[:, 2, i:i + 1], ALU.mult))
            then(dve.tensor_scalar(pick1[:, i, :], iota8, idx_f[:, i, 1:2], r_stat[:, 4, i:i + 1], ALU.is_equal, ALU.mult))
            then(dve.tensor_scalar(pick0[:, i, :], iota8, idx_f[:, i, 0:1], r_stat[:, 3, i:i + 1], ALU.is_equal, ALU.mult))
            then(dve.tensor_tensor(pick0[:, i, :], pick0[:, i, :], pick1[:, i, :], ALU.add))
            for g in range(N_GROUPS):
                then(dve.tensor_scalar(gates_moe[:, i, 8 * g:8 * g + 8], pick0[:, i, :], one_g[:, i, g:g + 1], None, ALU.mult))
        dve.memset(gates_moe[:, :, N_EXPERTS:], 0.0)
        dve.memset(rank[:, :, N_EXPERTS:], FAR)
        dve.tensor_scalar(member, gates_moe[:, :, 0:N_EXPERTS], 0.0, None, ALU.is_gt).then_inc(member_ready, 1)
        dve.wait_ge(member_ready, 1)
        j = pre["rank"][0]
        full(j)
        n = N_EXPERTS
        then(dve.tensor_scalar(member, member, -FAR, FAR, ALU.mult, ALU.add))
        then(dve.tensor_reduce(most, psum[j.bank][:, 2 * n:3 * n], AX.X, ALU.max))
        dve.tensor_scalar(crowded, most, CAP, None, ALU.is_gt).then_inc(crowded_ready, 1)
        dve.tensor_tensor(rank[:, :, 0:n], psum[j.bank][:, 0:2 * n].rearrange("p (i e) -> p i e", i=TT), member,
                          ALU.add).then_inc(bank_read[j.bank], 1)
        dve.wait_ge(bank_read[j.bank], j.count())

        def slots(r, turn, made):
            shape = [P, TT, 2 * PAIRS, CAP]
            now = [v[:, :, bass.ds(turn * 2 * PAIRS, 2 * PAIRS)].rearrange("p i (e o) -> p i e o", o=1).to_broadcast(shape)
                   for v in (rank, gates_moe)]
            places = C("iota").rearrange("p (i e s) -> p i e s", i=1, e=1).to_broadcast(shape)
            dve.tensor_tensor(one_hot, places, now[0], ALU.is_equal).then_inc(r.hot_ready, 1)
            dve.wait_ge(r.hot_ready, made + 1)
            dve.tensor_tensor(weighted, one_hot, now[1], ALU.mult).then_inc(r.slots_ready, 1)

        def experts(r, turn, at, made):
            gain = at1["norm2"].rearrange("p (k o) -> p k o", o=1)
            for step, pair in MOE_STEPS:
                if step not in ("pick", "gate", "up", "spread"):
                    continue
                for n, j in enumerate(r[step, pair]):
                    got = psum[j.bank]
                    if step == "pick":
                        dve.wait_ge(r.bank_full[j.bank], j.count(at))
                        ins = dve.tensor_tensor(x_e[:, pair, 4 * n:4 * n + 4, :], got[:, :].rearrange("p (k s) -> p k s", k=4),
                                                gain[:, 4 * n:4 * n + 4, :].to_broadcast([P, 4, P]), ALU.mult)
                    elif step == "gate":
                        dve.wait_ge(r.sig_ready, at * PAIRS + pair + 1)
                        ins = dve.tensor_tensor(hid_b[:, pair, :], got[:, :], hid_b[:, pair, :], ALU.mult)
                    elif step == "up":
                        before = r["gate", pair][0]
                        dve.wait_ge(r.bank_read[before.bank], before.count(at))
                        dve.wait_ge(r.bank_full[j.bank], j.count(at))
                        ins = dve.tensor_tensor(hid_b[:, pair, :], got[:, :], hid_b[:, pair, :], ALU.mult)
                    else:
                        if pair == PAIRS - 1 and n == 0:
                            used = r["turn", pair][0]
                            dve.wait_ge(r.bank_full[used.bank], used.count(at))
                            dve.wait_ge(r.slots_ready, made + 1)
                            slots(r, turn + 1, made + 1)
                        half, i = divmod(n, 2)
                        xs = x[:, i, half * 512:(half + 1) * 512]
                        dve.wait_ge(r.bank_full[j.bank], j.count(at))
                        ins = dve.tensor_tensor(xs, got[:, :], xs, ALU.add)
                    ins.then_inc(r.bank_read[j.bank], 1)

        slots(first_pass, 0, 0)
        with dve.Fori(0, MOE_TURNS) as turn:
            experts(first_pass, turn, turn, turn)
        dve.wait_ge(first_pass.slots_ready, SLOTS_MADE)
        dve.wait_ge(crowded_ready, 1)
        with dve.If(dve.value_load(crowded[0:1, :], min_val=0, max_val=1) > 0):
            dve.memset(mark, 0.0).then_inc(more_passes.turn_done, 1)
            with dve.Fori(0, PASSES - 1) as again:
                dve.tensor_scalar(rank, rank, -float(CAP), None, ALU.add).then_inc(more_passes.rank_ready, 1)
                dve.wait_ge(more_passes.rank_ready, again + 1)
                slots(more_passes, 0, again * (MOE_TURNS + 1))
                with dve.Fori(0, MOE_TURNS) as turn:
                    experts(more_passes, turn, again * MOE_TURNS + turn, again * (MOE_TURNS + 1) + turn)
                    dve.memset(mark, 0.0).then_inc(more_passes.turn_done, 1)
                dve.wait_ge(more_passes.slots_ready, again * SLOTS_MADE + SLOTS_MADE)
            dve.wait_ge(more_passes.turn_done, MOE_TURNS * (PASSES - 1) + 1)
        dve.end_ifs()
        dve.memset(mark, 0.0).then_inc(moe_done, 1)
        norm_x(3)
        dve.wait_ge(xn_ready, 6)
        dve.wait_ge(gain_loaded, 16)
        for i in range(TT):
            ins = dve.tensor_tensor(x[:, i, :], xn[:, i, :], gain_row, ALU.mult)
        ins.then_inc(x_ready, 1)
        with dve.Fori(0, LAYERS) as l:
            steps.enter(l, DVE_STEPS)
            def split_lo(h):
                if h < HALVES:
                    c, w, hi, lo = weight_half(h)
                    dve.wait_ge(hi_ready, HALVES * l + h + 1)
                    dve.tensor_tensor(lo, w, hi, ALU.subtract).then_inc(lo_ready, 1)

            def low_x(jobs, gain, lo, before):
                for n, j in enumerate(jobs):
                    dve.wait_ge(h2_hi_ready, 8 * l + (before + n + 1))
                    for t in range(2):
                        dt = 2 * n + t
                        ins = dve.scalar_tensor_tensor(lo[:, dt, :], psum[j.bank][:, t * S:(t + 1) * S], gain[:, dt:dt + 1],
                                                       h_hi[:, dt, :], ALU.mult, ALU.subtract)
                    ins.then_inc(bank_read[j.bank], 1)

            def next_lo(h):
                if h + 1 < LATE:
                    split_lo(h + 1)

            norm_x(2 * l + 4, xn_a)
            split_lo(0)
            dve.wait_ge(params2_loaded, 16 * l + 16)
            low_x(layer["ht"], at2["norm_mix"], h_lo, 0)
            for h in range(6):
                next_lo(h)

            marks = iter(range(WAIT_MARKS))

            def apart():
                n = next(marks)
                dve.memset(wait_marks[:, n:n + 1], 0.0)

            def rotate(j, v, tmp, cos, sin):
                full(j, l)
                n = v.shape[-1]
                tiles = v.shape[1] if len(v.shape) == 3 else 1
                if tiles > 1:
                    cos, sin = (c.rearrange("p (o n) -> p o n", o=1).to_broadcast([P, tiles, n]) for c in (cos, sin))
                    swapped = psum[j.bank][:, 0:tiles * S].rearrange("p (a n) -> p a n", a=tiles)
                else:
                    swapped = psum[j.bank][:, 0:n]
                dve.tensor_tensor(tmp, swapped, sin, ALU.mult).then_inc(bank_read[j.bank], 1)
                then(dve.tensor_tensor(v, v, cos, ALU.mult))
                dve.wait_ge(bank_read[j.bank], j.count(l))
                dve.tensor_tensor(v, v, tmp, ALU.add).then_inc(roped, 1)

            j = layer["nsa_f"][0]
            dve.wait_ge(bank_read[j.bank], j.count(l))
            lf2 = lf_fox.rearrange("p (i n) -> p i n", i=2)
            dve.tensor_tensor(lf2, fg[:, :, 0:8], at2["fox_b"].rearrange("p (o n) -> p o n", o=1).to_broadcast([P, TT, 8]),
                              ALU.add).then_inc(fox_sum, 1)
            for n, j in enumerate(layer["rope_q"]):
                rotate(j, q_n[:, 2 * n:2 * n + 2, :], rope_tmp[:, 2 * n:2 * n + 2, :], cos_t, sin_t)
            rotate(layer["rope_k"][0], k_sw, rope_tmp[:, 4:6, :], cos_t, sin_t)
            even = lambda v, w: v.rearrange("p (b s w) -> p b s w", s=CMP_STRIDE // 2, w=2)[:, :, :, w]
            for n, j in enumerate(layer["dup"]):
                full(j, l)
                for late in range(2):
                    for w in range(2):
                        rows = slice(HD * w, HD * w + HD)
                        pe_ = at2["pe_" + "kv"[n]][rows, 16 * late:16 * late + 16:2]
                        ins = dve.tensor_tensor(even(dup[rows, 2 * n + late, :], 0), even(psum[j.bank][rows, :], w),
                                                pe_.rearrange("p (o s) -> p o s", o=1).to_broadcast([HD, 32, 8]), ALU.add)
                        ins.then_inc(dup_ready, 1)
                dve.wait_ge(dup_ready, 8 * l + 4 * n + 4)
                dve.memset(mark, 0.0).then_inc(bank_read[j.bank], 1)
            for j in last_in_bank(layer["hid"]):
                dve.wait_ge(bank_read[j.bank], j.count(l))
            hx = hid_c.rearrange("p a b c -> p (a b c)")
            then(dve.tensor_tensor(gelu_tmp, hx, hx, ALU.mult))
            then(dve.tensor_scalar(gelu_tmp, gelu_tmp, 0.044715, 1.0, ALU.mult, ALU.add))
            dve.tensor_tensor(gelu_tmp, gelu_tmp, hx, ALU.mult).then_inc(gelu_in, 1)
            dve.wait_ge(gelu_sig, l + 1)
            dve.tensor_tensor(hx, hx, gelu_tmp, ALU.mult).then_inc(hid_ready, 1)
            j = layer["kc"][0]
            dve.wait_ge(bank_read[j.bank], j.count(l))
            ends = slice(CMP_LEN - 1, S, CMP_STRIDE)
            rotate(layer["rope_c"][0], k_cT, rope_tmp_c, cos_t[:, ends], sin_t[:, ends])
            j = layer["gla_la"][0]
            full(j, l)
            for t in range(2):
                ins = dve.tensor_scalar(la_m[:, t, :], psum[j.bank][:, t * S:(t + 1) * S], at2["b_alpha"][:, t:t + 1], None, ALU.add)
            ins.then_inc(bank_read[j.bank], 1)
            cmask = C("cmpmask").rearrange("p (i o c) -> p i o c", i=TT, o=1).to_broadcast([P, TT, NSA_HPG, N_CMP])
            for r, j in enumerate(layer["cs"]):
                full(j, l)
                got = psum[j.bank][:, 0:TT * NSA_HPG * N_CMP].rearrange("p (i m c) -> p i m c", i=TT, m=NSA_HPG)
                dve.tensor_tensor(p_c.rearrange("p i (m r) c -> p i m r c", r=2)[:, :, :, r, :], got, cmask,
                                  ALU.add).then_inc(bank_read[j.bank], 1)
            for j in last_in_bank(layer["cs"]):
                dve.wait_ge(bank_read[j.bank], j.count(l))
            pc16 = p_c.rearrange("p i h c -> p (i h) c")
            wide16 = lambda v: v.rearrange("p (n o) -> p n o", o=1).to_broadcast([P, 16, N_CMP])
            then(dve.tensor_reduce(c_max, pc16, AX.X, ALU.max))
            dve.tensor_tensor(pc16, pc16, wide16(c_max), ALU.subtract).then_inc(c_in, 1)
            dve.wait_ge(fox_lse, l + 1)
            then(dve.tensor_scalar(lf_fox, lf_fox, 0.0, None, ALU.min))
            dve.tensor_tensor(lf_fox, lf_fox, lse_fox, ALU.subtract).then_inc(lf_ready, 1)
            dve.wait_ge(la_ready, l + 1)
            then(dve.tensor_scalar(la_m, la_m, 0.0, None, ALU.min))
            for t in range(2):
                ins = dve.tensor_tensor_scan(b_cum[:, t, :], la_m[:, t, :], la_l[:, t, :], 0.0, ALU.add, ALU.subtract)
            then(ins)
            dve.wait_ge(c_exp, l + 1)
            then(dve.tensor_reduce(c_inv, pc16, AX.X, ALU.add))
            then(dve.reciprocal(c_inv, c_inv))
            c_inv3 = c_inv.rearrange("p (i h) -> p i h", i=TT)
            then(dve.tensor_tensor(c_inv3, c_inv3, C("rowvalid").rearrange("p (i o) -> p i o", o=1).to_broadcast([P, TT, HEADS]), ALU.mult))
            dve.wait_ge(nsa_gate_ready, l + 1)
            c_inv4 = c_inv.rearrange("p (i m r) -> p i m r", i=TT, r=2)
            then(dve.tensor_tensor(c_inv4, c_inv4, nsa_gate[:, :, :, :, 0], ALU.mult))
            dve.tensor_tensor(pc16, pc16, wide16(c_inv), ALU.mult).then_inc(c_ready, 1)

            def soft_max(j, n, k):
                full(j, l)
                apart()
                at = 2 * (k % NSA_N)
                dve.tensor_tensor_reduce(p_s[:, n, 0:P], psum[j.bank][:, 0:P], negmask[:, 0:P], 1.0, -BIG,
                                         ALU.add, ALU.max, s_max[:, at:at + 1])
                dve.tensor_tensor_reduce(p_s[:, n, P:384], psum[j.bank][:, P:384], negmask[:, P:384], 1.0, -BIG,
                                         ALU.add, ALU.max, s_max[:, at + 1:at + 2]).then_inc(bank_read[j.bank], 1)
                dve.wait_ge(bank_read[j.bank], j.count(l))
                dve.tensor_scalar(s_neg[:, at:at + 2], s_max[:, at:at + 2], -1.0, None, ALU.mult).then_inc(s_neg_ready, 1)

            def soft_inverse(k, gate=None):
                at = 2 * (k % NSA_N)
                dve.wait_ge(s_exp_ready, SOFTMAXES * l + k + 1)
                if gate is None:
                    dve.reciprocal(s_inv[:, at:at + 2], s_sum[:, at:at + 2]).then_inc(s_inv_ready, 1)
                else:
                    then(dve.reciprocal(s_inv[:, at:at + 2], s_sum[:, at:at + 2]))
                    dve.tensor_tensor(s_inv[:, at:at + 2], s_inv[:, at:at + 2], gate, ALU.mult).then_inc(s_inv_ready, 1)

            def value(j, tile):
                full(j, l)
                dve.tensor_copy(yT_all[:, tile, :], psum[j.bank][:, 0:S]).then_inc(bank_read[j.bank], 1)

            gate_of = lambda n: nsa_gate[:, :, n // 4, n // 2 % 2, 1 + n % 2]
            for kind, n in nsa_steps():
                if kind == "fill":
                    next_lo(filler_half[n])
                elif kind == "score":
                    soft_max(layer["nsa", kind, n][0], n % 8, n)
                    if n:
                        soft_inverse(n - 1, gate_of(n - 1))
                elif kind == "turn" and n == NSA_N - NSA_LAG:
                    soft_inverse(NSA_N - 1, gate_of(NSA_N - 1))
                elif kind == "value":
                    value(layer["nsa", kind, n][0], n)
            for kind, n in sb_steps():
                if kind == "fill":
                    next_lo(filler_half[n])
                elif kind == "score":
                    j = layer["sb", kind, n][0]
                    dve.wait_ge(sb_log, 8 * l + n + 1)
                    dve.scalar_tensor_tensor(p_s[:, n, :], psum[j.bank][:, 0:384], 0.0, p_s[:, n, :], ALU.max,
                                             ALU.add).then_inc(bank_read[j.bank], 1)
                    dve.wait_ge(bank_read[j.bank], j.count(l))
                    diag = p_s[:, n, :].rearrange("p (b c) -> p b c", b=3)[:, 0::2, :]
                    dve.tensor_tensor(diag, diag, C("strict").rearrange("p (o n) -> p o n", o=1).to_broadcast([P, 2, P]),
                                      ALU.mult).then_inc(sb_ready, 1)
                elif kind == "value":
                    value(layer["sb", kind, n][0], 4 + n)
            for kind, n in fox_steps():
                if kind == "fill":
                    next_lo(filler_half[n])
                elif kind == "score":
                    soft_max(layer["fox", kind, n][0], n, NSA_N + n)
                    if n:
                        soft_inverse(NSA_N + n - 1)
                elif kind == "turn" and n == FOX_N - FOX_LAG:
                    soft_inverse(NSA_N + FOX_N - 1)
                elif kind == "value":
                    value(layer["fox", kind, n][0], 8 + n)
            for j in last_in_bank(layer["gla_qk"]):
                dve.wait_ge(bank_read[j.bank], j.count(l))
            then(dve.memset(att, 0.0))

            def level_decay(n):
                h = GLA_LEVELS[n]
                blocks = lambda v: v.rearrange("p a (b s) -> p (a b) s", s=2 * h)
                b = blocks(b_cum)
                if n >= 2:
                    dve.wait_ge(level_ready, 8 * l + n - 1)
                dve.tensor_tensor(blocks(decay[:, n % 2]), b, b[:, :, h - 1:h].to_broadcast([P, S // h, 2 * h]),
                                  ALU.subtract).then_inc(decay_in, 1)

            def level_read(n):
                for r, j in enumerate(layer["gla", "level", n]):
                    full(j, l)
                    got = psum[j.bank][:, :].rearrange("p (h t) -> p h t", h=4)
                    if n == 0:
                        ins = dve.tensor_copy(att_far[:, r], got[:, 0:2, :])
                    else:
                        before = layer["gla", "level", n - 1][r]
                        dve.wait_ge(bank_read[before.bank], before.count(l))
                        apart()
                        mask = C("gla")[:, (n - 1) * P:n * P] if n < len(GLA_LEVELS) else ident
                        mask = mask.bitcast(U32).rearrange("p (o t) -> p o t", o=1).to_broadcast([P, 4, P])
                        ins = dve.copy_predicated(att[:, r], mask, got)
                    ins.then_inc(bank_read[j.bank], 1)

            level_decay(0)
            for kind, n in gla_steps():
                if kind == "fill":
                    next_lo(filler_half[n])
                    continue
                if n + 1 < len(GLA_LEVELS):
                    level_decay(n + 1)
                if n < len(GLA_LEVELS):
                    dve.wait_ge(decay_out, 8 * l + n + 1)
                    dve.tensor_tensor(q_lv[:, n % 2], q_g, decay[:, n % 2], ALU.mult)
                    dve.tensor_tensor(k_lv[:, n % 2], k_g, decay[:, n % 2], ALU.mult).then_inc(level_ready, 1)
                if n:
                    level_read(n - 1)
            level_read(len(GLA_LEVELS))

            dve.wait_ge(g_sig, l + 1)
            then(dve.tensor_tensor(sig_gg, sig_gg, g_g, ALU.mult))
            then(dve.tensor_tensor(heads8(sig_gg), heads8(sig_gg),
                                   at2["gla_norm"].rearrange("p (o e) -> p o e", o=1).to_broadcast([P, 8, P]), ALU.mult))
            for n in range(3):
                dve.wait_ge(y_hi_ready, 5 * l + n + 1)
                tiles = slice(4 * n, 4 * n + 4)
                dve.tensor_tensor(y_lo[:, tiles, :], yT_all[:, tiles, :], y_hi[:, tiles, :], ALU.subtract).then_inc(y_lo_ready, 1)
            dve.wait_ge(squared, 2 * l + 5)
            then(dve.tensor_reduce(mean, heads8(square_g), AX.X, ALU.add))
            dve.tensor_scalar(var8, mean, 1.0 / GLA_DV, EPS, ALU.mult, ALU.add).then_inc(var8_ready, 1)
            for j in last_in_bank(layer["gla_o"]):
                dve.wait_ge(bank_read[j.bank], j.count(l))
            dve.wait_ge(rstd8_ready, l + 3)
            then(dve.tensor_tensor(heads8(o_g), heads8(o_g), by_head(rstd8), ALU.mult))
            dve.tensor_tensor(o_g, o_g, sig_gg, ALU.mult).then_inc(y_gla, 1)
            for h in range(AHEAD):
                split_lo(LATE + h)
            for i, j in enumerate(layer["gla_t"]):
                dve.wait_ge(y_hi_ready, 5 * l + 4 + i)
                dve.tensor_tensor(y_lo[:, 12:16, i * P:(i + 1) * P], psum[j.bank][:, :].rearrange("p (h t) -> p h t", h=4),
                                  y_hi[:, 12:16, i * P:(i + 1) * P], ALU.subtract).then_inc(bank_read[j.bank], 1)
            for j in layer["gla_t"]:
                dve.wait_ge(bank_read[j.bank], j.count(l))
            dve.memset(mark, 0.0).then_inc(y_lo_ready, 2)
            for n, j in enumerate(layer["branch"]):
                br, k = divmod(n, 4)
                if n % 2 == 0:
                    split_lo(LATE + n // 2 + AHEAD)
                    dve.wait_ge(gate_sig, 8 * l + n // 2 + 1)
                full(j, l)
                got = psum[j.bank][:, :].rearrange("p (a t) -> p a t", a=2)
                pair = slice(2 * k, 2 * k + 2)
                g, m = gates[:, 2 * n:2 * n + 2, :], mixed[:, pair, :]
                dve.tensor_tensor(m if br == 0 else g, got, g, ALU.mult).then_inc(bank_read[j.bank], 1)
                if br:
                    dve.wait_ge(bank_read[j.bank], j.count(l))
                    ins = dve.tensor_tensor(m, m, g, ALU.add)
                    if br == N_BRANCH - 1:
                        then(ins)
                        then(dve.tensor_copy(mixed_hi[:, pair, :], m))
                        dve.tensor_tensor(mixed_lo[:, pair, :], m, mixed_hi[:, pair, :], ALU.subtract).then_inc(mixed_ready, 1)
                    elif k == 3:
                        then(ins)
            for n, j in enumerate(layer["out"]):
                split_lo(LATE + 8 + n + AHEAD)
                half, i = divmod(n, 2)
                if i == 1:
                    add_x(layer["out"][2 * half:2 * half + 2], l, half)
            norm_x(2 * l + 5)
            low_x(layer["h2"], at2["norm_ff"], h2_lo, 4)
            for n, j in enumerate(layer["ff1"]):
                split_lo(LATE + 12 + n + AHEAD)
                dve.wait_ge(bank_read[j.bank], j.count(l))
                pair = slice(2 * n, 2 * n + 2)
                hf = hid_ff[:, pair, :]
                then(dve.tensor_tensor(hf, hf, hf, ALU.mult))
                then(dve.tensor_copy(hid_hi[:, pair, :], hf))
                dve.tensor_tensor(hid_lo[:, pair, :], hf, hid_hi[:, pair, :], ALU.subtract).then_inc(ffh_ready, 1)
            for h in range(LATE + 28, HALVES - AHEAD):
                split_lo(h + AHEAD)
            add_x(layer["ff2"], l)
            for j in last_in_bank(layer["ff2"]):
                dve.wait_ge(bank_read[j.bank], j.count(l))
            dve.memset(mark, 0.0).then_inc(x_ready, 1)
            steps.leave(LAYERS)
        norm_x(2 * LAYERS + 4)
        dve.wait_ge(xn_ready, 2 * (2 * LAYERS + 4))
        dve.wait_ge(gain_loaded, 32)
        for i in range(TT):
            ins = dve.tensor_tensor(x[:, i, :], xn[:, i, :], last_gain, ALU.mult)
        ins.then_inc(x_ready, 1)

    block.__exit__(None, None, None)


def k_tiles(w):
    k, n = w.shape[0] // P, w.shape[1]
    return np.ascontiguousarray(w.reshape(k, P, n).transpose(1, 0, 2)).reshape(P, k * n)


def column(v):
    return v.reshape(-1, P).T


def wide(v):
    return np.broadcast_to(v.reshape(1, -1), (P, v.size))


def fill_chunk(out, w):
    out[:, 0:w.shape[1]] = w


def layout(a):
    f = np.float32
    w1 = np.zeros((PRE_CHUNKS + N_EXPERTS // 2 * PAIR_CHUNKS, P, CHUNK_COLS), f)
    for c in range(6):
        fill_chunk(w1[c], k_tiles(a["w_in"][0][:, 512 * c:512 * c + 512]))
    for c in range(2):
        fill_chunk(w1[6 + c], k_tiles(a["w_out"][0][:, 512 * c:512 * c + 512]))
    for e in range(N_EXPERTS):
        for n, name in enumerate(("w_eg", "w_eu", "w_ed")):
            fill_chunk(w1[PRE_CHUNKS + PAIR_CHUNKS * (e // 2) + 2 * n + e % 2], k_tiles(a[name][0, e]))
    prm1 = np.zeros((P, PRM1_COLS), f)

    def put1(name, v):
        prm1[:v.shape[0], PRM1[name]] = v

    put1("norm1", column(a["norm1_g"][0]))
    put1("norm2", column(a["norm2_g"][0]))
    put1("conv_w", a["conv_w"][0].reshape(CONV_W, 4, P).transpose(2, 1, 0).reshape(P, 16))
    put1("conv_b", column(a["conv_b"][0]))
    put1("m_norm", column(a["m_norm_g"][0]))
    put1("m_skip", column(a["m_skip"][0]))
    put1("da_norm", column(a["da_norm_g"][0]))
    put1("b_gate", wide(a["b_mgate"][0]))
    put1("lam", wide(a["lambda_qk"][0]))
    put1("w_q", a["w_mq"][0].transpose(1, 0, 2).reshape(P, 512))
    put1("w_k", a["w_mk"][0].transpose(1, 0, 2).reshape(P, 512))
    put1("w_gate", k_tiles(a["w_mgate"][0]))
    w_r = np.concatenate([a["w_rg"][0], a["w_re"][0].reshape(D, N_EXPERTS)], 1)
    put1("w_r", k_tiles(w_r))
    put1("b_r", wide(np.concatenate([a["b_rg"][0], a["b_re"][0].reshape(-1)])))
    put1("rel", a["rel_bias"])
    gain = np.stack([wide(a["normf_g"]), wide(a["norm_final_2"])])

    w2 = np.zeros((LAYERS * LAYER_CHUNKS, P, CHUNK_COLS), f)
    prm2 = np.zeros((LAYERS + 1, P, PRM2_COLS), f)
    head_pairs = [h for m in range(NSA_HPG) for h in (m, NSA_HPG + m)]
    pair_cols = np.concatenate([np.arange(h * HD, h * HD + HD) for h in head_pairs])
    gate_cols = np.concatenate([np.arange(n * D, n * D + D) for n in BRANCH_ORDER])
    for l in range(LAYERS):
        w = a["w_in_2"][l]
        at, o = {}, 0
        for name, n in (("q", 512), ("kc", 128), ("vc", 128), ("ks", 128), ("vs", 128), ("kw", 128), ("vw", 128),
                        ("g", 24), ("sbq", 512), ("sbk", 512), ("sbv", 512), ("gq", 256), ("gk", 256), ("gv", 512),
                        ("ga", 16), ("gg", 512), ("fq", 512), ("fk", 512), ("fv", 512), ("ff", 8), ("gates", 4096)):
            at[name] = w[:, o:o + n]
            o += n
        cat = lambda *names: np.concatenate([at[n] for n in names], 1)
        narrow = np.zeros((D, 512), f)
        v_cols = cat("vs", "vw", "ff", "g", "ga")
        narrow[:, 0:v_cols.shape[1]] = v_cols
        seq = [at["q"][:, pair_cols], cat("kc", "vc", "ks", "kw"), narrow]
        seq = [k_tiles(v) for v in seq]
        seq += [k_tiles(a[n][l]) for n in ("nsa_cmp_wk1_2", "nsa_cmp_wv1_2")]
        gates = at["gates"][:, gate_cols]
        gate_chunk = lambda n: k_tiles(gates[:, 512 * n:512 * n + 512])
        seq += [k_tiles(at[n]) for n in ("sbq", "sbk", "sbv")] + [gate_chunk(0)]
        seq += [k_tiles(at[n]) for n in ("fq", "fk", "fv")] + [gate_chunk(1)]
        seq += [k_tiles(cat("gq", "gk")), k_tiles(at["gv"]), k_tiles(at["gg"])] + [gate_chunk(n) for n in range(2, 8)]
        for n in range(N_BRANCH):
            wb = a["w_branch_2"][l, BRANCH_ORDER[n]]
            seq.append(k_tiles(wb[pair_cols] if n == 0 else wb))
        seq += [k_tiles(a["w_out_2"][l][:, 512 * c:512 * c + 512]) for c in range(2)]
        seq += [k_tiles(a["w_ff1_2"][l][:, 512 * c:512 * c + 512]) for c in range(8)]
        seq += [k_tiles(a["w_ff2_2"][l][512 * c:512 * c + 512]) for c in range(8)]
        assert len(seq) == LAYER_CHUNKS
        for c, v in enumerate(seq):
            fill_chunk(w2[l * LAYER_CHUNKS + c], v)

        def put2(name, v):
            prm2[l, :v.shape[0], PRM2[name]] = v

        put2("norm_mix", column(a["norm_mix_2"][l]))
        put2("norm_ff", column(a["norm_ff_2"][l]))
        put2("b_gate", column(a["b_gate_2"][l][gate_cols]))
        for name in ("k", "v"):
            pe = a[f"nsa_cmp_pos_{name}_2"][l]
            put2(f"pe_{name}", np.concatenate([np.repeat(pe[0::2].T, 2, 1), np.repeat(pe[1::2].T, 2, 1)], 0))
            put2(f"w_{name}2", k_tiles(a[f"nsa_cmp_w{name}2_2"][l]))
        put2("w_alpha", a["gla_w_alpha_2"][l])
        put2("b_alpha", column(a["gla_b_alpha_2"][l]))
        put2("gla_norm", wide(a["gla_norm_2"][l]))
        put2("fox_b", wide(a["fox_b_f_2"][l]))
    x = np.ascontiguousarray(a["x"][0].reshape(TT, P, D).transpose(1, 0, 2))
    pos = np.ascontiguousarray(np.broadcast_to(a["positions_2"].reshape(1, S), (P, S)))
    return {"x": x, "const": constants(), "prm1": prm1, "gain": gain, "w1": w1, "prm2": prm2, "w2": w2, "pos": pos}


def kernel(**inputs):
    import concourse.bacc as bacc
    from concourse.bass_utils import run_bass_kernel_spmd as run

    arrays = layout({n: np.asarray(v) for n, v in inputs.items()})
    nc = bacc.Bacc("TRN2", target_bir_lowering=False, num_devices=1)
    d = {n: nc.dram_tensor(f"in_{n}", a.shape, mybir.dt.from_np(a.dtype), kind="ExternalInput").ap()
         for n, a in arrays.items()}
    d["skew"] = nc.dram_tensor("rel_skew", (4 * P * 384,), F32, kind="Internal").ap()
    d["out"] = nc.dram_tensor("out_x", (P, TT, D), F32, kind="ExternalOutput").ap()
    program(nc, d)
    r = run(nc, [{f"in_{n}": a for n, a in arrays.items()}], core_ids=[0])
    out = np.asarray(r.results[0]["out_x"])
    return np.ascontiguousarray(out.transpose(1, 0, 2)).reshape(1, S, D)
```
